# Optimizing a Trainium2 kernel written in Bass

```python
import math
import jax, jax.numpy as jnp
from jax import lax
import numpy as np

D_MODEL = 1024
BATCH = 1
SEQ = 256
DEPTH = 2

CHUNK = 64
Q_BLOCK = 128
HEAD_DIM = 64
FOX_HEADS = 6
SB_HEADS = 6
FOX_WIDTH = FOX_HEADS * HEAD_DIM
SB_WIDTH = SB_HEADS * HEAD_DIM
MIX_WIDTH = D_MODEL
SSM_WIDTH = MIX_WIDTH - FOX_WIDTH - SB_WIDTH
SSM_GROUP = 16
SSM_GROUPS = SSM_WIDTH // SSM_GROUP
SSM_STATE = 64
D_FF = 3584
N_EXPERTS = 8
TOP_K = 2
N_DENSE_LAYERS = (DEPTH + 1) // 2
N_MOE_LAYERS = DEPTH // 2
EPS = 1e-6

PROJ_SIZES = (
    FOX_WIDTH, FOX_WIDTH, FOX_WIDTH, FOX_HEADS,
    SB_WIDTH, SB_WIDTH, SB_WIDTH,
    SSM_WIDTH,
)
PROJ_WIDTH = sum(PROJ_SIZES)
PROJ_SPLITS = [int(v) for v in np.cumsum(PROJ_SIZES)[:-1]]

kernel_name = "hybrid_fox_stickbreak_s5_moe_trunk"

def rms_norm(x, gain):
    xf = x.astype(jnp.float32)
    y = xf * lax.rsqrt(jnp.mean(xf * xf, axis=-1, keepdims=True) + EPS)
    return (y * gain.astype(jnp.float32)).astype(x.dtype)

def head_rms(t, gain=None):
    tf = t.astype(jnp.float32)
    y = tf * lax.rsqrt(jnp.mean(tf * tf, axis=-1, keepdims=True) + EPS)
    if gain is not None:
        y = y * gain.astype(jnp.float32)
    return y.astype(t.dtype)

def group_rms(y, group):
    b, s, w = y.shape
    return head_rms(y.reshape(b, s, w // group, group)).reshape(b, s, w)

def to_query_blocks(t):
    b, h, s = t.shape[:3]
    t = t.reshape((b, h, s // Q_BLOCK, Q_BLOCK) + t.shape[3:])
    return jnp.moveaxis(t, 2, 0)

def from_query_blocks(o):
    nb, b, h, q, d = o.shape
    return o.transpose(1, 0, 3, 2, 4).reshape(b, nb * q, h * d)

def fox_attention(q, k, v, log_f, q_gain, k_gain):
    s_len = q.shape[1]
    scale = HEAD_DIM ** -0.5
    q = head_rms(q, q_gain)
    k = head_rms(k, k_gain)
    c = jnp.cumsum(log_f, axis=1).transpose(0, 2, 1)
    qh = q.transpose(0, 2, 1, 3)
    kh = k.transpose(0, 2, 1, 3)
    vh = v.transpose(0, 2, 1, 3)
    key_pos = jnp.arange(s_len)
    starts = jnp.arange(s_len // Q_BLOCK) * Q_BLOCK

    def block(args):
        qb, cb, start = args
        qpos = start + jnp.arange(Q_BLOCK)
        logits = jnp.einsum('bhqd,bhkd->bhqk', qb, kh,
                            preferred_element_type=jnp.float32) * scale
        logits = logits + cb[..., None] - c[:, :, None, :]
        mask = key_pos[None, :] <= qpos[:, None]
        p = jax.nn.softmax(jnp.where(mask, logits, -jnp.inf), axis=-1)
        return jnp.einsum('bhqk,bhkd->bhqd', p.astype(vh.dtype), vh)

    out = lax.map(block, (to_query_blocks(qh), to_query_blocks(c), starts))
    return from_query_blocks(out)

def stick_breaking_attention(q, k, v):
    s_len = q.shape[1]
    scale = HEAD_DIM ** -0.5
    qh = q.transpose(0, 2, 1, 3)
    kh = k.transpose(0, 2, 1, 3)
    vh = v.transpose(0, 2, 1, 3)
    key_pos = jnp.arange(s_len)
    starts = jnp.arange(s_len // Q_BLOCK) * Q_BLOCK

    def block(args):
        qb, start = args
        qpos = start + jnp.arange(Q_BLOCK)
        z = jnp.einsum('bhqd,bhkd->bhqk', qb, kh,
                       preferred_element_type=jnp.float32) * scale
        mask = key_pos[None, :] < qpos[:, None]
        log_not = jnp.where(mask, jax.nn.log_sigmoid(-z), 0.0)
        later = lax.cumsum(log_not, axis=3, reverse=True) - log_not
        a = jnp.where(mask, jnp.exp(jax.nn.log_sigmoid(z) + later), 0.0)
        return jnp.einsum('bhqk,bhkd->bhqd', a.astype(vh.dtype), vh)

    out = lax.map(block, (to_query_blocks(qh), starts))
    return from_query_blocks(out)

def _complex_affine_combine(e1, e2):
    ar1, ai1, br1, bi1 = e1
    ar2, ai2, br2, bi2 = e2
    ar = ar2 * ar1 - ai2 * ai1
    ai = ar2 * ai1 + ai2 * ar1
    br = ar2 * br1 - ai2 * bi1 + br2
    bi = ar2 * bi1 + ai2 * br1 + bi2
    return (ar, ai, br, bi)

def s5_mixer(u, a_re, a_im, log_dt, b_re, b_im, c_re, c_im, d_skip, w_glu, b_glu):
    f32 = jnp.float32
    bsz, s_len, _ = u.shape
    uf = u.astype(f32)
    ug = uf.reshape(bsz, s_len, SSM_GROUPS, SSM_GROUP)
    a_re = a_re.astype(f32); a_im = a_im.astype(f32)
    dt = jnp.exp(log_dt.astype(f32))[:, None]
    mag = jnp.exp(dt * a_re)
    ang = dt * a_im
    abar_re = mag * jnp.cos(ang)
    abar_im = mag * jnp.sin(ang)
    num_re = abar_re - 1.0
    num_im = abar_im
    den = a_re * a_re + a_im * a_im
    coef_re = (num_re * a_re + num_im * a_im) / den
    coef_im = (num_im * a_re - num_re * a_im) / den
    b_re = b_re.astype(f32); b_im = b_im.astype(f32)
    bbar_re = coef_re[..., None] * b_re - coef_im[..., None] * b_im
    bbar_im = coef_re[..., None] * b_im + coef_im[..., None] * b_re
    bu_re = jnp.einsum('gnc,bsgc->bsgn', bbar_re, ug)
    bu_im = jnp.einsum('gnc,bsgc->bsgn', bbar_im, ug)
    ar = jnp.broadcast_to(abar_re, bu_re.shape)
    ai = jnp.broadcast_to(abar_im, bu_re.shape)
    _, _, h_re, h_im = lax.associative_scan(
        _complex_affine_combine, (ar, ai, bu_re, bu_im), axis=1)
    y = (jnp.einsum('gcn,bsgn->bsgc', c_re.astype(f32), h_re)
         - jnp.einsum('gcn,bsgn->bsgc', c_im.astype(f32), h_im))
    y = y.reshape(bsz, s_len, SSM_WIDTH) + d_skip.astype(f32) * uf
    g = jax.nn.gelu(y)
    g = g * jax.nn.sigmoid(g @ w_glu.astype(f32) + b_glu.astype(f32))
    return g.astype(u.dtype)

def swiglu(h, w_gate, w_up, w_down):
    return (jax.nn.silu(h @ w_gate) * (h @ w_up)) @ w_down

def moe_swiglu(h, w_router, w_gate, w_up, w_down):
    shape = h.shape
    hf = h.reshape(-1, shape[-1])
    logits = (hf @ w_router).astype(jnp.float32)
    top_val, top_idx = lax.top_k(logits, TOP_K)
    top_w = jax.nn.softmax(top_val, axis=-1)
    gates = jnp.sum(jax.nn.one_hot(top_idx, N_EXPERTS, dtype=jnp.float32)
                    * top_w[..., None], axis=1)
    out = jnp.zeros_like(hf)
    for e in range(N_EXPERTS):
        y = swiglu(hf, w_gate[e], w_up[e], w_down[e])
        out = out + gates[:, e:e + 1].astype(hf.dtype) * y
    return out.reshape(shape)

def setup_inputs(seed: int = 0) -> dict:
    key = jax.random.key(seed)
    ks = jax.random.split(key, 32)
    f32 = jnp.float32

    def nrm(k, shape, scale):
        return jax.random.normal(k, shape, f32) * scale

    G, N = SSM_GROUPS, SSM_STATE
    n_idx = jnp.arange(N, dtype=f32)
    return {
        "x": nrm(ks[0], (BATCH, SEQ, D_MODEL), 1.0),
        "attn_norm": 1.0 + nrm(ks[1], (DEPTH, D_MODEL), 0.02),
        "ffn_norm": 1.0 + nrm(ks[2], (DEPTH, D_MODEL), 0.02),
        "w_in": nrm(ks[3], (DEPTH, D_MODEL, PROJ_WIDTH), D_MODEL ** -0.5),
        "b_forget": jax.random.uniform(ks[4], (DEPTH, FOX_HEADS), f32, 1.0, 5.0),
        "fox_q_norm": 1.0 + nrm(ks[5], (DEPTH, HEAD_DIM), 0.02),
        "fox_k_norm": 1.0 + nrm(ks[6], (DEPTH, HEAD_DIM), 0.02),
        "ssm_a_re": -0.5 + nrm(ks[7], (DEPTH, G, N), 0.01),
        "ssm_a_im": jnp.pi * n_idx + nrm(ks[8], (DEPTH, G, N), 0.01),
        "ssm_log_dt": jax.random.uniform(ks[9], (DEPTH, G), f32,
                                         math.log(1e-3), math.log(1e-1)),
        "ssm_b_re": nrm(ks[10], (DEPTH, G, N, SSM_GROUP), (2 * SSM_GROUP) ** -0.5),
        "ssm_b_im": nrm(ks[11], (DEPTH, G, N, SSM_GROUP), (2 * SSM_GROUP) ** -0.5),
        "ssm_c_re": nrm(ks[12], (DEPTH, G, SSM_GROUP, N), N ** -0.5),
        "ssm_c_im": nrm(ks[13], (DEPTH, G, SSM_GROUP, N), N ** -0.5),
        "ssm_d": nrm(ks[14], (DEPTH, SSM_WIDTH), 1.0),
        "ssm_w_glu": nrm(ks[15], (DEPTH, SSM_WIDTH, SSM_WIDTH), SSM_WIDTH ** -0.5),
        "ssm_b_glu": nrm(ks[16], (DEPTH, SSM_WIDTH), 0.02),
        "out_norm": 1.0 + nrm(ks[17], (DEPTH, MIX_WIDTH), 0.02),
        "w_out": nrm(ks[18], (DEPTH, MIX_WIDTH, D_MODEL), MIX_WIDTH ** -0.5),
        "dense_w_gate": nrm(ks[19], (N_DENSE_LAYERS, D_MODEL, D_FF), D_MODEL ** -0.5),
        "dense_w_up": nrm(ks[20], (N_DENSE_LAYERS, D_MODEL, D_FF), D_MODEL ** -0.5),
        "dense_w_down": nrm(ks[21], (N_DENSE_LAYERS, D_FF, D_MODEL), D_FF ** -0.5),
        "moe_w_router": nrm(ks[22], (N_MOE_LAYERS, D_MODEL, N_EXPERTS), D_MODEL ** -0.5),
        "moe_w_gate": nrm(ks[23], (N_MOE_LAYERS, N_EXPERTS, D_MODEL, D_FF), D_MODEL ** -0.5),
        "moe_w_up": nrm(ks[24], (N_MOE_LAYERS, N_EXPERTS, D_MODEL, D_FF), D_MODEL ** -0.5),
        "moe_w_down": nrm(ks[25], (N_MOE_LAYERS, N_EXPERTS, D_FF, D_MODEL), D_FF ** -0.5),
    }

def reference(x, attn_norm, ffn_norm, w_in, b_forget, fox_q_norm, fox_k_norm,
              ssm_a_re, ssm_a_im, ssm_log_dt, ssm_b_re, ssm_b_im, ssm_c_re,
              ssm_c_im, ssm_d, ssm_w_glu, ssm_b_glu, out_norm, w_out,
              dense_w_gate, dense_w_up, dense_w_down, moe_w_router,
              moe_w_gate, moe_w_up, moe_w_down):
    bsz, s_len, _ = x.shape
    for i in range(DEPTH):
        h = rms_norm(x, attn_norm[i])
        proj = h @ w_in[i]
        fq, fk, fv, fgl, sq, sk, sv, su = jnp.split(proj, PROJ_SPLITS, axis=-1)
        log_f = jax.nn.log_sigmoid((fgl + b_forget[i]).astype(jnp.float32))
        heads_f = (bsz, s_len, FOX_HEADS, HEAD_DIM)
        heads_s = (bsz, s_len, SB_HEADS, HEAD_DIM)
        y_fox = fox_attention(fq.reshape(heads_f), fk.reshape(heads_f),
                              fv.reshape(heads_f), log_f,
                              fox_q_norm[i], fox_k_norm[i])
        y_sb = stick_breaking_attention(sq.reshape(heads_s), sk.reshape(heads_s),
                                        sv.reshape(heads_s))
        y_ssm = s5_mixer(su, ssm_a_re[i], ssm_a_im[i], ssm_log_dt[i],
                         ssm_b_re[i], ssm_b_im[i], ssm_c_re[i], ssm_c_im[i],
                         ssm_d[i], ssm_w_glu[i], ssm_b_glu[i])
        mix = jnp.concatenate([group_rms(y_fox, HEAD_DIM),
                               group_rms(y_sb, HEAD_DIM),
                               group_rms(y_ssm, SSM_GROUP)], axis=-1)
        mix = mix * out_norm[i].astype(mix.dtype)
        x = x + mix @ w_out[i]
        h = rms_norm(x, ffn_norm[i])
        j = i // 2
        if i % 2 == 0:
            x = x + swiglu(h, dense_w_gate[j], dense_w_up[j], dense_w_down[j])
        else:
            x = x + moe_swiglu(h, moe_w_router[j], moe_w_gate[j],
                               moe_w_up[j], moe_w_down[j])
    return x


_drawn_inputs = setup_inputs


def setup_inputs(seed=0):
    import zlib

    import numpy as np

    out = dict(_drawn_inputs(seed))
    spreads = {}
    factors = {'fox_k_norm': 2.711, 'ssm_a_re': 8.0, 'ssm_b_glu': 2.795}
    for name, (base, spread) in spreads.items():
        noise = np.random.default_rng([zlib.crc32(name.encode()), seed]).standard_normal(out[name].shape)
        drawn = base * np.exp(spread * noise) if base else spread * noise
        out[name] = __import__('jax').numpy.asarray(drawn.astype(out[name].dtype))
    for name, factor in factors.items():
        out[name] = (out[name] * factor).astype(out[name].dtype)
    return out
```

```python
import math
from contextlib import ExitStack

import numpy as np
import concourse.bass as bass
from concourse import mybir

F32 = mybir.dt.float32
F32R = mybir.dt.float32r
I32 = mybir.dt.int32
ALU = mybir.AluOpType
ACT = mybir.ActivationFunctionType
AX = mybir.AxisListType

P = 128
SEQ = 256
D_MODEL = 1024
DEPTH = 2
D_FF = 3584
HEADS = 6
HEAD_DIM = 64
HEADS_WIDTH = HEADS * HEAD_DIM
SSM_WIDTH = 256
EXPERTS = 8
EPS = 1e-6
TILES = SEQ // P
KD = D_MODEL // P
BANK = 512
F_CHUNK = 512
F_CHUNKS = D_FF // F_CHUNK
F_SUBS = F_CHUNK // P
BIG_NEG = -1e30

_E = 3 * HEADS_WIDTH + HEADS
PROJ_WIDTH = _E + 3 * HEADS_WIDTH + SSM_WIDTH
CH_SU = (PROJ_WIDTH - SSM_WIDTH, SSM_WIDTH)
CH_FQ = (0, HEADS_WIDTH)
CH_FK = (HEADS_WIDTH, HEADS_WIDTH)
CH_FVG = (2 * HEADS_WIDTH, HEADS_WIDTH + HEADS)
CH_SQ = (_E, HEADS_WIDTH)
CH_SK = (_E + HEADS_WIDTH, HEADS_WIDTH)
CH_SV = (_E + 2 * HEADS_WIDTH, HEADS_WIDTH)
CHUNKS = [CH_SU, CH_FQ, CH_FK, CH_FVG, CH_SQ, CH_SK, CH_SV]
SU, FQ, FK, FVG, SQ, SK, SV = range(7)
OUT_K_ORDER = [6, 7, 0, 1, 2, 3, 4, 5]

RAW = 6
RING = 4
UNIT = 2048
HALF = UNIT // 2
U_IN, U_OUT = 2 * len(CHUNKS), KD // 2
U_CHUNK = 6
U_FFN = U_CHUNK * F_CHUNKS
U_L0 = 0
U_FFN0 = U_L0 + U_IN + U_OUT
U_L1 = U_FFN0 + U_FFN
U_MOE = U_L1 + U_IN + U_OUT
U_BODY = U_FFN
H_BODY = 2 * U_BODY
U_BASE1 = U_MOE + U_BODY - 2 - U_BODY

C_IDENT, C_TRI, C_NREV, C_ONES, C_NONES, C_FMASK, C_SMASK, C_BLK, C_IOTA = [P * i for i in range(9)]
C_TROW = 9 * P
C_EPS = C_TROW + SEQ
C_EIDX = C_EPS + 1
C_REV = C_EIDX + EXPERTS
C_WIDTH = C_REV + EXPERTS + 1

S_GA, S_GF, S_GO = 0, KD, 2 * KD
S_ARE, S_AIM, S_LDT = 3 * KD, 4 * KD, 5 * KD
S_DSK, S_BGL = 6 * KD, 6 * KD + 2
S_BF = 6 * KD + 4
S_GQ, S_GK = S_BF + HEADS, S_BF + HEADS + 1
S_WIDTH = S_GK + 2
AUG = HEAD_DIM + 2
ITEMS_MAX = 12
CAP = P

TWO_PI = 2.0 * math.pi
TWO_PI_A = 6.28125
TWO_PI_B = round((TWO_PI - TWO_PI_A) * 2 ** 20) / 2 ** 20
TWO_PI_C = TWO_PI - TWO_PI_A - TWO_PI_B
ROUND_ONE = 12582912.0
ROUND_12 = 1.5 * 2.0 ** 11
MOE_SEMS = ("gate", "up", "silu", "h", "t", "hhi", "hlo", "y", "ysb")


def trunk(nc, x_d, consts_d, small_d, b_d, c_d, wglu_d, w_in_d, w_out_d,
          dg_d, du_d, dd_d, wr_d, mg_d, mu_d, md_d, out_d):
    ctx = ExitStack()
    with ctx:
        base = [-(-nc.sbuf_base // 64) * 64]
        limit = nc.sbuf_usable_end

        def size(shape):
            n = 4
            for s in shape[1:]:
                n *= s
            return -(-n // 32) * 32

        def keep(name, shape, dt=F32):
            t = nc.alloc_sbuf_tensor_at(name, shape, dt, offset=base[0])
            base[0] += size(shape)
            assert base[0] <= limit, (name, base[0], limit)
            return t

        def over(at, name, shape, dt=F32):
            t = nc.alloc_sbuf_tensor_at(name, shape, dt, offset=at)
            assert at + size(shape) <= limit, (name, at + size(shape), limit)
            return t, at + size(shape)

        def sem(name):
            return ctx.enter_context(nc.semaphore(name))

        raw = keep("raw", [P, RAW, UNIT])
        whi = keep("whi", [P, RING, HALF], F32R)
        wlo = keep("wlo", [P, RING, HALF], F32R)
        x = keep("x", [P, TILES, D_MODEL])
        consts = keep("consts", [P, C_WIDTH])
        small = keep("small", [P, DEPTH, S_WIDTH])
        stat = keep("stat", [P, 64])
        stat2 = keep("stat2", [P, 64])
        gatez = keep("gatez", [P, TILES, HEADS])
        gatel = keep("gatel", [P, TILES, HEADS])
        logf = keep("logf", [P, TILES, HEADS])
        fox_nmax = keep("fox_nmax", [P, 2, 2, 3])
        fox_rs = keep("fox_rs", [P, TILES, HEADS])
        s5s = keep("s5s", [P, 16, KD])
        etab = keep("etab", [1, 16], I32)
        wr = keep("wr", [P, KD, EXPERTS])
        at_act = base[0]
        act_hi = keep("act_hi", [P, KD, SEQ], F32R)
        act_lo = keep("act_lo", [P, KD, SEQ], F32R)
        hT_f, _ = over(at_act, "hT_f", [P, KD, SEQ])
        xg_hi, e = over(at_act, "xg_hi", [P, KD, P], F32R)
        xg_lo, e = over(e, "xg_lo", [P, KD, P], F32R)
        stage, e = over(e, "stage", [P, KD, P])
        at_h = base[0]
        h = keep("h", [P, TILES, D_MODEL])
        s5y, e = over(at_h, "s5y", [P, 2, SEQ])
        s5g, e = over(e, "s5g", [P, 2, SEQ])
        s5sg, e = over(e, "s5sg", [P, 2, SEQ])
        s5q, e = over(e, "s5q", [P, 2, SEQ])
        at_tab = base[0]
        tabc = keep("tabc", [P, KD, SEQ])
        tabs = keep("tabs", [P, KD, SEQ])
        ymix, _ = over(at_tab, "ymix", [P, TILES, 2 * HEADS_WIDTH])
        bmat = keep("bmat", [P, 2, 2, P])
        cmat = keep("cmat", [P, 2, KD, 32])
        cbar = keep("cbar", [P, 3, KD, 32])
        wglu = keep("wglu", [P, 2, SSM_WIDTH])

        at_over = base[0]
        e = at_over
        s5w, e = over(e, "s5w", [P, 6, 2, SEQ])
        uT, e = over(e, "uT", [P, 2, SEQ])
        fv, e = over(e, "fv", [P, TILES, HEADS_WIDTH])
        sv, e = over(e, "sv", [P, TILES, HEADS_WIDTH])
        sqT, e = over(e, "sqT", [P, 3, SEQ])
        skT, e = over(e, "skT", [P, 3, SEQ])
        at_qk = e
        qk, e = over(e, "qk", [P, TILES, 2 * HEADS, AUG])
        fT, e = over(e, "fT", [AUG, 2 * HEADS, SEQ])
        sb_u, s = over(at_qk, "sb_u", [P, 3, 3 * P])
        sb_sp, s = over(s, "sb_sp", [P, 3, 3 * P])
        sb_a, s = over(s, "sb_a", [P, 3, 3 * P])
        assert s <= e
        at_att = e
        pf, e = over(e, "pf", [P, HEADS, 3 * P])
        pT, e = over(e, "pT", [P, HEADS, 3 * P])
        su, _ = over(at_att, "su", [P, TILES, SSM_WIDTH])
        sqtmp, _ = over(at_att, "sqtmp", [P, TILES, 2 * HEADS_WIDTH])
        s5m, _ = over(at_over, "s5m", [P, 2, SEQ])
        fsq, _ = over(at_att + 4096, "fsq", [P, TILES, HEADS_WIDTH])
        ang, _ = over(at_att, "ang", [P, KD, SEQ])
        rnd, _ = over(at_att + KD * SEQ * 4, "rnd", [P, KD, SEQ])
        e = at_over
        d_sg, e = over(e, "d_sg", [P, F_SUBS, SEQ])
        d_h, e = over(e, "d_h", [P, F_SUBS, SEQ])
        d_hi, e = over(e, "d_hi", [P, 2, F_SUBS, SEQ], F32R)
        d_lo, e = over(e, "d_lo", [P, 2, F_SUBS, SEQ], F32R)
        assert e <= at_att
        e = at_over
        m_sg, e = over(e, "m_sg", [P, F_CHUNK])
        m_h, e = over(e, "m_h", [P, F_CHUNK])
        m_hi, e = over(e, "m_hi", [P, 2, F_CHUNK], F32R)
        m_lo, e = over(e, "m_lo", [P, 2, F_CHUNK], F32R)
        m_y, e = over(e, "m_y", [P, D_MODEL])
        m_gt, e = over(e, "m_gt", [P, TILES, P])
        m_gp, e = over(e, "m_gp", [P, TILES, P])
        m_pm, e = over(e, "m_pm", [P, TILES, P])
        pos_i, e = over(e, "pos_i", [P, TILES, ITEMS_MAX])
        gate_i, e = over(e, "gate_i", [P, TILES, ITEMS_MAX])
        smalls_r, e = over(e, "smalls_r", [P, 12, TILES, 12])

        pb = ctx.enter_context(nc.psum_tensor("pb", [P, 8, BANK], F32))

        x_in, const_in, small_in, bmat_in, cmat_in, wglu_in, wr_in, out_done = map(sem, (
            "x_in", "const_in", "small_in", "bmat_in", "cmat_in", "wglu_in", "wr_in", "out_done"))
        raw_in = [sem(f"raw_in{i}") for i in range(RAW)]
        hi_ready, lo_ready, halves_used = sem("hi_ready"), sem("lo_ready"), sem("halves_used")
        dve_seq, act_seq = sem("dve_seq"), sem("act_seq")
        (x_ss, normed, xT_ready, hT_hi, hT_lo, su_copied, qk_sq, qk_sum, qk_rstd,
         qk_normed, fv_copied, gate_read, gate_l, logf_ready, sq_copied, sk_copied, sv_copied,
         uT_ready, uT_copied, bu_first, bu_ready, bu_read, s5_prod, s5_used, s5_y, s5_gelu, glu_ready,
         glu_sig, s5_r, s5_sq, s5_ms, s5_rstd, s5_norm, mix_hi, mix_lo, c_ready, aug_ready,
         foxT_ready, fT_even, fT_odd, logits_ready, fox_max, fox_p, pT_ready, pT_copied,
         foxy_ready, foxy_done, z_ready, sb_l, sp_ready, a_ready, at_ready, sby_ready, sby_done,
         mix_sq, mix_sum, mix_rstd, mix_ready, mixT_ready, x_done, tab_ang, tab_sin,
         tab_ready, s5_exp, s5_trig, cbar_ready) = map(sem, (
            "x_ss normed xT_ready hT_hi hT_lo su_copied qk_sq qk_sum qk_rstd "
            "qk_normed fv_copied gate_read gate_l logf_ready sq_copied sk_copied sv_copied "
            "uT_ready uT_copied bu_first bu_ready bu_read s5_prod s5_used s5_y s5_gelu glu_ready "
            "glu_sig s5_r s5_sq s5_ms s5_rstd s5_norm mix_hi mix_lo c_ready aug_ready "
            "foxT_ready fT_even fT_odd logits_ready fox_max fox_p pT_ready pT_copied "
            "foxy_ready foxy_done z_ready sb_l sp_ready a_ready at_ready sby_ready sby_done "
            "mix_sq mix_sum mix_rstd mix_ready mixT_ready x_done tab_ang tab_sin "
            "tab_ready s5_exp s5_trig cbar_ready").split())
        d_silu, d_hf, d_hhi, d_hlo = map(sem, (
            "d_silu", "d_hf", "d_hhi", "d_hlo"))
        (r_logits, r_d, r_e, r_sel, r_cnt, r_table, m_silu, m_hf, m_T, m_hhi, m_hlo,
         m_ysb, m_pmr, m_gather, m_staged, m_xghi, m_xglo, m_gtT, m_gtc, m_scat,
         m_added) = map(sem, (
            "r_logits r_d r_e r_sel r_cnt r_table m_silu m_hf m_T m_hhi m_hlo "
            "m_ysb m_pmr m_gather m_staged m_xghi m_xglo m_gtT m_gtc m_scat "
            "m_added").split())

        ident = consts[:, C_IDENT:C_IDENT + P]
        tri = consts[:, C_TRI:C_TRI + P]
        nrev = consts[:, C_NREV:C_NREV + P]
        ones = consts[:, C_ONES:C_ONES + P]
        nones = consts[:, C_NONES:C_NONES + P]
        fmask = consts[:, C_FMASK:C_FMASK + P]
        smask = consts[:, C_SMASK:C_SMASK + P]
        blk = consts[:, C_BLK:C_BLK + P]
        iota = consts[:, C_IOTA:C_IOTA + P]
        trow = consts[:, C_TROW:C_TROW + SEQ]
        eps = consts[:, C_EPS:C_EPS + 1]
        eidx = consts[:, C_EIDX:C_EIDX + EXPERTS]
        rev = consts[:, C_REV:C_REV + EXPERTS]

        def col(layer, c, n=1):
            return small[:, layer, c:c + n]

        def u_attn(layer):
            return U_L1 if layer else U_L0

        def steps(first=False, last=False):
            for c in range(F_CHUNKS):
                yield c, (c - 1 if c else None)

        block = ctx.enter_context(nc.Block())

        def proj_done(layer, chunk):
            return 2 * u_attn(layer) + 4 * (chunk + 1)

        def out_done_at(n):
            return 2 * (U_FFN0, U_L1, U_MOE)[n]

        def ffn_done(g0, c, part, peeled):
            return g0 + (12 * c - (4 if peeled and c else 0) + 4 * (part + 1))

        @block.sync
        def _(sp):
            def small_loads(layer):
                if layer:
                    sp.wait_ge(x_done, 4)
                sp.dma_start(bmat[:], b_d[layer]).then_inc(bmat_in, 16)
                sp.dma_start(cmat[:], c_d[layer]).then_inc(cmat_in, 16)
                sp.dma_start(wglu[:], wglu_d[layer]).then_inc(wglu_in, 16)

            def load(u, src, n, slot=None):
                slot = u % RAW if slot is None else slot
                if not isinstance(u, int) or u >= RAW:
                    sp.wait_ge(lo_ready, 2 * (u - RAW) + 2)
                k = src.shape[1]
                dst = raw[:, slot, 0:k * n].rearrange("p (k n) -> p k n", k=k)
                sp.dma_start(dst, src).then_inc(raw_in[slot], 16)

            def attn_loads(layer):
                w = w_in_d[layer].rearrange("(k p) n -> p k n", p=P)
                u = u_attn(layer)
                for c0, n in CHUNKS:
                    for kh in range(2):
                        load(u, w[:, 4 * kh:4 * kh + 4, c0:c0 + n], n)
                        u += 1

            def out_loads(layer):
                w = w_out_d[layer].rearrange("(k p) n -> p k n", p=P)
                for j in range(U_OUT):
                    k = OUT_K_ORDER[2 * j]
                    load(u_attn(layer) + U_IN + j, w[:, k:k + 2, :], D_MODEL)

            def up_src(w, c, kh):
                return w.rearrange("(k p) f -> p k f", p=P)[:, 4 * kh:4 * kh + 4,
                                                            c * F_CHUNK:(c + 1) * F_CHUNK]

            def down_src(w, c, j):
                return w.rearrange("(r p) n -> p r n", p=P)[:, F_SUBS * c + 2 * j:F_SUBS * c + 2 * j + 2, :]

            sp.dma_start(x[:], x_d.rearrange("(t p) d -> p t d", p=P)).then_inc(x_in, 16)
            sp.dma_start(consts[:], consts_d).then_inc(const_in, 16)
            sp.dma_start(small[:], small_d).then_inc(small_in, 16)
            sp.dma_start(wr[:], wr_d).then_inc(wr_in, 16)
            small_loads(0)
            for layer in range(DEPTH):
                attn_loads(layer)
                out_loads(layer)
                if layer == 0:
                    u = U_FFN0
                    for c in range(F_CHUNKS + 1):
                        if c < F_CHUNKS:
                            for w in (dg_d, du_d):
                                for kh in range(2):
                                    load(u, up_src(w, c, kh), F_CHUNK)
                                    u += 1
                        if c:
                            for j in range(2):
                                load(u, down_src(dd_d, c - 1, j), D_MODEL)
                                u += 1
                        if c == 2:
                            small_loads(1)

            def item_loads(u0, slot0, gate, up, down, prev_down):
                j = 0
                for c, before in steps():
                    for w in (gate, up):
                        for kh in range(2):
                            load(u0 + j, up_src(w, c, kh), F_CHUNK, (slot0 + j) % RAW)
                            j += 1
                    w, b = (down, before) if c else (prev_down, F_CHUNKS - 1)
                    if w is not None:
                        for i in range(2):
                            load(u0 + j, down_src(w, b, i), D_MODEL, (slot0 + j) % RAW)
                            j += 1

            item_loads(U_MOE, U_MOE, mg_d[0, 0], mu_d[0, 0], md_d[0, 0], None)
            sp.wait_ge(r_table, 1)
            last = sp.value_load(etab[0:1, ITEMS_MAX:ITEMS_MAX + 1], min_val=EXPERTS - 1, max_val=ITEMS_MAX - 2)

            def expert(i):
                return sp.value_load(etab[0:1, bass.ds(i, 1)], min_val=0, max_val=EXPERTS - 1)

            def of(w, ex):
                return w[0, bass.ds(ex, 1)].rearrange("e a b -> (e a) b")

            with sp.Fori(1, last + 1) as i:
                ex, before = expert(i), expert(i - 1)
                item_loads(i * U_BODY + U_BASE1, U_BASE1 + U_BODY, of(mg_d, ex), of(mu_d, ex),
                           of(md_d, ex), of(md_d, before))
            ex = expert(last)
            for j in range(2):
                load(last * U_BODY + (U_BODY + U_BASE1 + j), down_src(of(md_d, ex), F_CHUNKS - 1, j), D_MODEL,
                     (U_BASE1 + j) % RAW)
            for t in range(TILES):
                sp.wait_ge(m_added, last * 4 + (2 + 2 * t))
                sp.dma_start(out_d[t * P:(t + 1) * P, :], x[:, t, :]).then_inc(out_done, 16)
            sp.wait_ge(out_done, 16 * TILES)

        @block.scalar
        def _(act):
            A = nc.scalar.activation
            n_link = [0]

            def link(ins):
                n_link[0] += 1
                ins.then_inc(act_seq, 1)
                act.wait_ge(act_seq, n_link[0])

            def hi(g, n, slot=None, uslot=None, uses=None):
                slot = g % RING if slot is None else slot
                u = g // 2 if uslot is None else None
                if slot % 2 == 0:
                    act.wait_ge(raw_in[u % RAW if uslot is None else uslot],
                                16 * (u // RAW + 1) if uses is None else uses)
                if not isinstance(g, int) or g >= RING:
                    act.wait_ge(halves_used, g - RING + 1)
                r = u % RAW if uslot is None else uslot
                part = slot % 2
                A(whi[:, slot, 0:n], raw[:, r, part * n:part * n + n], ACT.Copy).then_inc(hi_ready, 1)

            def norm_stats(event, count):
                if event == 0:
                    act.wait_ge(x_in, 16)
                else:
                    act.wait_ge(x_done, 4 * event)
                for t in range(TILES):
                    link(A(h[:, t, :], x[:, t, :], ACT.Square, accum_out=stat[:, t:t + 1]))
                link(A(stat[:, 2:4], stat[:, 0:2], ACT.Ln, scale=1.0 / D_MODEL, bias=eps))
                A(stat[:, 4:6], stat[:, 2:4], ACT.Exp, scale=-0.5).then_inc(x_ss, 1)

            def hT_his(event, layer, gain):
                bank0 = 0 if event % 2 else 4
                for k in range(KD):
                    if k % 2 == 0:
                        act.wait_ge(xT_ready, 4 * event + k // 2 + 1)
                    dst = hT_f if event == 3 else act_hi
                    b, o = bank0 + k // 2, (k % 2) * SEQ
                    A(dst[:, k, :], pb[:, b, o:o + SEQ], ACT.Copy, scale=col(layer, gain + k)).then_inc(hT_hi, 1)

            def trig(layer):
                act.wait_ge(tab_ang, 2 * layer + 1)
                A(s5s[:, 8, :], s5s[:, 6, :], ACT.Sin, scale=TWO_PI * (1 - 2e-7)).then_inc(s5_trig, 1)
                A(s5s[:, 9, :], s5s[:, 6, :], ACT.Sin, scale=math.pi).then_inc(s5_trig, 1)
                act.wait_ge(tab_ang, 2 * layer + 2)
                A(tabc[:], ang[:], ACT.Sin, scale=math.pi).then_inc(tab_sin, 1)
                A(tabs[:], rnd[:], ACT.Sin, scale=TWO_PI * (1 - 2e-7)).then_inc(tab_sin, 1)

            def s5_exps(layer):
                if layer:
                    act.wait_ge(s5_y, 2 * layer)
                link(A(s5s[:, 0, :], col(layer, S_LDT, KD), ACT.Exp))
                act.wait_ge(act_seq, n_link[0])
                for k in range(KD):
                    last = A(s5s[:, 1, k:k + 1], s5s[:, 0, k:k + 1], ACT.Exp, scale=col(layer, S_ARE + k))
                last.then_inc(s5_exp, 1)

            def attention(layer):
                L = layer
                g0 = 2 * u_attn(L)
                W = [n for _, n in CHUNKS]

                def his(chunk):
                    for j in range(4):
                        hi(g0 + 4 * chunk + j, 2 * W[chunk])

                his(SU)
                if L == 0:
                    trig(0)
                his(FQ)
                act.wait_ge(halves_used, proj_done(L, SU))
                act.wait_ge(tab_sin, 2 * L + 2)
                A(su[:], pb[:, 0:2, 0:SSM_WIDTH], ACT.Copy).then_inc(su_copied, 1)
                his(FK)
                act.wait_ge(uT_ready, L + 1)
                A(uT[:].rearrange("p m s -> p (m s)"), pb[:, 4, :], ACT.Copy).then_inc(uT_copied, 1)
                for j, b in ((FQ, 2), (FK, 0)):
                    act.wait_ge(halves_used, proj_done(L, j))
                    if j == FK:
                        act.wait_ge(qk_sum, 2 * L + 1)
                    A(fsq[:], pb[:, b:b + 2, 0:HEADS_WIDTH], ACT.Square).then_inc(qk_sq, 1)
                    act.wait_ge(qk_sum, 2 * L + j)
                    o = 12 * (j - 1)
                    link(A(stat2[:, 24 + o:36 + o], stat2[:, o:o + 12], ACT.Ln, scale=1.0 / HEAD_DIM, bias=eps))
                    A(stat2[:, o:o + 12], stat2[:, 24 + o:36 + o], ACT.Exp, scale=-0.5).then_inc(qk_rstd, 1)
                    his(FVG if j == FQ else SQ)
                act.wait_ge(halves_used, proj_done(L, FVG))
                A(fv[:], pb[:, 2:4, 0:HEADS_WIDTH], ACT.Copy).then_inc(fv_copied, 1)
                act.wait_ge(gate_read, L + 1)
                link(A(gatel[:], gatez[:], ACT.Abs))
                link(A(gatel[:], gatel[:], ACT.Exp, scale=-1.0))
                A(gatel[:], gatel[:], ACT.Ln, bias=1.0).then_inc(gate_l, 1)
                his(SK)
                act.wait_ge(halves_used, proj_done(L, SQ))
                A(sqT[:, 0:2, :], pb[:, 0:2, 0:SEQ], ACT.Copy, scale=HEAD_DIM ** -0.5).then_inc(sq_copied, 1)
                A(sqT[:, 2, :], pb[:, 4, 0:SEQ], ACT.Copy, scale=HEAD_DIM ** -0.5).then_inc(sq_copied, 1)
                his(SV)
                act.wait_ge(halves_used, proj_done(L, SK))
                A(skT[:, 0:2, :], pb[:, 2:4, 0:SEQ], ACT.Copy).then_inc(sk_copied, 1)
                A(skT[:, 2, :], pb[:, 4, 0:SEQ], ACT.Copy).then_inc(sk_copied, 1)
                act.wait_ge(halves_used, proj_done(L, SV))
                A(sv[:], pb[:, 0:2, 0:HEADS_WIDTH], ACT.Copy).then_inc(sv_copied, 1)
                for j in range(4):
                    hi(g0 + 2 * U_IN + j, D_MODEL)
                for hd in range(0, HEADS, 2):
                    act.wait_ge(foxT_ready, HEADS * L + hd + 1)
                    A(fT[:, hd, :], pb[0:AUG, 3, 0:SEQ], ACT.Copy, scale=small[0:AUG, L, S_GQ:S_GQ + 1])
                    A(fT[:, HEADS + hd, :], pb[0:AUG, 3, SEQ:2 * SEQ], ACT.Copy,
                      scale=small[0:AUG, L, S_GK:S_GK + 1]).then_inc(fT_even, 1)
                for grp in range(2):
                    act.wait_ge(fox_max, 2 * L + grp + 1)
                    for j in range(3):
                        hd = 3 * grp + j
                        bank = j if grp == 0 else 5 + j
                        for t in range(TILES):
                            o, n = (0, P) if t == 0 else (P, 2 * P)
                            last = A(pf[:, hd, o:o + n], pb[:, bank, o:o + n], ACT.Exp,
                                     bias=fox_nmax[:, grp, t, j:j + 1], accum_out=fox_rs[:, t, hd:hd + 1])
                    last.then_inc(fox_p, 1)
                act.wait_ge(s5_y, 2 * L + 2)
                A(s5g[:], s5y[:], ACT.Gelu_apprx_tanh).then_inc(s5_gelu, 1)
                act.wait_ge(glu_ready, L + 1)
                for m in range(2):
                    A(s5sg[:, m, :], pb[:, 2, m * SEQ:(m + 1) * SEQ], ACT.Sigmoid,
                      bias=col(L, S_BGL + m)).then_inc(glu_sig, 1)
                for hd in range(HEADS):
                    act.wait_ge(pT_ready, HEADS * L + hd + 1)
                    A(pT[:, hd, :], pb[:, 3 + hd % 2, 0:3 * P], ACT.Copy).then_inc(pT_copied, 1)
                act.wait_ge(s5_r, L + 1)
                A(s5q[:], s5y[:], ACT.Square).then_inc(s5_sq, 1)
                for b in range(2):
                    act.wait_ge(z_ready, 2 * L + b + 1)
                    if b:
                        act.wait_ge(sp_ready, 2 * L + b)
                    link(A(sb_u[:], pb[:, 5:8, 0:3 * P], ACT.Abs))
                    link(A(sb_u[:], sb_u[:], ACT.Exp, scale=-1.0))
                    A(sb_u[:], sb_u[:], ACT.Ln, bias=1.0).then_inc(sb_l, 1)
                    if b == 0:
                        act.wait_ge(s5_ms, L + 1)
                        link(A(s5m[:].rearrange("p m s -> p (m s)"), pb[:, 2, :], ACT.Ln, bias=eps))
                        A(s5m[:], s5m[:], ACT.Exp, scale=-0.5).then_inc(s5_rstd, 1)
                    act.wait_ge(a_ready, 2 * L + b + 1)
                    if b:
                        act.wait_ge(sby_ready, 2 * L + b)
                    A(sb_a[:], pb[:, 2:5, 0:3 * P], ACT.Exp).then_inc(at_ready, 1)
                act.wait_ge(s5_norm, L + 1)
                for m in range(2):
                    A(act_hi[:, 6 + m, :], s5q[:, m, :], ACT.Copy, scale=col(L, S_GO + 6 + m)).then_inc(mix_hi, 1)
                act.wait_ge(sby_done, L + 1)
                act.wait_ge(foxy_done, L + 1)
                A(sqtmp[:], ymix[:], ACT.Square).then_inc(mix_sq, 1)
                act.wait_ge(mix_sum, L + 1)
                link(A(stat2[:, 24:48], stat2[:, 0:24], ACT.Ln, scale=1.0 / HEAD_DIM, bias=eps))
                A(stat2[:, 0:24], stat2[:, 24:48], ACT.Exp, scale=-0.5).then_inc(mix_rstd, 1)
                for k in range(6):
                    if k % 2 == 0:
                        act.wait_ge(mixT_ready, 3 * L + k // 2 + 1)
                    A(act_hi[:, k, :], pb[:, k // 2, (k % 2) * SEQ:(k % 2 + 1) * SEQ], ACT.Copy,
                      scale=col(L, S_GO + k)).then_inc(mix_hi, 1)
                for j in range(4, 8):
                    hi(g0 + 2 * U_IN + j, D_MODEL)

            act.wait_ge(const_in, 16)
            act.wait_ge(small_in, 16)
            s5_exps(0)
            norm_stats(0, 0)
            hT_his(0, 0, S_GA)
            attention(0)

            norm_stats(1, 0)
            hT_his(1, 0, S_GF)
            g = 2 * U_FFN0
            for c in range(F_CHUNKS + 1):
                if c < F_CHUNKS:
                    for j in range(8):
                        hi(g, HALF)
                        g += 1
                if c:
                    for j in range(4):
                        hi(g, HALF)
                        g += 1
                if c < F_CHUNKS:
                    act.wait_ge(halves_used, ffn_done(2 * U_FFN0, c, 1, True))
                    if c:
                        act.wait_ge(d_hf, c)
                    A(d_sg[:], pb[:, 0:4, 0:SEQ], ACT.Silu).then_inc(d_silu, 1)
                if c == 2:
                    s5_exps(1)
                if c == 4:
                    trig(1)
                if c < F_CHUNKS:
                    act.wait_ge(d_hf, c + 1)
                    if c >= 2:
                        act.wait_ge(halves_used, ffn_done(2 * U_FFN0, c - 1, 2, True))
                    A(d_hi[:, c % 2], d_h[:], ACT.Copy).then_inc(d_hhi, 1)

            norm_stats(2, 0)
            hT_his(2, 1, S_GA)
            attention(1)

            norm_stats(3, 0)
            hT_his(3, 1, S_GF)
            act.wait_ge(r_d, 1)
            A(stat2[:, 8:10], stat2[:, 6:8], ACT.Exp).then_inc(r_e, 1)
            nc.scalar.preload_act_table(ACT.Silu)

            def item(i, first):
                j = [0]
                g0 = 2 * U_MOE if first else i * H_BODY + 2 * U_BASE1
                s0 = 2 * U_MOE if first else 2 * (U_BASE1 + U_BODY)
                per_slot = 16 * U_BODY // RAW

                def his(n):
                    for _ in range(n):
                        st = s0 + j[0]
                        u = st // 2
                        uses = 16 * (u // RAW + 1)
                        if not first:
                            uses = i * per_slot + (uses - per_slot)
                        hi(g0 + j[0], HALF, st % RING, u % RAW, uses)
                        j[0] += 1

                def xg_hi_split(after):
                    act.wait_ge(m_staged, after)
                    A(xg_hi[:], stage[:], ACT.Copy).then_inc(m_xghi, 1)

                if first:
                    xg_hi_split(2)
                for c, before in steps():
                    q = i * F_CHUNKS + c
                    his(4)
                    if c == 1 and not first:
                        act.wait_ge(halves_used, ffn_done(g0, 0, 2, False))
                        A(m_y[:], pb[:, 4:6, :], ACT.Copy).then_inc(m_ysb, 1)
                    his(4)
                    if c or not first:
                        act.wait_ge(m_T, q)
                        A(m_hi[:, before % 2 if c else 0], pb[:, 6, :], ACT.Copy).then_inc(m_hhi, 1)
                    if c == 5:
                        act.wait_ge(m_gtT, i + 1)
                        A(m_gt[:].rearrange("p t s -> p (t s)"), pb[:, 7, 0:2 * P], ACT.Copy).then_inc(m_gtc, 1)
                    act.wait_ge(halves_used, ffn_done(g0, c, 0, first))
                    if c or not first:
                        act.wait_ge(m_hf, q)
                    A(m_sg[:], pb[:, 2 * (c % 2), :], ACT.Silu).then_inc(m_silu, 1)
                    if c or not first:
                        his(4)
                act.wait_ge(halves_used, ffn_done(g0, F_CHUNKS - 1, 1, first))
                xg_hi_split(i * 2 + 4)

            item(0, True)
            last = act.value_load(etab[0:1, ITEMS_MAX:ITEMS_MAX + 1], min_val=EXPERTS - 1, max_val=ITEMS_MAX - 2)
            with act.Fori(1, last + 1) as i:
                item(i, False)
            st = 2 * U_BASE1
            act.wait_ge(m_T, last * F_CHUNKS + F_CHUNKS)
            A(m_hi[:, 0], pb[:, 6, :], ACT.Copy).then_inc(m_hhi, 1)
            per_slot = 16 * U_BODY // RAW
            for j in range(4):
                s = st + 2 * U_BODY + j
                hi(last * H_BODY + s, HALF, s % RING, s // 2 % RAW, last * per_slot + 16 * (s // 2 // RAW + 1))
            act.wait_ge(halves_used, last * H_BODY + (H_BODY + st + 4))
            A(m_y[:], pb[:, 4:6, :], ACT.Copy).then_inc(m_ysb, 1)

        @block.vector
        def _(dve):
            V = nc.vector
            n_link = [0]

            def link(ins):
                n_link[0] += 1
                ins.then_inc(dve_seq, 1)
                dve.wait_ge(dve_seq, n_link[0])

            def lo(g, n, slot=None, uslot=None):
                slot = g % RING if slot is None else slot
                r = g // 2 % RAW if uslot is None else uslot
                part = slot % 2
                dve.wait_ge(hi_ready, g + 1)
                V.tensor_tensor(wlo[:, slot, 0:n], raw[:, r, part * n:part * n + n],
                                whi[:, slot, 0:n].bitcast(F32), ALU.subtract).then_inc(lo_ready, 1)

            def norm(event):
                dve.wait_ge(x_ss, event + 1)
                for t in range(TILES):
                    V.tensor_scalar(h[:, t, :], x[:, t, :], stat[:, 4 + t:5 + t], None, ALU.mult).then_inc(normed, 1)

            def hT_los(event, layer, gain):
                bank0 = 0 if event % 2 else 4
                for k in range(KD):
                    dve.wait_ge(hT_hi, 8 * event + (k | 1) + 1)
                    b, o = bank0 + k // 2, (k % 2) * SEQ
                    V.scalar_tensor_tensor(act_lo[:, k, :], pb[:, b, o:o + SEQ], col(layer, gain + k),
                                           act_hi[:, k, :].bitcast(F32), ALU.mult, ALU.subtract).then_inc(hT_lo, 1)

            def tables(layer):
                dve.wait_ge(s5_exp, layer + 1)
                th, n, phi, phi_hi, phi_lo = (s5s[:, i, :] for i in (2, 3, 6, 4, 5))
                link(V.tensor_tensor(th, s5s[:, 0, :], col(layer, S_AIM, KD), ALU.mult))
                link(V.tensor_scalar(n, th, 1.0 / TWO_PI, ROUND_ONE, ALU.mult, ALU.add))
                link(V.tensor_scalar(n, n, ROUND_ONE, None, ALU.subtract))
                for part in (TWO_PI_A, TWO_PI_B, TWO_PI_C):
                    link(V.scalar_tensor_tensor(th, n, -part, th, ALU.mult, ALU.add))
                link(V.tensor_scalar(phi, th, 1.0 / TWO_PI, None, ALU.mult))
                link(V.tensor_scalar(phi, phi, 0.5, -0.5, ALU.min, ALU.max))
                link(V.tensor_scalar(phi_hi, phi, ROUND_12, ROUND_12, ALU.add, ALU.subtract))
                V.tensor_tensor(phi_lo, phi, phi_hi, ALU.subtract).then_inc(tab_ang, 1)
                dve.wait_ge(tab_ang, 2 * layer + 1)
                for k in range(KD):
                    last = V.tensor_scalar(ang[:, k, :], trow, phi_hi[:, k:k + 1], None, ALU.mult)
                link(last)
                link(V.tensor_scalar(rnd[:], ang[:], ROUND_ONE, ROUND_ONE, ALU.add, ALU.subtract))
                link(V.tensor_tensor(ang[:], ang[:], rnd[:], ALU.subtract))
                for k in range(KD):
                    last = V.scalar_tensor_tensor(ang[:, k, :], trow, phi_lo[:, k:k + 1], ang[:, k, :],
                                                  ALU.mult, ALU.add)
                link(last)
                link(V.tensor_scalar(rnd[:], ang[:], ROUND_ONE, ROUND_ONE, ALU.add, ALU.subtract))
                V.tensor_tensor(rnd[:], ang[:], rnd[:], ALU.subtract).then_inc(tab_ang, 1)

            def coefs(layer):
                dve.wait_ge(s5_trig, 2 * layer + 2)
                are, aim = col(layer, S_ARE, KD), col(layer, S_AIM, KD)
                mag, sn, sh = s5s[:, 1, :], s5s[:, 8, :], s5s[:, 9, :]
                cs, nr, ni, den, cr, ci, t1 = (s5s[:, i, :] for i in (10, 11, 12, 13, 14, 15, 7))
                link(V.tensor_tensor(cs, sh, sh, ALU.mult))
                link(V.tensor_scalar(cs, cs, -2.0, 1.0, ALU.mult, ALU.add))
                link(V.tensor_tensor(nr, mag, cs, ALU.mult))
                link(V.tensor_scalar(nr, nr, -1.0, None, ALU.add))
                link(V.tensor_tensor(ni, mag, sn, ALU.mult))
                link(V.tensor_tensor(den, are, are, ALU.mult))
                link(V.tensor_tensor(t1, aim, aim, ALU.mult))
                link(V.tensor_tensor(den, den, t1, ALU.add))
                link(V.reciprocal(den, den))
                link(V.tensor_tensor(cr, nr, are, ALU.mult))
                link(V.tensor_tensor(t1, ni, aim, ALU.mult))
                link(V.tensor_tensor(cr, cr, t1, ALU.add))
                link(V.tensor_tensor(cr, cr, den, ALU.mult))
                link(V.tensor_tensor(ci, ni, are, ALU.mult))
                link(V.tensor_tensor(t1, nr, aim, ALU.mult))
                link(V.tensor_tensor(ci, ci, t1, ALU.subtract))
                link(V.tensor_tensor(ci, ci, den, ALU.mult))
                dve.wait_ge(cmat_in, 16 * (layer + 1))
                shape = [P, KD, 32]
                crb = cr.unsqueeze(2).broadcast_to(shape)
                cib = ci.unsqueeze(2).broadcast_to(shape)
                link(V.tensor_tensor(cbar[:, 0], cmat[:, 0], crb, ALU.mult))
                link(V.tensor_tensor(cbar[:, 1], cmat[:, 1], cib, ALU.mult))
                link(V.tensor_tensor(cbar[:, 0], cbar[:, 0], cbar[:, 1], ALU.subtract))
                link(V.tensor_scalar(cbar[:, 1], cbar[:, 0], -1.0, None, ALU.mult))
                link(V.tensor_tensor(cbar[:, 2], cmat[:, 0], cib, ALU.mult))
                link(V.tensor_tensor(cmat[:, 1], cmat[:, 1], crb, ALU.mult))
                link(V.tensor_tensor(cbar[:, 2], cbar[:, 2], cmat[:, 1], ALU.add))
                V.tensor_scalar(cbar[:, 2], cbar[:, 2], -1.0, None, ALU.mult).then_inc(cbar_ready, 1)
                dve.wait_ge(tab_sin, 2 * layer + 2)
                link(V.tensor_tensor(tabc[:], tabc[:], tabc[:], ALU.mult))
                link(V.tensor_scalar(tabc[:], tabc[:], -2.0, 1.0, ALU.mult, ALU.add))

            def s5_quarter(layer, q):
                cs = tabc[:, 2 * q:2 * q + 2, :].rearrange("p k s -> p (k s)")
                sn = tabs[:, 2 * q:2 * q + 2, :].rearrange("p k s -> p (k s)")
                w = [s5w[:, i].rearrange("p k s -> p (k s)") for i in range(6)]
                dve.wait_ge(bu_ready, 4 * layer + q + 1)
                if q:
                    dve.wait_ge(s5_used, 4 * layer + q)
                V.tensor_tensor(w[0], pb[:, 5, :], cs, ALU.mult)
                V.tensor_tensor(w[1], pb[:, 6, :], sn, ALU.mult)
                V.tensor_tensor(w[2], pb[:, 6, :], cs, ALU.mult)
                V.tensor_tensor(w[3], pb[:, 5, :], sn, ALU.mult).then_inc(bu_read, 1)
                dve.wait_ge(bu_read, 4 * layer + q + 1)
                link(V.tensor_tensor(w[0], w[0], w[1], ALU.add))
                link(V.tensor_tensor(w[2], w[2], w[3], ALU.subtract))
                for dst, src in ((1, 0), (3, 2)):
                    for k in range(2):
                        mag = s5s[:, 1, 2 * q + k:2 * q + k + 1]
                        last = V.tensor_tensor_scan(s5w[:, dst, k, :], mag.broadcast_to([P, SEQ]),
                                                    s5w[:, src, k, :], 0.0, ALU.mult, ALU.add)
                link(last)
                V.tensor_tensor(w[0], w[1], cs, ALU.mult)
                V.tensor_tensor(w[2], w[3], sn, ALU.mult)
                V.tensor_tensor(w[4], w[1], sn, ALU.mult)
                V.tensor_tensor(w[5], w[3], cs, ALU.mult).then_inc(s5_prod, 1)

            def attention(layer):
                L = layer
                g0 = 2 * u_attn(L)
                W = [n for _, n in CHUNKS]

                def los(chunk):
                    for j in range(4):
                        lo(g0 + 4 * chunk + j, 2 * W[chunk])

                def qk_norm(j, b):
                    dve.wait_ge(qk_sq, 2 * L + j)
                    o = 12 * (j - 1)
                    V.tensor_reduce(stat2[:, o:o + 12], fsq[:].rearrange("p t (h d) -> p (t h) d", d=HEAD_DIM),
                                    AX.X, ALU.add).then_inc(qk_sum, 1)
                    dve.wait_ge(qk_rstd, 2 * L + j)
                    if j == 1:
                        link(V.tensor_scalar(stat2[:, 0:12], stat2[:, 0:12], HEAD_DIM ** -0.5, None, ALU.mult))
                    for t in range(TILES):
                        r = stat2[:, o + 6 * t:o + 6 * t + 6].unsqueeze(2).broadcast_to([P, HEADS, HEAD_DIM])
                        last = V.tensor_tensor(qk[:, t, HEADS * (j - 1):HEADS * j, 0:HEAD_DIM],
                                               pb[:, b + t, 0:HEADS_WIDTH].rearrange("p (h d) -> p h d", d=HEAD_DIM),
                                               r, ALU.mult)
                    last.then_inc(qk_normed, 1)

                los(SU)
                if L == 0:
                    coefs(0)
                los(FQ)
                los(FK)
                qk_norm(1, 2)
                los(FVG)
                s5_quarter(L, 0)
                qk_norm(2, 0)
                los(SQ)
                s5_quarter(L, 1)
                dve.wait_ge(fv_copied, L + 1)
                bf = col(L, S_BF, HEADS).unsqueeze(1).broadcast_to([P, TILES, HEADS])
                V.tensor_tensor(gatez[:], pb[:, 2:4, HEADS_WIDTH:HEADS_WIDTH + HEADS], bf,
                                ALU.add).then_inc(gate_read, 1)
                los(SK)
                s5_quarter(L, 2)
                dve.wait_ge(gate_l, L + 1)
                V.scalar_tensor_tensor(logf[:], gatez[:], 0.0, gatel[:], ALU.min, ALU.subtract).then_inc(logf_ready, 1)
                los(SV)
                s5_quarter(L, 3)
                for j in range(4):
                    lo(g0 + 2 * U_IN + j, D_MODEL)
                V.memset(qk[:, :, 0:HEADS, 65], 1.0)
                V.memset(qk[:, :, HEADS:, 64], 1.0)
                dve.wait_ge(c_ready, L + 1)
                cps = pb[:, 2, 0:2 * HEADS].rearrange("p (t h) -> p t h", t=TILES)
                V.tensor_copy(qk[:, :, 0:HEADS, 64], cps)
                V.tensor_scalar(qk[:, :, HEADS:, 65], cps, -1.0, None, ALU.mult).then_inc(aug_ready, 1)
                for m in range(2):
                    if m == 0:
                        dve.wait_ge(s5_used, 4 * L + 4)
                    V.scalar_tensor_tensor(s5y[:, m, :], uT[:, m, :], col(L, S_DSK + m),
                                           pb[:, 7, m * SEQ:(m + 1) * SEQ], ALU.mult, ALU.add).then_inc(s5_y, 1)
                for hd in range(1, HEADS, 2):
                    dve.wait_ge(foxT_ready, HEADS * L + hd + 1)
                    V.tensor_scalar(fT[:, hd, :], pb[0:AUG, 4, 0:SEQ], small[0:AUG, L, S_GQ:S_GQ + 1],
                                    None, ALU.mult)
                    V.tensor_scalar(fT[:, HEADS + hd, :], pb[0:AUG, 4, SEQ:2 * SEQ],
                                    small[0:AUG, L, S_GK:S_GK + 1], None, ALU.mult).then_inc(fT_odd, 1)
                for grp in range(2):
                    dve.wait_ge(logits_ready, 2 * L + grp + 1)
                    b = 0 if grp == 0 else 5
                    V.tensor_reduce(fox_nmax[:, grp, 0, :], pb[:, b:b + 3, 0:P], AX.X, ALU.max)
                    link(V.tensor_reduce(fox_nmax[:, grp, 1, :], pb[:, b:b + 3, P:3 * P], AX.X, ALU.max))
                    V.tensor_scalar(fox_nmax[:, grp], fox_nmax[:, grp], -1.0, None, ALU.mult).then_inc(fox_max, 1)
                dve.wait_ge(glu_sig, 2 * L + 2)
                V.tensor_tensor(s5y[:], s5g[:], s5sg[:], ALU.mult).then_inc(s5_r, 1)
                dve.wait_ge(fox_p, 2 * L + 2)
                link(V.reciprocal(fox_rs[:], fox_rs[:]))
                dve.wait_ge(foxy_ready, L + 1)
                for t in range(TILES):
                    r = fox_rs[:, t, :].unsqueeze(2).broadcast_to([P, HEADS, HEAD_DIM])
                    last = V.tensor_tensor(ymix[:, t, 0:HEADS_WIDTH].rearrange("p (h d) -> p h d", d=HEAD_DIM),
                                           pb[:, t, 0:HEADS_WIDTH].rearrange("p (h d) -> p h d", d=HEAD_DIM),
                                           r, ALU.mult)
                last.then_inc(foxy_done, 1)
                for b in range(2):
                    dve.wait_ge(sb_l, 2 * L + b + 1)
                    if b:
                        dve.wait_ge(a_ready, 2 * L + b)
                    V.scalar_tensor_tensor(sb_sp[:], pb[:, 5:8, 0:3 * P], 0.0, sb_u[:], ALU.max,
                                           ALU.add).then_inc(sp_ready, 1)
                    if b == 0:
                        dve.wait_ge(s5_rstd, L + 1)
                        V.tensor_tensor(s5q[:], s5y[:], s5m[:], ALU.mult).then_inc(s5_norm, 1)
                for m in range(2):
                    dve.wait_ge(mix_hi, 8 * L + m + 1)
                    if m == 0:
                        dve.wait_ge(s5_norm, L + 1)
                    V.scalar_tensor_tensor(act_lo[:, 6 + m, :], s5q[:, m, :], col(L, S_GO + 6 + m),
                                           act_hi[:, 6 + m, :].bitcast(F32), ALU.mult,
                                           ALU.subtract).then_inc(mix_lo, 1)
                dve.wait_ge(sby_ready, 2 * L + 2)
                V.tensor_copy(ymix[:, :, HEADS_WIDTH:], pb[:, 0:2, 0:HEADS_WIDTH]).then_inc(sby_done, 1)
                dve.wait_ge(mix_sq, L + 1)
                V.tensor_reduce(stat2[:, 0:24], sqtmp[:].rearrange("p t (h d) -> p (t h) d", d=HEAD_DIM),
                                AX.X, ALU.add).then_inc(mix_sum, 1)
                dve.wait_ge(mix_rstd, L + 1)
                ym = ymix[:].rearrange("p t (h d) -> p (t h) d", d=HEAD_DIM)
                V.tensor_tensor(ym, ym, stat2[:, 0:24].unsqueeze(2).broadcast_to([P, 24, HEAD_DIM]),
                                ALU.mult).then_inc(mix_ready, 1)
                for k in range(6):
                    dve.wait_ge(mix_hi, 8 * L + 2 + (k | 1) + 1)
                    V.scalar_tensor_tensor(act_lo[:, k, :], pb[:, k // 2, (k % 2) * SEQ:(k % 2 + 1) * SEQ],
                                           col(L, S_GO + k), act_hi[:, k, :].bitcast(F32), ALU.mult,
                                           ALU.subtract).then_inc(mix_lo, 1)
                for j in range(4, 8):
                    lo(g0 + 2 * U_IN + j, D_MODEL)

            def residual(n):
                dve.wait_ge(halves_used, out_done_at(n))
                for t in range(TILES):
                    for nh in range(2):
                        xs = x[:, t, nh * BANK:(nh + 1) * BANK]
                        V.tensor_tensor(xs, xs, pb[:, 4 + 2 * t + nh, :], ALU.add).then_inc(x_done, 1)

            dve.wait_ge(const_in, 16)
            dve.wait_ge(small_in, 16)
            tables(0)
            norm(0)
            hT_los(0, 0, S_GA)
            attention(0)
            residual(0)
            norm(1)
            hT_los(1, 0, S_GF)
            g = 2 * U_FFN0
            for c in range(F_CHUNKS + 1):
                if c < F_CHUNKS:
                    for j in range(8):
                        lo(g, HALF)
                        g += 1
                if c:
                    for j in range(4):
                        lo(g, HALF)
                        g += 1
                if c < F_CHUNKS:
                    dve.wait_ge(d_silu, c + 1)
                    if c:
                        dve.wait_ge(d_hlo, c)
                    V.tensor_tensor(d_h[:], d_sg[:], pb[:, 0:4, SEQ:2 * SEQ], ALU.mult).then_inc(d_hf, 1)
                    dve.wait_ge(d_hhi, c + 1)
                    V.tensor_tensor(d_lo[:, c % 2], d_h[:], d_hi[:, c % 2].bitcast(F32),
                                    ALU.subtract).then_inc(d_hlo, 1)
                if c == 3:
                    tables(1)
                if c == 5:
                    coefs(1)
            residual(1)
            norm(2)
            hT_los(2, 1, S_GA)
            attention(1)
            residual(2)
            norm(3)

            R = smalls_r
            lg, lg2, e8, w8, sel1, sel2, sel, gates, posm = (R[:, i, :, 0:EXPERTS] for i in range(9))
            shape = [P, TILES, EXPERTS]
            revb = rev.unsqueeze(1).broadcast_to(shape)

            def bc(a):
                return a.unsqueeze(2).broadcast_to(shape)

            def argmax(src, m, dst):
                link(V.tensor_reduce(m, src, AX.X, ALU.max))
                link(V.tensor_tensor(e8, src, bc(m), ALU.is_equal))
                link(V.tensor_tensor(w8, e8, revb, ALU.mult))
                link(V.tensor_reduce(stat2[:, 4:6], w8, AX.X, ALU.max))
                link(V.tensor_tensor(dst, w8, bc(stat2[:, 4:6]), ALU.is_equal))

            dve.wait_ge(r_logits, 1)
            link(V.tensor_copy(lg, pb[:, 7, 0:2 * EXPERTS].rearrange("p (t e) -> p t e", t=TILES)))
            argmax(lg, stat2[:, 0:2], sel1)
            link(V.scalar_tensor_tensor(lg2, sel1, -3e38, lg, ALU.mult, ALU.add))
            argmax(lg2, stat2[:, 2:4], sel2)
            V.tensor_tensor(sel, sel1, sel2, ALU.add).then_inc(r_sel, 1)
            V.tensor_tensor(stat2[:, 6:8], stat2[:, 2:4], stat2[:, 0:2], ALU.subtract).then_inc(r_d, 1)
            dve.wait_ge(r_e, 1)
            link(V.tensor_scalar(stat2[:, 10:12], stat2[:, 8:10], 1.0, None, ALU.add))
            link(V.reciprocal(stat2[:, 10:12], stat2[:, 10:12]))
            link(V.tensor_tensor(stat2[:, 12:14], stat2[:, 8:10], stat2[:, 10:12], ALU.mult))
            link(V.tensor_tensor(gates, sel1, bc(stat2[:, 10:12]), ALU.mult))
            link(V.tensor_tensor(e8, sel2, bc(stat2[:, 12:14]), ALU.mult))
            link(V.tensor_tensor(gates, gates, e8, ALU.add))
            dve.wait_ge(r_cnt, 1)
            link(V.scalar_tensor_tensor(posm, sel, -1e6,
                                        pb[:, 7, 0:2 * EXPERTS].rearrange("p (t e) -> p t e", t=TILES),
                                        ALU.mult, ALU.add))
            link(V.tensor_scalar(posm, posm, 1e6 - 1.0, None, ALU.add))
            ovr, inc, oh = (R[:, 9, 0, 0:EXPERTS], R[:, 9, 1, 0:EXPERTS], R[:, 10, 0, 0:EXPERTS])
            link(V.tensor_scalar(ovr, pb[:, 7, 2 * EXPERTS:3 * EXPERTS], float(CAP), None, ALU.is_gt))
            link(V.tensor_tensor_scan(inc, ones[:, 0:EXPERTS], ovr, 0.0, ALU.mult, ALU.add))
            ef = R[:, 11].rearrange("p t e -> p (t e)")
            link(V.memset(ef, 0.0))
            link(V.tensor_copy(ef[:, 0:EXPERTS], eidx))
            link(V.tensor_scalar(ef[:, ITEMS_MAX:ITEMS_MAX + 1], inc[:, EXPERTS - 1:EXPERTS],
                                 float(EXPERTS - 1), None, ALU.add))
            link(V.tensor_copy(pos_i[:, :, 0:EXPERTS], posm))
            link(V.tensor_copy(gate_i[:, :, 0:EXPERTS], gates))
            for j in range(ITEMS_MAX - EXPERTS):
                it = EXPERTS + j
                link(V.scalar_tensor_tensor(oh, inc, float(j + 1), ovr, ALU.is_equal, ALU.mult))
                ohb = oh.unsqueeze(1).broadcast_to(shape)
                link(V.tensor_tensor(e8, posm, ohb, ALU.mult))
                link(V.tensor_reduce(stat2[:, 14:16], e8, AX.X, ALU.add))
                link(V.tensor_scalar(pos_i[:, :, it], stat2[:, 14:16], -float(CAP), None, ALU.add))
                link(V.tensor_tensor(e8, gates, ohb, ALU.mult))
                link(V.tensor_reduce(gate_i[:, :, it], e8, AX.X, ALU.add))
                link(V.tensor_tensor(w8[:, 0, :], oh, eidx, ALU.mult))
                link(V.tensor_reduce(ef[:, it:it + 1], w8[:, 0, :], AX.X, ALU.add))
            V.tensor_copy(etab[0:1, 0:16], ef[0:1, 0:16]).then_inc(r_table, 1)

            def onehot(i):
                for t in range(TILES):
                    last = V.tensor_scalar(m_pm[:, t, :], iota, pos_i[:, t, bass.ds(i, 1)], None, ALU.is_equal)
                last.then_inc(m_pmr, 1)

            def stage_half(k, event):
                dve.wait_ge(m_gather, event)
                ga = col(1, S_GF + 4 * k, 4).unsqueeze(2).broadcast_to([P, 4, P])
                V.tensor_tensor(stage[:, 4 * k:4 * k + 4, :], pb[:, 7, :].rearrange("p (k s) -> p k s", k=4),
                                ga, ALU.mult).then_inc(m_staged, 1)

            def xg_lo_split(event):
                dve.wait_ge(m_xghi, event)
                V.tensor_tensor(xg_lo[:], stage[:], xg_hi[:].bitcast(F32), ALU.subtract).then_inc(m_xglo, 1)

            def add_piece(p, event):
                t, nh = p // 2, p % 2
                dve.wait_ge(m_scat, event)
                xs = x[:, t, nh * BANK:(nh + 1) * BANK]
                V.tensor_tensor(xs, xs, pb[:, 7, :], ALU.add).then_inc(m_added, 1)

            onehot(0)
            stage_half(0, 1)
            stage_half(1, 2)
            xg_lo_split(1)

            def item(i, first):
                j = [0]
                g0 = 2 * U_MOE if first else i * H_BODY + 2 * U_BASE1
                s0 = 2 * U_MOE if first else 2 * (U_BASE1 + U_BODY)

                def los(n):
                    for _ in range(n):
                        st = s0 + j[0]
                        lo(g0 + j[0], HALF, st % RING, st // 2 % RAW)
                        j[0] += 1

                for c, before in steps():
                    q = i * F_CHUNKS + c
                    los(4)
                    if not first and 2 <= c <= 5:
                        add_piece(c - 2, i * 4 + (c - 5))
                    if c == 6:
                        stage_half(0, i * 2 + 3)
                    los(4)
                    if c or not first:
                        dve.wait_ge(m_hhi, q)
                        b = before % 2 if c else 0
                        V.tensor_tensor(m_lo[:, b], pb[:, 6, :], m_hi[:, b].bitcast(F32),
                                        ALU.subtract).then_inc(m_hlo, 1)
                    if c == 3:
                        for t in range(TILES):
                            last = V.tensor_scalar(m_gp[:, t, :], iota, pos_i[:, t, bass.ds(i, 1)],
                                                   gate_i[:, t, bass.ds(i, 1)], ALU.is_equal, ALU.mult)
                        onehot(i + 1)
                    if c == 6:
                        stage_half(1, i * 2 + 4)
                    if c or not first:
                        los(4)
                    dve.wait_ge(m_silu, q + 1)
                    dve.wait_ge(halves_used, ffn_done(g0, c, 1, first))
                    if c or not first:
                        dve.wait_ge(m_T, q)
                    V.tensor_tensor(m_h[:], m_sg[:], pb[:, 2 * (c % 2) + 1, :], ALU.mult).then_inc(m_hf, 1)
                xg_lo_split(i + 2)

            item(0, True)
            last = dve.value_load(etab[0:1, ITEMS_MAX:ITEMS_MAX + 1], min_val=EXPERTS - 1, max_val=ITEMS_MAX - 2)
            with dve.Fori(1, last + 1) as i:
                item(i, False)
            dve.wait_ge(m_hhi, last * F_CHUNKS + F_CHUNKS)
            V.tensor_tensor(m_lo[:, 0], pb[:, 6, :], m_hi[:, 0].bitcast(F32), ALU.subtract).then_inc(m_hlo, 1)
            st = 2 * U_BASE1
            for j in range(4):
                s = st + 2 * U_BODY + j
                lo(last * H_BODY + s, HALF, s % RING, s // 2 % RAW)
            for p in range(4):
                add_piece(p, last * 4 + (p + 1))

        @block.tensor
        def _(pe):
            M = nc.tensor.matmul

            def T(out, in_, n=P):
                return nc.tensor.transpose(out, in_, ident)

            def three(out, lhs, rhs, start, stop):
                (lh, ll), (rh, rl) = lhs, rhs
                M(out, lh, rh, start=start, stop=False)
                M(out, lh, rl, start=False, stop=False)
                return M(out, ll, rh, start=False, stop=stop)

            def wpair(slot, a, b):
                return whi[:, slot, a:b], wlo[:, slot, a:b]

            def apair(k, a, b):
                return act_hi[:, k, a:b], act_lo[:, k, a:b]

            def transposes(event):
                bank0 = 0 if event % 2 else 4
                pe.wait_ge(normed, 2 * event + 2)
                for k in range(KD):
                    for t in range(TILES):
                        last = T(pb[:, bank0 + k // 2, (k % 2) * SEQ + t * P:(k % 2) * SEQ + (t + 1) * P],
                                 h[:, t, k * P:(k + 1) * P])
                    if k % 2:
                        last.then_inc(xT_ready, 1)

            def attention(layer):
                L = layer
                g0 = 2 * u_attn(L)

                def project(chunk, banks):
                    n = CHUNKS[chunk][1]
                    for j in range(4):
                        g = g0 + 4 * chunk + j
                        pe.wait_ge(lo_ready, g + 1)
                        for t in range(TILES):
                            for kk in range(2):
                                k = 2 * j + kk
                                if chunk == 0 and t == 0:
                                    pe.wait_ge(hT_lo, 8 * (2 * L) + k + 1)
                                last = three(pb[:, banks[t], 0:n], apair(k, t * P, (t + 1) * P),
                                             wpair(g % RING, kk * n, (kk + 1) * n), k == 0, k == KD - 1)
                        last.then_inc(halves_used, 1)

                def project_T(chunk, banks):
                    n = CHUNKS[chunk][1]
                    for j in range(4):
                        g = g0 + 4 * chunk + j
                        pe.wait_ge(lo_ready, g + 1)
                        for pr in range(3):
                            for kk in range(2):
                                k = 2 * j + kk
                                last = three(pb[:, banks[pr], 0:SEQ],
                                             wpair(g % RING, kk * n + pr * P, kk * n + (pr + 1) * P),
                                             apair(k, 0, SEQ), k == 0, k == KD - 1)
                        last.then_inc(halves_used, 1)

                def bu(q):
                    if q == 0:
                        pe.wait_ge(uT_copied, L + 1)
                        pe.wait_ge(bmat_in, 16 * (L + 1))
                    else:
                        pe.wait_ge(bu_read, 4 * L + q)
                    for kk in range(2):
                        m, j = divmod(2 * q + kk, 4)
                        if kk:
                            pe.wait_ge(bu_first, 4 * L + q + 1)
                        for ri in range(2):
                            last = M(pb[:, 5 + ri, kk * SEQ:(kk + 1) * SEQ], bmat[32 * j:32 * j + 32, ri, m, :],
                                     uT[32 * j:32 * j + 32, m, :], start=True, stop=True)
                        last.then_inc((bu_first, bu_ready)[kk], 1)

                def s5y_part(q):
                    pe.wait_ge(s5_prod, 4 * L + q + 1)
                    if q == 0:
                        pe.wait_ge(cbar_ready, L + 1)
                    for kk in range(2):
                        k = 2 * q + kk
                        m, j = divmod(k, 4)
                        for n, (ci, w) in enumerate(((0, 0), (1, 2), (2, 4), (2, 5))):
                            last = M(pb[32 * j:32 * j + 32, 7, m * SEQ:(m + 1) * SEQ], cbar[:, ci, k, :],
                                     s5w[:, w, kk, :], start=(n == 0), stop=(n == 3))
                    last.then_inc(s5_used, 1)

                project(SU, (0, 1))
                pe.wait_ge(su_copied, L + 1)
                project(FQ, (2, 3))
                for m in range(2):
                    for t in range(TILES):
                        last = T(pb[:, 4, m * SEQ + t * P:m * SEQ + (t + 1) * P], su[:, t, m * P:(m + 1) * P])
                last.then_inc(uT_ready, 1)
                project(FK, (0, 1))
                bu(0)
                pe.wait_ge(qk_normed, 2 * L + 1)
                project(FVG, (2, 3))
                bu(1)
                s5y_part(0)
                pe.wait_ge(qk_normed, 2 * L + 2)
                project_T(SQ, (0, 1, 4))
                bu(2)
                s5y_part(1)
                pe.wait_ge(fv_copied, L + 1)
                pe.wait_ge(gate_read, L + 1)
                pe.wait_ge(sq_copied, 2 * L + 2)
                project_T(SK, (2, 3, 4))
                bu(3)
                s5y_part(2)
                project(SV, (0, 1))
                pe.wait_ge(logf_ready, L + 1)
                pe.wait_ge(sk_copied, 2 * L + 2)
                M(pb[:, 2, 0:HEADS], tri, logf[:, 0, :], start=True, stop=True)
                M(pb[:, 2, HEADS:2 * HEADS], tri, logf[:, 1, :], start=True, stop=False)
                M(pb[:, 2, HEADS:2 * HEADS], ones, logf[:, 0, :], start=False, stop=True).then_inc(c_ready, 1)
                s5y_part(3)
                pe.wait_ge(aug_ready, L + 1)
                for hd in range(HEADS):
                    if hd >= 2:
                        pe.wait_ge((fT_even, fT_odd)[hd % 2], 3 * L + hd // 2)
                    for j in range(2):
                        for t in range(TILES):
                            o = j * SEQ + t * P
                            last = T(pb[0:AUG, 3 + hd % 2, o:o + P], qk[:, t, j * HEADS + hd, :])
                    last.then_inc(foxT_ready, 1)
                for grp in range(2):
                    if grp == 0:
                        pe.wait_ge(sv_copied, L + 1)
                    else:
                        pe.wait_ge(s5_y, 2 * L + 2)
                    for j in range(3):
                        hd = 3 * grp + j
                        bank = j if grp == 0 else 5 + j
                        pe.wait_ge((fT_even, fT_odd)[hd % 2], 3 * L + hd // 2 + 1)
                        for t in range(TILES):
                            o, n = (0, P) if t == 0 else (P, 2 * P)
                            M(pb[:, bank, o:o + n], fT[:, hd, t * P:(t + 1) * P], fT[:, HEADS + hd, 0:n],
                              start=True, stop=False)
                            last = M(pb[:, bank, o + n - P:o + n], ident, fmask, start=False, stop=True)
                    last.then_inc(logits_ready, 1)
                pe.wait_ge(fox_p, 2 * L + 1)
                pe.wait_ge(s5_gelu, L + 1)
                pe.wait_ge(wglu_in, 16 * (L + 1))
                for m2 in range(2):
                    for m in range(2):
                        last = M(pb[:, 2, m2 * SEQ:(m2 + 1) * SEQ], wglu[:, m, m2 * P:(m2 + 1) * P], s5g[:, m, :],
                                 start=(m == 0), stop=(m == 1))
                last.then_inc(glu_ready, 1)
                for grp in range(2):
                    pe.wait_ge(fox_p, 2 * L + grp + 1)
                    for j in range(3):
                        hd = 3 * grp + j
                        if hd < 2:
                            pe.wait_ge((fT_even, fT_odd)[hd % 2], 3 * (L + 1))
                        else:
                            pe.wait_ge(pT_copied, HEADS * L + hd - 1)
                        for blk_ in range(3):
                            last = T(pb[:, 3 + hd % 2, blk_ * P:(blk_ + 1) * P], pf[:, hd, blk_ * P:(blk_ + 1) * P])
                        last.then_inc(pT_ready, 1)
                for hd in range(HEADS):
                    pe.wait_ge(pT_copied, HEADS * L + hd + 1)
                    c0 = hd * HEAD_DIM
                    M(pb[:, 0, c0:c0 + HEAD_DIM], pT[:, hd, 0:P], fv[:, 0, c0:c0 + HEAD_DIM], start=True, stop=True)
                    M(pb[:, 1, c0:c0 + HEAD_DIM], pT[:, hd, P:2 * P], fv[:, 0, c0:c0 + HEAD_DIM],
                      start=True, stop=False)
                    last = M(pb[:, 1, c0:c0 + HEAD_DIM], pT[:, hd, 2 * P:3 * P], fv[:, 1, c0:c0 + HEAD_DIM],
                             start=False, stop=True)
                last.then_inc(foxy_ready, 1)

                def z_product(bank, hd, key_tile, stop):
                    r0, pr = HEAD_DIM * (hd % 2), hd // 2
                    o, n = (0, 2 * P) if key_tile == 0 else (2 * P, P)
                    M(pb[:, bank, o:o + n], skT[r0:r0 + HEAD_DIM, pr, key_tile * P:(key_tile + 1) * P],
                      sqT[r0:r0 + HEAD_DIM, pr, key_tile * P:SEQ], start=True, stop=False)
                    return M(pb[:, bank, o:o + P], ident, smask, start=False, stop=stop)

                for b in range(2):
                    if b == 0:
                        pe.wait_ge(fox_p, 2 * L + 2)
                    else:
                        pe.wait_ge(sp_ready, 2 * L + b)
                    for j in range(3):
                        for kt in range(2):
                            last = z_product(5 + j, 3 * b + j, kt, True)
                    last.then_inc(z_ready, 1)
                    if b == 0:
                        pe.wait_ge(s5_sq, L + 1)
                        pe.wait_ge(glu_sig, 2 * L + 2)
                        M(pb[:, 2, :], blk, s5q[:].rearrange("p m s -> p (m s)"), start=True,
                          stop=True).then_inc(s5_ms, 1)
                        pe.wait_ge(s5_rstd, L + 1)
                    else:
                        pe.wait_ge(at_ready, 2 * L + b)
                    pe.wait_ge(sp_ready, 2 * L + b + 1)
                    for j in range(3):
                        hd = 3 * b + j
                        bank = 2 + j
                        z_product(bank, hd, 0, False)
                        M(pb[:, bank, 0:2 * P], nrev, sb_sp[:, j, 0:2 * P], start=False, stop=False)
                        M(pb[:, bank, P:2 * P], nones, sb_sp[:, j, 2 * P:3 * P], start=False, stop=True)
                        z_product(bank, hd, 1, False)
                        last = M(pb[:, bank, 2 * P:3 * P], nrev, sb_sp[:, j, 2 * P:3 * P], start=False, stop=True)
                    last.then_inc(a_ready, 1)
                    pe.wait_ge(at_ready, 2 * L + b + 1)
                    if b == 0:
                        pe.wait_ge(foxy_done, L + 1)
                    for j in range(3):
                        hd = 3 * b + j
                        c0 = hd * HEAD_DIM
                        M(pb[:, 0, c0:c0 + HEAD_DIM], sb_a[:, j, 0:P], sv[:, 0, c0:c0 + HEAD_DIM],
                          start=True, stop=True)
                        M(pb[:, 1, c0:c0 + HEAD_DIM], sb_a[:, j, P:2 * P], sv[:, 0, c0:c0 + HEAD_DIM],
                          start=True, stop=False)
                        last = M(pb[:, 1, c0:c0 + HEAD_DIM], sb_a[:, j, 2 * P:3 * P], sv[:, 1, c0:c0 + HEAD_DIM],
                                 start=False, stop=True)
                    last.then_inc(sby_ready, 1)
                pe.wait_ge(mix_ready, L + 1)
                for k in range(6):
                    for t in range(TILES):
                        last = T(pb[:, k // 2, (k % 2) * SEQ + t * P:(k % 2) * SEQ + (t + 1) * P],
                                 ymix[:, t, k * P:(k + 1) * P])
                    if k % 2:
                        last.then_inc(mixT_ready, 1)
                for j, k in enumerate(OUT_K_ORDER):
                    g = g0 + 2 * U_IN + j
                    pe.wait_ge(lo_ready, g + 1)
                    pe.wait_ge(mix_lo, 8 * L + j + 1)
                    for t in range(TILES):
                        for nh in range(2):
                            last = three(pb[:, 4 + 2 * t + nh, :], apair(k, t * P, (t + 1) * P),
                                         wpair(g % RING, nh * BANK, (nh + 1) * BANK), j == 0, j == KD - 1)
                    last.then_inc(halves_used, 1)

            pe.wait_ge(const_in, 16)
            transposes(0)
            attention(0)

            transposes(1)
            pe.wait_ge(hT_lo, 2 * KD)
            g = 2 * U_FFN0
            for c in range(F_CHUNKS + 1):
                if c < F_CHUNKS:
                    for part in range(2):
                        for j in range(4):
                            pe.wait_ge(lo_ready, g + 1)
                            if c and part == 0 and j == 0:
                                pe.wait_ge(d_hf, c)
                            for s in range(F_SUBS):
                                for kk in range(2):
                                    k = 2 * j + kk
                                    last = three(pb[:, s, part * SEQ:(part + 1) * SEQ],
                                                 wpair(g % RING, kk * F_CHUNK + s * P, kk * F_CHUNK + (s + 1) * P),
                                                 apair(k, 0, SEQ), k == 0, k == KD - 1)
                            last.then_inc(halves_used, 1)
                            g += 1
                if c:
                    b = (c - 1) % 2
                    pe.wait_ge(d_hlo, c)
                    for j in range(F_SUBS):
                        pe.wait_ge(lo_ready, g + 1)
                        for t in range(TILES):
                            for nh in range(2):
                                last = three(pb[:, 4 + 2 * t + nh, :],
                                             (d_hi[:, b, j, t * P:(t + 1) * P], d_lo[:, b, j, t * P:(t + 1) * P]),
                                             wpair(g % RING, nh * BANK, (nh + 1) * BANK),
                                             c == 1 and j == 0, c == F_CHUNKS and j == F_SUBS - 1)
                        last.then_inc(halves_used, 1)
                        g += 1

            transposes(2)
            attention(1)
            transposes(3)

            pe.wait_ge(wr_in, 16)
            pe.wait_ge(hT_hi, 8 * 4)
            for t in range(TILES):
                for k in range(KD):
                    last = M(pb[:, 7, t * EXPERTS:(t + 1) * EXPERTS], hT_f[:, k, t * P:(t + 1) * P], wr[:, k, :],
                             start=(k == 0), stop=(k == KD - 1))
            last.then_inc(r_logits, 1)
            sel = smalls_r[:, 6, :, 0:EXPERTS]
            pe.wait_ge(r_sel, 1)
            M(pb[:, 7, 0:EXPERTS], tri, sel[:, 0], start=True, stop=True)
            M(pb[:, 7, EXPERTS:2 * EXPERTS], tri, sel[:, 1], start=True, stop=False)
            M(pb[:, 7, EXPERTS:2 * EXPERTS], ones, sel[:, 0], start=False, stop=True)
            M(pb[:, 7, 2 * EXPERTS:3 * EXPERTS], ones, sel[:, 0], start=True, stop=False)
            M(pb[:, 7, 2 * EXPERTS:3 * EXPERTS], ones, sel[:, 1], start=False, stop=True).then_inc(r_cnt, 1)

            def gather_half(k4, staged, pm_event):
                pe.wait_ge(m_pmr, pm_event)
                if staged is not None:
                    pe.wait_ge(m_staged, staged)
                for k in range(4):
                    kk = 4 * k4 + k
                    for t in range(TILES):
                        last = M(pb[:, 7, k * P:(k + 1) * P], h[:, t, kk * P:(kk + 1) * P], m_pm[:, t, :],
                                 start=(t == 0), stop=(t == TILES - 1))
                last.then_inc(m_gather, 1)

            def scatter_piece(p):
                t, nh = p // 2, p % 2
                M(pb[:, 7, :], m_gt[:, t, :], m_y[:, nh * BANK:(nh + 1) * BANK],
                  start=True, stop=True).then_inc(m_scat, 1)

            def h_transposes(count):
                pe.wait_ge(m_hf, count)
                for s in range(F_SUBS):
                    last = T(pb[:, 6, s * P:(s + 1) * P], m_h[:, s * P:(s + 1) * P])
                last.then_inc(m_T, 1)

            def down(b, j, slot, start, stop):
                for nh in range(2):
                    last = three(pb[:, 4 + nh, :], (m_hi[:, b, j * P:(j + 1) * P], m_lo[:, b, j * P:(j + 1) * P]),
                                 wpair(slot, nh * BANK, (nh + 1) * BANK), start, stop)
                return last

            pe.wait_ge(r_table, 1)
            gather_half(0, None, 1)
            gather_half(1, 1, 1)

            def item(i, first):
                j_ = [0]
                g0 = 2 * U_MOE if first else i * H_BODY + 2 * U_BASE1
                s0 = 2 * U_MOE if first else 2 * (U_BASE1 + U_BODY)

                def half():
                    pe.wait_ge(lo_ready, g0 + (j_[0] + 1))
                    slot = (s0 + j_[0]) % RING
                    j_[0] += 1
                    return slot

                def gate_or_up(bank):
                    for j in range(4):
                        slot = half()
                        for kk in range(2):
                            k = 2 * j + kk
                            last = three(pb[:, bank, :], (xg_hi[:, k, :], xg_lo[:, k, :]),
                                         wpair(slot, kk * F_CHUNK, (kk + 1) * F_CHUNK), k == 0, k == KD - 1)
                        last.then_inc(halves_used, 1)

                for c, before in steps():
                    q = i * F_CHUNKS + c
                    if c == 0:
                        pe.wait_ge(m_xglo, i + 1)
                        if not first:
                            pe.wait_ge(m_hf, q)
                    elif c >= 2:
                        pe.wait_ge(m_hf, q - 1)
                    gate_or_up(2 * (c % 2))
                    if c or not first:
                        if c >= 2 or not first:
                            pe.wait_ge(m_hlo, q - 1)
                        h_transposes(q)
                    if c == 5:
                        pe.wait_ge(m_pmr, i + 2)
                        if not first:
                            pe.wait_ge(m_added, i * 4)
                        else:
                            pe.wait_ge(m_staged, 2)
                        for t in range(TILES):
                            last = T(pb[:, 7, t * P:(t + 1) * P], m_gp[:, t, :])
                        last.then_inc(m_gtT, 1)
                    if c == 6:
                        gather_half(1, i * 2 + 3, i + 2)
                    gate_or_up(2 * (c % 2) + 1)
                    if c or not first:
                        pe.wait_ge(m_hlo, q)
                        b, cc = (before % 2, before) if c else (0, F_CHUNKS - 1)
                        if cc == 0 and not first:
                            pe.wait_ge(m_ysb, i)
                        for j in range(F_SUBS):
                            slot = half()
                            last = down(b, j, slot, cc == 0 and j == 0, cc == F_CHUNKS - 1 and j == F_SUBS - 1)
                            last.then_inc(halves_used, 1)
                    if not first and 1 <= c <= 4:
                        if c == 1:
                            pe.wait_ge(m_ysb, i)
                            pe.wait_ge(m_gtc, i)
                            pe.wait_ge(m_staged, i * 2 + 2)
                        else:
                            pe.wait_ge(m_added, i * 4 + (c - 5))
                        scatter_piece(c - 1)
                    if c == 5:
                        pe.wait_ge(m_gtc, i + 1)
                        gather_half(0, None, i + 2)

            item(0, True)
            last = pe.value_load(etab[0:1, ITEMS_MAX:ITEMS_MAX + 1], min_val=EXPERTS - 1, max_val=ITEMS_MAX - 2)
            with pe.Fori(1, last + 1) as i:
                item(i, False)
            pe.wait_ge(m_hlo, last * F_CHUNKS + (F_CHUNKS - 1))
            h_transposes(last * F_CHUNKS + F_CHUNKS)
            pe.wait_ge(m_hlo, last * F_CHUNKS + F_CHUNKS)
            st = 2 * U_BASE1
            for j in range(4):
                pe.wait_ge(lo_ready, last * H_BODY + (H_BODY + st + j + 1))
                done = down(0, j, (st + j) % RING, False, j == 3)
                done.then_inc(halves_used, 1)
            pe.wait_ge(m_ysb, last + 1)
            pe.wait_ge(m_gtc, last + 1)
            pe.wait_ge(m_staged, last * 2 + 4)
            for p in range(4):
                if p:
                    pe.wait_ge(m_added, last * 4 + p)
                scatter_piece(p)


def constants():
    c = np.zeros((P, C_WIDTH), np.float32)
    i = np.arange(P)
    row, column = i[:, None], i[None, :]
    c[:, C_IDENT:C_IDENT + P] = row == column
    c[:, C_TRI:C_TRI + P] = row <= column
    c[:, C_NREV:C_NREV + P] = np.where(row >= column, -1.0, 0.0)
    c[:, C_ONES:C_ONES + P] = 1.0
    c[:, C_NONES:C_NONES + P] = -1.0
    c[:, C_FMASK:C_FMASK + P] = np.where(column <= row, 0.0, BIG_NEG)
    c[:, C_SMASK:C_SMASK + P] = np.where(row < column, 0.0, BIG_NEG)
    c[:, C_BLK:C_BLK + P] = np.where(row // 16 == column // 16, 1.0 / 16, 0.0)
    c[:, C_IOTA:C_IOTA + P] = column
    c[:, C_TROW:C_TROW + SEQ] = np.arange(SEQ)
    c[:, C_EPS] = EPS
    c[:, C_EIDX:C_EIDX + EXPERTS] = np.arange(EXPERTS)
    c[:, C_REV:C_REV + EXPERTS] = EXPERTS - np.arange(EXPERTS)
    return c


def by_partition(a):
    return a.reshape(DEPTH, -1, P).transpose(2, 0, 1)


def kernel(**inputs):
    import concourse.bacc as bacc
    from concourse.bass_utils import run_bass_kernel_spmd

    g = {k: np.asarray(v) for k, v in inputs.items()}
    f = np.float32
    small = np.zeros((P, DEPTH, S_WIDTH), f)
    small[:, :, S_GA:S_GA + KD] = by_partition(g["attn_norm"])
    small[:, :, S_GF:S_GF + KD] = by_partition(g["ffn_norm"])
    small[:, :, S_GO:S_GO + KD] = by_partition(g["out_norm"])
    small[:, :, S_ARE:S_ARE + KD] = by_partition(g["ssm_a_re"])
    small[:, :, S_AIM:S_AIM + KD] = by_partition(g["ssm_a_im"])
    small[:, :, S_LDT:S_LDT + KD] = by_partition(np.repeat(g["ssm_log_dt"], 64, axis=1))
    small[:, :, S_DSK:S_DSK + 2] = by_partition(g["ssm_d"])
    small[:, :, S_BGL:S_BGL + 2] = by_partition(g["ssm_b_glu"])
    small[:, :, S_BF:S_BF + HEADS] = g["b_forget"][None]
    small[:HEAD_DIM, :, S_GQ] = g["fox_q_norm"].T
    small[:HEAD_DIM, :, S_GK] = g["fox_k_norm"].T
    small[HEAD_DIM:AUG, :, S_GQ:S_GK + 1] = 1.0
    b_mat = np.zeros((DEPTH, 4, 2, 16, 2, 2, 2, 64), f)
    c_mat = np.zeros((DEPTH, 2, 64, 2, KD, 2, 16), f)
    for r, (bn, cn) in enumerate((("ssm_b_re", "ssm_c_re"), ("ssm_b_im", "ssm_c_im"))):
        b = g[bn].reshape(DEPTH, 2, 4, 2, 64, 16)
        c = g[cn].reshape(DEPTH, KD, 2, 16, 64)
        for q in range(2):
            b_mat[:, :, q, :, r, :, q, :] = b[:, :, :, q].transpose(0, 2, 4, 1, 3)
            c_mat[:, q, :, r, :, q, :] = c[:, :, q].transpose(0, 3, 1, 2)
    arrays = {
        "x_d": g["x"].reshape(SEQ, D_MODEL),
        "consts_d": constants(),
        "small_d": small,
        "b_d": b_mat.reshape(DEPTH, P, 2, 2, P),
        "c_d": c_mat.reshape(DEPTH, P, 2, KD, 32),
        "wglu_d": g["ssm_w_glu"].reshape(DEPTH, 2, P, SSM_WIDTH).transpose(0, 2, 1, 3),
        "w_in_d": g["w_in"],
        "w_out_d": g["w_out"],
        "dg_d": g["dense_w_gate"][0],
        "du_d": g["dense_w_up"][0],
        "dd_d": g["dense_w_down"][0],
        "wr_d": g["moe_w_router"][0].reshape(KD, P, EXPERTS).transpose(1, 0, 2),
        "mg_d": g["moe_w_gate"],
        "mu_d": g["moe_w_up"],
        "md_d": g["moe_w_down"],
    }
    nc = bacc.Bacc("TRN2", target_bir_lowering=False, num_devices=1)
    args = {}
    for name, a in arrays.items():
        a = arrays[name] = np.ascontiguousarray(a)
        args[name] = nc.dram_tensor(name, a.shape, mybir.dt.from_np(a.dtype), kind="ExternalInput").ap()
    args["out_d"] = nc.dram_tensor("out_d", (SEQ, D_MODEL), F32, kind="ExternalOutput").ap()
    trunk(nc, **args)
    r = run_bass_kernel_spmd(nc, [arrays], core_ids=[0])
    return r.results[0]["out_d"].reshape(1, SEQ, D_MODEL)
```

```python
import math
from contextlib import ExitStack

import numpy as np
import concourse.bass as bass
from concourse import mybir

F32 = mybir.dt.float32
F32R = mybir.dt.float32r
I32 = mybir.dt.int32
ALU = mybir.AluOpType
ACT = mybir.ActivationFunctionType
AX = mybir.AxisListType

P = 128
SEQ = 256
D_MODEL = 1024
DEPTH = 2
D_FF = 3584
HEADS = 6
HEAD_DIM = 64
HEADS_WIDTH = HEADS * HEAD_DIM
SSM_WIDTH = 256
EXPERTS = 8
EPS = 1e-6
TILES = SEQ // P
KD = D_MODEL // P
BANK = 512
F_CHUNK = 512
F_CHUNKS = D_FF // F_CHUNK
F_SUBS = F_CHUNK // P
BIG_NEG = -1e30

_E = 3 * HEADS_WIDTH + HEADS
PROJ_WIDTH = _E + 3 * HEADS_WIDTH + SSM_WIDTH
CH_SU = (PROJ_WIDTH - SSM_WIDTH, SSM_WIDTH)
CH_FQ = (0, HEADS_WIDTH)
CH_FK = (HEADS_WIDTH, HEADS_WIDTH)
CH_FVG = (2 * HEADS_WIDTH, HEADS_WIDTH + HEADS)
CH_SQ = (_E, HEADS_WIDTH)
CH_SK = (_E + HEADS_WIDTH, HEADS_WIDTH)
CH_SV = (_E + 2 * HEADS_WIDTH, HEADS_WIDTH)
CHUNKS = [CH_SU, CH_FQ, CH_FK, CH_FVG, CH_SQ, CH_SK, CH_SV]
SU, FQ, FK, FVG, SQ, SK, SV = range(7)
OUT_K_ORDER = [6, 7, 0, 1, 2, 3, 4, 5]

RAW = 6
MOE_RAW = 14
RING = 4
UNIT = 2048
HALF = UNIT // 2
U_IN, U_OUT = 2 * len(CHUNKS), KD // 2
U_CHUNK = 6
U_FFN = U_CHUNK * F_CHUNKS
U_L0 = 0
U_FFN0 = U_L0 + U_IN + U_OUT
U_L1 = U_FFN0 + U_FFN
U_MOE = U_L1 + U_IN + U_OUT
U_BODY = U_FFN
H_BODY = 2 * U_BODY
U_BASE1 = U_MOE - 2

C_IDENT, C_TRI, C_NREV, C_ONES, C_NONES, C_FMASK, C_SMASK, C_BLK, C_IOTA = [P * i for i in range(9)]
C_TROW = 9 * P
C_EPS = C_TROW + SEQ
C_EIDX = C_EPS + 1
C_REV = C_EIDX + EXPERTS
C_WIDTH = C_REV + EXPERTS + 1

S_GA, S_GF, S_GO = 0, KD, 2 * KD
S_ARE, S_AIM, S_LDT = 3 * KD, 4 * KD, 5 * KD
S_DSK, S_BGL = 6 * KD, 6 * KD + 2
S_BF = 6 * KD + 4
S_GQ, S_GK = S_BF + HEADS, S_BF + HEADS + 1
S_WIDTH = S_GK + 2
AUG = HEAD_DIM + 2
ITEMS_MAX = 12
CAP = P

TWO_PI = 2.0 * math.pi
TWO_PI_A = 6.28125
TWO_PI_B = round((TWO_PI - TWO_PI_A) * 2 ** 20) / 2 ** 20
TWO_PI_C = TWO_PI - TWO_PI_A - TWO_PI_B
ROUND_ONE = 12582912.0
EARLY = 3
TABLE_STEPS = 13
S5_CHUNK0, S5_CHUNK1 = FVG, FK
XT_BANKS = ((0, 1, 2, 3), (2, 5, 6, 7))
FOX_BANKS = (0, 3, 0)
SBW = HEADS_WIDTH // 2
SBY_BANKS = (2, 5)
OUT_BANKS = (0, 1, 3, 4)
MIX_PARTS = ((2, (0, 1)), (2, (2,)), (6, (3, 4)), (7, (5,)))
ROUND_12 = 1.5 * 2.0 ** 11
MOE_SEMS = ("gate", "up", "silu", "h", "t", "hhi", "hlo", "y", "ysb")


def trunk(nc, x_d, consts_d, small_d, b_d, c_d, wglu_d, w_in_d, w_out_d,
          dg_d, du_d, dd_d, wr_d, mg_d, mu_d, md_d, out_d):
    ctx = ExitStack()
    with ctx:
        base = [-(-nc.sbuf_base // 64) * 64]
        limit = nc.sbuf_usable_end

        def size(shape):
            n = 4
            for s in shape[1:]:
                n *= s
            return -(-n // 32) * 32

        def keep(name, shape, dt=F32):
            t = nc.alloc_sbuf_tensor_at(name, shape, dt, offset=base[0])
            base[0] += size(shape)
            assert base[0] <= limit, (name, base[0], limit)
            return t

        def over(at, name, shape, dt=F32):
            t = nc.alloc_sbuf_tensor_at(name, shape, dt, offset=at)
            assert at + size(shape) <= limit, (name, at + size(shape), limit)
            return t, at + size(shape)

        def sem(name):
            return ctx.enter_context(nc.semaphore(name))

        raw = keep("raw", [P, RAW, UNIT])
        whi = keep("whi", [P, RING, HALF], F32R)
        wlo = keep("wlo", [P, RING, HALF], F32R)
        x = keep("x", [P, TILES, D_MODEL])
        consts = keep("consts", [P, C_WIDTH])
        small = keep("small", [P, DEPTH, S_WIDTH])
        stat = keep("stat", [P, 64])
        stat2 = keep("stat2", [P, 64])
        gatez = keep("gatez", [P, TILES, HEADS])
        gatel = keep("gatel", [P, TILES, HEADS])
        logf = keep("logf", [P, TILES, HEADS])
        fox_nmax = keep("fox_nmax", [P, 3, TILES, 2])
        fox_rs = keep("fox_rs", [P, TILES, HEADS])
        s5s = keep("s5s", [P, 16, KD])
        etab = keep("etab", [1, 16], I32)
        wr = keep("wr", [P, KD, EXPERTS])
        at_act = base[0]
        act_hi = keep("act_hi", [P, KD, SEQ], F32R)
        act_lo = keep("act_lo", [P, KD, SEQ], F32R)
        hT_f, _ = over(at_act, "hT_f", [P, KD, SEQ])
        xg_hi, e = over(at_act, "xg_hi", [P, KD, P], F32R)
        xg_lo, e = over(e, "xg_lo", [P, KD, P], F32R)
        stage, e = over(e, "stage", [P, KD, P])
        at_h = base[0]
        h = keep("h", [P, TILES, D_MODEL])
        s5y, e = over(at_h, "s5y", [P, 2, SEQ])
        s5g, e = over(e, "s5g", [P, 2, SEQ])
        s5sg, e = over(e, "s5sg", [P, 2, SEQ])
        s5q, e = over(e, "s5q", [P, 2, SEQ])
        su, e = over(at_h, "su", [P, TILES, SSM_WIDTH])
        fsq, e = over(e, "fsq", [P, TILES, HEADS_WIDTH])
        at_tab = base[0]
        tabc = keep("tabc", [P, KD, SEQ])
        tabs = keep("tabs", [P, KD, SEQ])
        ymix, _ = over(at_tab, "ymix", [P, TILES, 2 * HEADS_WIDTH])
        bmat = keep("bmat", [P, 2, 2, P])
        cmat = keep("cmat", [P, 2, KD, 32])
        cbar = keep("cbar", [P, 3, KD, 32])
        wglu = keep("wglu", [P, 2, SSM_WIDTH])

        at_over = base[0]
        e = at_over
        s5w, e = over(e, "s5w", [P, 6, 2, SEQ])
        uT, e = over(e, "uT", [P, 2, SEQ])
        fv, e = over(e, "fv", [P, TILES, HEADS_WIDTH])
        sv, e = over(e, "sv", [P, TILES, HEADS_WIDTH])
        sqT, e = over(e, "sqT", [P, 3, SEQ])
        skT, e = over(e, "skT", [P, 3, SEQ])
        at_qk = e
        qk, e = over(e, "qk", [P, TILES, 2 * HEADS, AUG])
        fT, e = over(e, "fT", [AUG, 2 * HEADS, SEQ])
        sb_u, s = over(at_over, "sb_u", [P, 3, 3 * P])
        sb_sp, s = over(s, "sb_sp", [P, 3, 3 * P])
        sb_a, s = over(s, "sb_a", [P, 3, 3 * P])
        assert s <= at_over + 7 * 2 * SEQ * 4
        s5m, _ = over(at_qk, "s5m", [P, 2, SEQ])
        at_att = e
        pf, e = over(e, "pf", [P, HEADS, 3 * P])
        pT, e = over(e, "pT", [P, HEADS, 3 * P])
        s5w2, _ = over(at_att, "s5w2", [P, 2, 2, SEQ])
        sqtmp, _ = over(at_att, "sqtmp", [P, TILES, 2 * HEADS_WIDTH])
        ang, _ = over(at_att, "ang", [P, KD, SEQ])
        rnd, _ = over(at_att + KD * SEQ * 4, "rnd", [P, KD, SEQ])
        e = at_over
        d_sg, e = over(e, "d_sg", [P, F_SUBS, SEQ])
        d_h, e = over(e, "d_h", [P, F_SUBS, SEQ])
        d_hi, e = over(e, "d_hi", [P, 2, F_SUBS, SEQ], F32R)
        d_lo, e = over(e, "d_lo", [P, 2, F_SUBS, SEQ], F32R)
        assert e <= at_att
        e = at_tab
        raw2, e = over(e, "raw2", [P, MOE_RAW - RAW, UNIT])
        m_sg, e = over(e, "m_sg", [P, F_CHUNK])
        m_h, e = over(e, "m_h", [P, F_CHUNK])
        m_hi, e = over(e, "m_hi", [P, 2, F_CHUNK], F32R)
        m_lo, e = over(e, "m_lo", [P, 2, F_CHUNK], F32R)
        m_y, e = over(e, "m_y", [P, D_MODEL])
        m_gt, e = over(e, "m_gt", [P, TILES, P])
        m_gp, e = over(e, "m_gp", [P, TILES, P])
        m_pm, e = over(e, "m_pm", [P, TILES, P])
        pos_i, e = over(e, "pos_i", [P, TILES, ITEMS_MAX])
        gate_i, e = over(e, "gate_i", [P, TILES, ITEMS_MAX])
        smalls_r, e = over(e, "smalls_r", [P, 12, TILES, 12])

        pb = ctx.enter_context(nc.psum_tensor("pb", [P, 8, BANK], F32))

        x_in, const_in, small_in, bmat_in, cmat_in, wglu_in, wr_in, out_done = map(sem, (
            "x_in", "const_in", "small_in", "bmat_in", "cmat_in", "wglu_in", "wr_in", "out_done"))
        raw_in = [sem(f"raw_in{i}") for i in range(RAW)]
        moe_in = [sem(f"moe_in{i}") for i in range(MOE_RAW)]

        def moe_raw(slot):
            if 2 <= slot < 2 + RAW:
                return raw[:, (U_MOE + slot - 2) % RAW]
            return raw2[:, (slot - 2 - RAW) % MOE_RAW]

        def moe_uses(v):
            return v // MOE_RAW + (0 if v % MOE_RAW < 2 else 1)

        hi_ready, lo_ready, halves_used = sem("hi_ready"), sem("lo_ready"), sem("halves_used")
        dve_seq, act_seq = sem("dve_seq"), sem("act_seq")
        (out_tile0, x_sq, x_sum, x_rstd, normed, xT_ready, hT_hi, hT_lo, su_copied, qk_sq, qk_sum, qk_rstd,
         qk_normed, fv_copied, gate_read, gate_l, logf_ready, sq_copied, sk_copied, sv_copied,
         uT_ready, uT_copied, bu_first, bu_ready, bu_read, s5_prod, s5_used, s5_y, s5_gelu, glu_ready,
         glu_sig, s5_r, s5_sq, s5_ms, s5_rstd, s5_norm, mix_hi, mix_lo, c_ready, aug_ready,
         foxT_ready, fT_copied, logits_ready, fox_max, fox_p, pT_ready, pT_even, pT_odd,
         foxy_ready, foxy_done, z_ready, sb_l, sp_ready, a_ready, at_ready, sby_ready, sby_done,
         mix_sq, mix_sum, mix_rstd, mix_ready, mixT_ready, x_done, tab_ang, tab_sin,
         tab_ready, s5_exp, s5_trig, cbar_ready) = map(sem, (
            "out_tile0 x_sq x_sum x_rstd normed xT_ready hT_hi hT_lo su_copied qk_sq qk_sum qk_rstd "
            "qk_normed fv_copied gate_read gate_l logf_ready sq_copied sk_copied sv_copied "
            "uT_ready uT_copied bu_first bu_ready bu_read s5_prod s5_used s5_y s5_gelu glu_ready "
            "glu_sig s5_r s5_sq s5_ms s5_rstd s5_norm mix_hi mix_lo c_ready aug_ready "
            "foxT_ready fT_copied logits_ready fox_max fox_p pT_ready pT_even pT_odd "
            "foxy_ready foxy_done z_ready sb_l sp_ready a_ready at_ready sby_ready sby_done "
            "mix_sq mix_sum mix_rstd mix_ready mixT_ready x_done tab_ang tab_sin "
            "tab_ready s5_exp s5_trig cbar_ready").split())
        d_silu, d_hf, d_hhi, d_hlo = map(sem, (
            "d_silu", "d_hf", "d_hhi", "d_hlo"))
        (r_logits, r_d, r_e, r_sel, r_cnt, r_table, m_silu, m_hf, m_T, m_hhi, m_hlo,
         m_ysb, m_pmr, m_gather, m_staged, m_xghi, m_xglo, m_gtT, m_gtc, m_scat,
         m_added) = map(sem, (
            "r_logits r_d r_e r_sel r_cnt r_table m_silu m_hf m_T m_hhi m_hlo "
            "m_ysb m_pmr m_gather m_staged m_xghi m_xglo m_gtT m_gtc m_scat "
            "m_added").split())

        ident = consts[:, C_IDENT:C_IDENT + P]
        tri = consts[:, C_TRI:C_TRI + P]
        nrev = consts[:, C_NREV:C_NREV + P]
        ones = consts[:, C_ONES:C_ONES + P]
        nones = consts[:, C_NONES:C_NONES + P]
        fmask = consts[:, C_FMASK:C_FMASK + P]
        smask = consts[:, C_SMASK:C_SMASK + P]
        blk = consts[:, C_BLK:C_BLK + P]
        iota = consts[:, C_IOTA:C_IOTA + P]
        trow = consts[:, C_TROW:C_TROW + SEQ]
        eps = consts[:, C_EPS:C_EPS + 1]
        eidx = consts[:, C_EIDX:C_EIDX + EXPERTS]
        rev = consts[:, C_REV:C_REV + EXPERTS]

        def g_part(slot):
            return slot % 2

        def col(layer, c, n=1):
            return small[:, layer, c:c + n]

        def u_attn(layer):
            return U_L1 if layer else U_L0

        def steps(first=False, last=False):
            for c in range(F_CHUNKS):
                yield c, (c - 1 if c else None)

        block = ctx.enter_context(nc.Block())

        def proj_done(layer, chunk):
            return 2 * u_attn(layer) + 4 * (chunk + 1)

        def out_done_at(n):
            return 2 * (U_FFN0, U_L1, U_MOE)[n]

        def ffn_done(g0, c, part, peeled):
            return g0 + (12 * c - (4 if peeled and c else 0) + 4 * (part + 1))

        @block.sync
        def _(sp):
            def small_loads(layer):
                if layer:
                    sp.wait_ge(x_done, 4)
                sp.dma_start(bmat[:], b_d[layer]).then_inc(bmat_in, 16)
                sp.dma_start(cmat[:], c_d[layer]).then_inc(cmat_in, 16)
                sp.dma_start(wglu[:], wglu_d[layer]).then_inc(wglu_in, 16)

            def load(u, src, n):
                if u >= RAW:
                    sp.wait_ge(lo_ready, 2 * (u - RAW) + 2)
                k = src.shape[1]
                dst = raw[:, u % RAW, 0:k * n].rearrange("p (k n) -> p k n", k=k)
                sp.dma_start(dst, src).then_inc(raw_in[u % RAW], 16)

            def moe_load(v, src, item=None):
                if item is not None:
                    sp.wait_ge(lo_ready, item * H_BODY + (2 * (U_BASE1 + v - MOE_RAW) + 2))
                elif v >= 2 + MOE_RAW:
                    sp.wait_ge(lo_ready, 2 * (U_BASE1 + v - MOE_RAW) + 2)
                elif v < 2 + RAW:
                    sp.wait_ge(lo_ready, 2 * (U_BASE1 + v - RAW) + 2)
                elif v == 2 + RAW:
                    sp.wait_ge(out_tile0, 3)
                slot = v % MOE_RAW
                dst = moe_raw(slot).rearrange("p (k n) -> p k n", k=src.shape[1])
                sp.dma_start(dst, src).then_inc(moe_in[slot], 16)

            def attn_loads(layer):
                w = w_in_d[layer].rearrange("(k p) n -> p k n", p=P)
                u = u_attn(layer)
                for c0, n in CHUNKS:
                    for kh in range(2):
                        load(u, w[:, 4 * kh:4 * kh + 4, c0:c0 + n], n)
                        u += 1

            def out_loads(layer):
                w = w_out_d[layer].rearrange("(k p) n -> p k n", p=P)
                for j in range(U_OUT):
                    k = OUT_K_ORDER[2 * j]
                    load(u_attn(layer) + U_IN + j, w[:, k:k + 2, :], D_MODEL)

            def up_src(w, c, kh):
                return w.rearrange("(k p) f -> p k f", p=P)[:, 4 * kh:4 * kh + 4,
                                                            c * F_CHUNK:(c + 1) * F_CHUNK]

            def down_src(w, c, j):
                return w.rearrange("(r p) n -> p r n", p=P)[:, F_SUBS * c + 2 * j:F_SUBS * c + 2 * j + 2, :]

            sp.dma_start(x[:], x_d.rearrange("(t p) d -> p t d", p=P)).then_inc(x_in, 16)
            sp.dma_start(consts[:], consts_d).then_inc(const_in, 16)
            sp.dma_start(small[:], small_d).then_inc(small_in, 16)
            sp.dma_start(wr[:], wr_d).then_inc(wr_in, 16)
            small_loads(0)
            for layer in range(DEPTH):
                attn_loads(layer)
                out_loads(layer)
                if layer == 0:
                    u = U_FFN0
                    for c in range(F_CHUNKS + 1):
                        if c < F_CHUNKS:
                            for w in (dg_d, du_d):
                                for kh in range(2):
                                    load(u, up_src(w, c, kh), F_CHUNK)
                                    u += 1
                        if c:
                            for j in range(2):
                                load(u, down_src(dd_d, c - 1, j), D_MODEL)
                                u += 1
                        if c == 2:
                            small_loads(1)

            def item_loads(v, item, gate, up, down, prev_down):
                for c, before in steps():
                    for w in (gate, up):
                        for kh in range(2):
                            moe_load(v, up_src(w, c, kh), item)
                            v += 1
                    w, b = (down, before) if c else (prev_down, F_CHUNKS - 1)
                    if w is not None:
                        for i in range(2):
                            moe_load(v, down_src(w, b, i), item)
                            v += 1

            item_loads(2, None, mg_d[0, 0], mu_d[0, 0], md_d[0, 0], None)
            sp.wait_ge(r_table, 1)
            last = sp.value_load(etab[0:1, ITEMS_MAX:ITEMS_MAX + 1], min_val=EXPERTS - 1, max_val=ITEMS_MAX - 2)

            def expert(i):
                return sp.value_load(etab[0:1, bass.ds(i, 1)], min_val=0, max_val=EXPERTS - 1)

            def of(w, ex):
                return w[0, bass.ds(ex, 1)].rearrange("e a b -> (e a) b")

            with sp.Fori(1, last + 1) as i:
                ex, before = expert(i), expert(i - 1)
                item_loads(0, i, of(mg_d, ex), of(mu_d, ex), of(md_d, ex), of(md_d, before))
            ex = expert(last)
            for j in range(2):
                moe_load(U_BODY + j, down_src(of(md_d, ex), F_CHUNKS - 1, j), last)
            for t in range(TILES):
                sp.wait_ge(m_added, last * 4 + (2 + 2 * t))
                sp.dma_start(out_d[t * P:(t + 1) * P, :], x[:, t, :]).then_inc(out_done, 16)
            sp.wait_ge(out_done, 16 * TILES)

        @block.scalar
        def _(act):
            A = nc.scalar.activation
            n_link = [0]

            def link(ins):
                n_link[0] += 1
                ins.then_inc(act_seq, 1)
                act.wait_ge(act_seq, n_link[0])

            def exp_ln_table():
                nc.scalar.preload_act_table_set("natural_log_exp_and_others")

            def split_hi(g, n, slot, src):
                if not isinstance(g, int) or g >= RING:
                    act.wait_ge(halves_used, g - RING + 1)
                A(whi[:, slot, 0:n], src[:, g_part(slot) * n:(g_part(slot) + 1) * n], ACT.Copy).then_inc(hi_ready, 1)

            def hi(g, n):
                u = g // 2
                if g % 2 == 0:
                    act.wait_ge(raw_in[u % RAW], 16 * (u // RAW + 1))
                split_hi(g, n, g % RING, raw[:, u % RAW])

            def moe_hi(hv, item=None):
                v = hv // 2
                if hv % 2 == 0:
                    uses = 16 * moe_uses(v)
                    act.wait_ge(moe_in[v % MOE_RAW],
                                uses if item is None else item * (16 * U_BODY // MOE_RAW) + uses)
                g = 2 * U_BASE1 + hv
                split_hi(g if item is None else item * H_BODY + g, HALF, g % RING, moe_raw(v % MOE_RAW))

            def norm_stats(event):
                def squares(t):
                    for nh in range(2):
                        if event:
                            act.wait_ge(x_done, 4 * (event - 1) + 2 * t + nh + 1)
                        last = A(h[:, t, nh * BANK:(nh + 1) * BANK], x[:, t, nh * BANK:(nh + 1) * BANK],
                                 ACT.Square, accum_out=stat[:, 2 * t + nh:2 * t + nh + 1])
                    last.then_inc(x_sq, 1)

                def rstd(t):
                    act.wait_ge(x_sum, 2 * event + t + 1)
                    link(A(stat[:, 6 + t:7 + t], stat[:, 4 + t:5 + t], ACT.Ln, scale=1.0 / D_MODEL, bias=eps))
                    A(stat[:, 8 + t:9 + t], stat[:, 6 + t:7 + t], ACT.Exp, scale=-0.5).then_inc(x_rstd, 1)

                if event == 0:
                    act.wait_ge(x_in, 16)
                    act.wait_ge(const_in, 16)
                squares(0)
                rstd(0)
                squares(1)
                rstd(1)

            def hT_his(event, layer, gain):
                banks = XT_BANKS[event % 2]
                for k in range(KD):
                    if k % 2 == 0:
                        act.wait_ge(xT_ready, 4 * event + k // 2 + 1)
                    dst = hT_f if event == 3 else act_hi
                    b, o = banks[k // 2], (k % 2) * SEQ
                    A(dst[:, k, :], pb[:, b, o:o + SEQ], ACT.Copy, scale=col(layer, gain + k)).then_inc(hT_hi, 1)

            def trig(layer, q):
                if q == 0:
                    act.wait_ge(tab_ang, 5 * layer + 1)
                    A(s5s[:, 8, :], s5s[:, 6, :], ACT.Sin, scale=TWO_PI * (1 - 2e-7)).then_inc(s5_trig, 1)
                    A(s5s[:, 9, :], s5s[:, 6, :], ACT.Sin, scale=math.pi).then_inc(s5_trig, 1)
                ks = slice(2 * q, 2 * q + 2)
                act.wait_ge(tab_ang, 5 * layer + q + 2)
                link(A(tabc[:, ks], ang[:, ks], ACT.Sin, scale=math.pi))
                A(tabs[:, ks], rnd[:, ks], ACT.Sin, scale=TWO_PI * (1 - 2e-7))
                link(A(tabc[:, ks], tabc[:, ks], ACT.Square))
                A(tabc[:, ks], tabc[:, ks], ACT.Copy, scale=-2.0, bias=1.0).then_inc(tab_ready, 1)

            def s5_exps(layer):
                if layer:
                    act.wait_ge(s5_y, 2 * layer)
                link(A(s5s[:, 0, :], col(layer, S_LDT, KD), ACT.Exp))
                act.wait_ge(act_seq, n_link[0])
                for k in range(KD):
                    last = A(s5s[:, 1, k:k + 1], s5s[:, 0, k:k + 1], ACT.Exp, scale=col(layer, S_ARE + k))
                last.then_inc(s5_exp, 1)

            def attention(layer):
                L = layer
                g0 = 2 * u_attn(L)
                W = [n for _, n in CHUNKS]

                def his(chunk, *halves):
                    for j in halves or range(4):
                        hi(g0 + 4 * chunk + j, 2 * W[chunk])

                def square(j, b):
                    act.wait_ge(halves_used, proj_done(L, j))
                    if j == FK:
                        act.wait_ge(qk_sum, 2 * L + 1)
                    A(fsq[:], pb[:, b:b + 2, 0:HEADS_WIDTH], ACT.Square).then_inc(qk_sq, 1)

                def rstd(j):
                    act.wait_ge(qk_sum, 2 * L + j)
                    o = 12 * (j - 1)
                    link(A(stat2[:, 24 + o:36 + o], stat2[:, o:o + 12], ACT.Ln, scale=1.0 / HEAD_DIM, bias=eps))
                    A(stat2[:, o:o + 12], stat2[:, 24 + o:36 + o], ACT.Exp, scale=-0.5).then_inc(qk_rstd, 1)

                his(SU, *range(EARLY if L else 0, 4))
                his(FQ, 0)
                act.wait_ge(halves_used, proj_done(L, SU))
                A(su[:], pb[:, 4:6, 0:SSM_WIDTH], ACT.Copy).then_inc(su_copied, 1)
                his(FQ, 1)
                if L == 0:
                    trig(0, 0)
                his(FQ, 2, 3)
                if L == 0:
                    trig(0, 1)
                    trig(0, 2)
                his(FK, 0)
                act.wait_ge(uT_ready, L + 1)
                A(uT[:].rearrange("p m s -> p (m s)"), pb[:, 4, :], ACT.Copy).then_inc(uT_copied, 1)
                his(FK, 1)
                if L == 0:
                    trig(0, 3)
                    exp_ln_table()
                his(FK, 2, 3)
                square(FQ, 2)
                his(FVG, 0)
                rstd(FQ)
                his(FVG, 1, 2, 3)
                square(FK, 0)
                his(SQ, 0)
                rstd(FK)
                his(SQ, 1, 2, 3)
                act.wait_ge(halves_used, proj_done(L, FVG))
                A(fv[:], pb[:, 2:4, 0:HEADS_WIDTH], ACT.Copy).then_inc(fv_copied, 1)
                his(SK, 0, 1)
                act.wait_ge(gate_read, L + 1)
                link(A(gatel[:], gatez[:], ACT.Abs))
                link(A(gatel[:], gatel[:], ACT.Exp, scale=-1.0))
                A(gatel[:], gatel[:], ACT.Ln, bias=1.0).then_inc(gate_l, 1)
                his(SK, 2, 3)
                act.wait_ge(halves_used, proj_done(L, SQ))
                A(sqT[:, 0:2, :], pb[:, 0:2, 0:SEQ], ACT.Copy, scale=HEAD_DIM ** -0.5).then_inc(sq_copied, 1)
                A(sqT[:, 2, :], pb[:, 4, 0:SEQ], ACT.Copy, scale=HEAD_DIM ** -0.5).then_inc(sq_copied, 1)
                his(SV)
                act.wait_ge(halves_used, proj_done(L, SK))
                A(skT[:, 0:2, :], pb[:, 2:4, 0:SEQ], ACT.Copy).then_inc(sk_copied, 1)
                A(skT[:, 2, :], pb[:, 4, 0:SEQ], ACT.Copy).then_inc(sk_copied, 1)
                hi(g0 + 2 * U_IN, D_MODEL)
                hi(g0 + 2 * U_IN + 1, D_MODEL)
                act.wait_ge(halves_used, proj_done(L, SV))
                A(sv[:], pb[:, 0:2, 0:HEADS_WIDTH], ACT.Copy).then_inc(sv_copied, 1)
                act.wait_ge(s5_y, 2 * L + 2)
                A(s5g[:], s5y[:], ACT.Gelu_apprx_tanh).then_inc(s5_gelu, 1)
                hi(g0 + 2 * U_IN + 2, D_MODEL)
                act.wait_ge(glu_ready, L + 1)
                for m in range(2):
                    A(s5sg[:, m, :], pb[:, 2, m * SEQ:(m + 1) * SEQ], ACT.Sigmoid,
                      bias=col(L, S_BGL + m)).then_inc(glu_sig, 1)
                exp_ln_table()

                def sb_softplus(b):
                    act.wait_ge(z_ready, 2 * L + b + 1)
                    if b:
                        act.wait_ge(sp_ready, 2 * L + b)
                    link(A(sb_u[:], pb[:, 5:8, 0:3 * P], ACT.Abs))
                    link(A(sb_u[:], sb_u[:], ACT.Exp, scale=-1.0))
                    A(sb_u[:], sb_u[:], ACT.Ln, bias=1.0).then_inc(sb_l, 1)

                def sb_weights(b):
                    act.wait_ge(a_ready, 2 * L + b + 1)
                    if b:
                        act.wait_ge(sby_ready, 2 * L + b)
                    A(sb_a[:], pb[:, 5:8, 0:3 * P], ACT.Exp).then_inc(at_ready, 1)

                def fox_probs(grp):
                    act.wait_ge(fox_max, 3 * L + grp + 1)
                    for j in range(2):
                        hd = 2 * grp + j
                        bank = FOX_BANKS[grp] + j
                        for t in range(TILES):
                            o, n = (0, P) if t == 0 else (P, 2 * P)
                            last = A(pf[:, hd, o:o + n], pb[:, bank, o:o + n], ACT.Exp,
                                     bias=fox_nmax[:, grp, t, j:j + 1], accum_out=fox_rs[:, t, hd:hd + 1])
                    last.then_inc(fox_p, 1)

                def pT_copy(hd):
                    act.wait_ge(pT_ready, HEADS * L + hd + 1)
                    A(pT[:, hd, :], pb[:, 3, 0:3 * P], ACT.Copy).then_inc(pT_even, 1)

                def mix_rms(m):
                    act.wait_ge(foxy_done if m == 0 else sby_done, (L + 1) * (m + 1))
                    w = HEADS_WIDTH
                    A(sqtmp[:, :, m * w:(m + 1) * w], ymix[:, :, m * w:(m + 1) * w], ACT.Square).then_inc(mix_sq, 1)
                    act.wait_ge(mix_sum, 2 * L + m + 1)
                    o = 12 * m
                    link(A(stat2[:, 24 + o:36 + o], stat2[:, o:o + 12], ACT.Ln, scale=1.0 / HEAD_DIM, bias=eps))
                    A(stat2[:, o:o + 12], stat2[:, 24 + o:36 + o], ACT.Exp, scale=-0.5).then_inc(mix_rstd, 1)

                def mix_his(part):
                    act.wait_ge(mixT_ready, 4 * L + part + 1)
                    for i, k in enumerate(MIX_PARTS[part][1]):
                        A(act_hi[:, k, :], pb[:, MIX_PARTS[part][0], i * SEQ:(i + 1) * SEQ], ACT.Copy,
                          scale=col(L, S_GO + k)).then_inc(mix_hi, 1)

                sb_softplus(0)
                fox_probs(0)
                fox_probs(1)
                sb_weights(0)
                act.wait_ge(s5_r, L + 1)
                A(s5q[:], s5y[:], ACT.Square).then_inc(s5_sq, 1)
                fox_probs(2)
                pT_copy(0)
                pT_copy(2)
                act.wait_ge(s5_ms, L + 1)
                link(A(s5m[:].rearrange("p m s -> p (m s)"), pb[:, 2, :], ACT.Ln, bias=eps))
                A(s5m[:], s5m[:], ACT.Exp, scale=-0.5).then_inc(s5_rstd, 1)
                sb_softplus(1)
                pT_copy(4)
                act.wait_ge(s5_norm, L + 1)
                for m in range(2):
                    A(act_hi[:, 6 + m, :], s5q[:, m, :], ACT.Copy, scale=col(L, S_GO + 6 + m)).then_inc(mix_hi, 1)
                hi(g0 + 2 * U_IN + 3, D_MODEL)
                mix_rms(0)
                sb_weights(1)
                mix_his(0)
                hi(g0 + 2 * U_IN + 4, D_MODEL)
                mix_his(1)
                hi(g0 + 2 * U_IN + 5, D_MODEL)
                mix_rms(1)
                mix_his(2)
                mix_his(3)
                for j in range(6, 8 + EARLY):
                    if L and j >= 8:
                        moe_hi(4 + j - 8)
                    else:
                        hi(g0 + 2 * U_IN + j, D_MODEL)

            exp_ln_table()
            norm_stats(0)
            act.wait_ge(small_in, 16)
            s5_exps(0)
            hT_his(0, 0, S_GA)
            attention(0)

            norm_stats(1)
            hT_his(1, 0, S_GF)
            g = 2 * U_FFN0 + EARLY
            for c in range(F_CHUNKS + 1):
                if c < F_CHUNKS:
                    for j in range(EARLY if c < 2 else 0, 8 if c else 8 + EARLY):
                        hi(g, HALF)
                        g += 1
                        if c == 5 and j % 2:
                            trig(1, j // 2)
                if c:
                    for j in range(4):
                        hi(g, HALF)
                        g += 1
                if c == F_CHUNKS:
                    for j in range(EARLY):
                        hi(g + j, 2 * SSM_WIDTH)
                if c < F_CHUNKS:
                    act.wait_ge(halves_used, ffn_done(2 * U_FFN0, c, 1, True))
                    if c:
                        act.wait_ge(d_hf, c)
                    A(d_sg[:], pb[:, 0:4, 0:SEQ], ACT.Silu).then_inc(d_silu, 1)
                if c == 2:
                    s5_exps(1)
                if c < F_CHUNKS:
                    act.wait_ge(d_hf, c + 1)
                    if c >= 2:
                        act.wait_ge(halves_used, ffn_done(2 * U_FFN0, c - 1, 2, True))
                    A(d_hi[:, c % 2], d_h[:], ACT.Copy).then_inc(d_hhi, 1)

            exp_ln_table()
            norm_stats(2)
            hT_his(2, 1, S_GA)
            attention(1)

            norm_stats(3)
            hT_his(3, 1, S_GF)
            act.wait_ge(r_d, 1)
            A(stat2[:, 8:10], stat2[:, 6:8], ACT.Exp).then_inc(r_e, 1)
            nc.scalar.preload_act_table(ACT.Silu)
            moe_hi(4 + EARLY)

            def item(i, first):
                hv = [4 + EARLY + 1 if first else 0]
                g0 = 2 * U_MOE if first else i * H_BODY + 2 * U_BASE1

                def his(n):
                    for _ in range(n):
                        moe_hi(hv[0], None if first else i)
                        hv[0] += 1

                def xg_hi_split(after):
                    act.wait_ge(m_staged, after)
                    A(xg_hi[:], stage[:], ACT.Copy).then_inc(m_xghi, 1)

                if first:
                    xg_hi_split(2)
                for c, before in steps():
                    q = i * F_CHUNKS + c
                    his(3 - EARLY if first and c == 0 else 4)
                    if c == 1 and not first:
                        act.wait_ge(halves_used, ffn_done(g0, 0, 2, False))
                        A(m_y[:], pb[:, 4:6, :], ACT.Copy).then_inc(m_ysb, 1)
                    his(4)
                    if c or not first:
                        act.wait_ge(m_T, q)
                        A(m_hi[:, before % 2 if c else 0], pb[:, 6, :], ACT.Copy).then_inc(m_hhi, 1)
                    if c == 5:
                        act.wait_ge(m_gtT, i + 1)
                        A(m_gt[:].rearrange("p t s -> p (t s)"), pb[:, 7, 0:2 * P], ACT.Copy).then_inc(m_gtc, 1)
                    act.wait_ge(halves_used, ffn_done(g0, c, 0, first))
                    if c or not first:
                        act.wait_ge(m_hf, q)
                    A(m_sg[:], pb[:, 2 * (c % 2), :], ACT.Silu).then_inc(m_silu, 1)
                    if c or not first:
                        his(4)
                act.wait_ge(halves_used, ffn_done(g0, F_CHUNKS - 1, 1, first))
                xg_hi_split(i * 2 + 4)

            item(0, True)
            act.wait_ge(r_table, 1)
            last = act.value_load(etab[0:1, ITEMS_MAX:ITEMS_MAX + 1], min_val=EXPERTS - 1, max_val=ITEMS_MAX - 2)
            with act.Fori(1, last + 1) as i:
                item(i, False)
            st = 2 * U_BASE1
            act.wait_ge(m_T, last * F_CHUNKS + F_CHUNKS)
            A(m_hi[:, 0], pb[:, 6, :], ACT.Copy).then_inc(m_hhi, 1)
            for j in range(4):
                moe_hi(H_BODY + j, last)
            act.wait_ge(halves_used, last * H_BODY + (H_BODY + st + 4))
            A(m_y[:], pb[:, 4:6, :], ACT.Copy).then_inc(m_ysb, 1)

        @block.vector
        def _(dve):
            V = nc.vector
            n_link = [0]

            def link(ins):
                n_link[0] += 1
                ins.then_inc(dve_seq, 1)
                dve.wait_ge(dve_seq, n_link[0])

            def split_lo(g, n, slot, src):
                dve.wait_ge(hi_ready, g + 1)
                V.tensor_tensor(wlo[:, slot, 0:n], src[:, g_part(slot) * n:(g_part(slot) + 1) * n],
                                whi[:, slot, 0:n].bitcast(F32), ALU.subtract).then_inc(lo_ready, 1)

            def lo(g, n):
                split_lo(g, n, g % RING, raw[:, g // 2 % RAW])

            def moe_lo(hv, item=None):
                g = 2 * U_BASE1 + hv
                split_lo(g if item is None else item * H_BODY + g, HALF, g % RING, moe_raw(hv // 2 % MOE_RAW))

            def norm_step(event, t, scale):
                if scale:
                    dve.wait_ge(x_rstd, 2 * event + t + 1)
                    V.tensor_scalar(h[:, t, :], x[:, t, :], stat[:, 8 + t:9 + t], None, ALU.mult).then_inc(normed, 1)
                else:
                    dve.wait_ge(x_sq, 2 * event + t + 1)
                    V.tensor_tensor(stat[:, 4 + t:5 + t], stat[:, 2 * t:2 * t + 1], stat[:, 2 * t + 1:2 * t + 2],
                                    ALU.add).then_inc(x_sum, 1)

            def hT_los(event, layer, gain):
                banks = XT_BANKS[event % 2]
                for k in range(KD):
                    dve.wait_ge(hT_hi, 8 * event + (k | 1) + 1)
                    b, o = banks[k // 2], (k % 2) * SEQ
                    V.scalar_tensor_tensor(act_lo[:, k, :], pb[:, b, o:o + SEQ], col(layer, gain + k),
                                           act_hi[:, k, :].bitcast(F32), ALU.mult, ALU.subtract).then_inc(hT_lo, 1)

            def tables(layer, step):
                th, n, phi, phi_hi, phi_lo = (s5s[:, i, :] for i in (2, 3, 6, 4, 5))
                k, part = divmod(step - 1, 3)
                ks = slice(2 * k, 2 * k + 2)
                if step == 0:
                    dve.wait_ge(s5_exp, layer + 1)
                    link(V.tensor_tensor(th, s5s[:, 0, :], col(layer, S_AIM, KD), ALU.mult))
                    link(V.tensor_scalar(n, th, 1.0 / TWO_PI, ROUND_ONE, ALU.mult, ALU.add))
                    link(V.tensor_scalar(n, n, ROUND_ONE, None, ALU.subtract))
                    for two_pi in (TWO_PI_A, TWO_PI_B, TWO_PI_C):
                        link(V.scalar_tensor_tensor(th, n, -two_pi, th, ALU.mult, ALU.add))
                    link(V.tensor_scalar(phi, th, 1.0 / TWO_PI, None, ALU.mult))
                    link(V.tensor_scalar(phi, phi, 0.5, -0.5, ALU.min, ALU.max))
                    link(V.tensor_scalar(phi_hi, phi, ROUND_12, ROUND_12, ALU.add, ALU.subtract))
                    V.tensor_tensor(phi_lo, phi, phi_hi, ALU.subtract).then_inc(tab_ang, 1)
                    dve.wait_ge(tab_ang, 5 * layer + 1)
                elif part == 0:
                    for kk in (2 * k, 2 * k + 1):
                        last = V.tensor_scalar(ang[:, kk, :], trow, phi_hi[:, kk:kk + 1], None, ALU.mult)
                    link(last)
                    link(V.tensor_scalar(rnd[:, ks], ang[:, ks], ROUND_ONE, ROUND_ONE, ALU.add, ALU.subtract))
                elif part == 1:
                    link(V.tensor_tensor(ang[:, ks], ang[:, ks], rnd[:, ks], ALU.subtract))
                    for kk in (2 * k, 2 * k + 1):
                        last = V.scalar_tensor_tensor(ang[:, kk, :], trow, phi_lo[:, kk:kk + 1], ang[:, kk, :],
                                                      ALU.mult, ALU.add)
                    link(last)
                else:
                    link(V.tensor_scalar(rnd[:, ks], ang[:, ks], ROUND_ONE, ROUND_ONE, ALU.add, ALU.subtract))
                    V.tensor_tensor(rnd[:, ks], ang[:, ks], rnd[:, ks], ALU.subtract).then_inc(tab_ang, 1)

            def coefs(layer):
                dve.wait_ge(s5_trig, 2 * layer + 2)
                are, aim = col(layer, S_ARE, KD), col(layer, S_AIM, KD)
                mag, sn, sh = s5s[:, 1, :], s5s[:, 8, :], s5s[:, 9, :]
                cs, nr, ni, den, cr, ci, t1 = (s5s[:, i, :] for i in (10, 11, 12, 13, 14, 15, 7))
                link(V.tensor_tensor(cs, sh, sh, ALU.mult))
                link(V.tensor_scalar(cs, cs, -2.0, 1.0, ALU.mult, ALU.add))
                link(V.tensor_tensor(nr, mag, cs, ALU.mult))
                link(V.tensor_scalar(nr, nr, -1.0, None, ALU.add))
                link(V.tensor_tensor(ni, mag, sn, ALU.mult))
                link(V.tensor_tensor(den, are, are, ALU.mult))
                link(V.tensor_tensor(t1, aim, aim, ALU.mult))
                link(V.tensor_tensor(den, den, t1, ALU.add))
                link(V.reciprocal(den, den))
                link(V.tensor_tensor(cr, nr, are, ALU.mult))
                link(V.tensor_tensor(t1, ni, aim, ALU.mult))
                link(V.tensor_tensor(cr, cr, t1, ALU.add))
                link(V.tensor_tensor(cr, cr, den, ALU.mult))
                link(V.tensor_tensor(ci, ni, are, ALU.mult))
                link(V.tensor_tensor(t1, nr, aim, ALU.mult))
                link(V.tensor_tensor(ci, ci, t1, ALU.subtract))
                link(V.tensor_tensor(ci, ci, den, ALU.mult))
                dve.wait_ge(cmat_in, 16 * (layer + 1))
                shape = [P, KD, 32]
                crb = cr.unsqueeze(2).broadcast_to(shape)
                cib = ci.unsqueeze(2).broadcast_to(shape)
                link(V.tensor_tensor(cbar[:, 0], cmat[:, 0], crb, ALU.mult))
                link(V.tensor_tensor(cbar[:, 1], cmat[:, 1], cib, ALU.mult))
                link(V.tensor_tensor(cbar[:, 0], cbar[:, 0], cbar[:, 1], ALU.subtract))
                link(V.tensor_scalar(cbar[:, 1], cbar[:, 0], -1.0, None, ALU.mult))
                link(V.tensor_tensor(cbar[:, 2], cmat[:, 0], cib, ALU.mult))
                link(V.tensor_tensor(cmat[:, 1], cmat[:, 1], crb, ALU.mult))
                link(V.tensor_tensor(cbar[:, 2], cbar[:, 2], cmat[:, 1], ALU.add))
                V.tensor_scalar(cbar[:, 2], cbar[:, 2], -1.0, None, ALU.mult).then_inc(cbar_ready, 1)

            def s5_piece(layer, q, piece):
                cs = tabc[:, 2 * q:2 * q + 2, :].rearrange("p k s -> p (k s)")
                sn = tabs[:, 2 * q:2 * q + 2, :].rearrange("p k s -> p (k s)")
                w = [s5w[:, i].rearrange("p k s -> p (k s)") for i in range(6)]
                w += [s5w2[:, i].rearrange("p k s -> p (k s)") for i in range(2)]
                if piece == 0:
                    dve.wait_ge(bu_ready, 4 * layer + q + 1)
                    dve.wait_ge(tab_ready, 4 * layer + 4)
                    if q:
                        dve.wait_ge(s5_prod, 4 * layer + q)
                    V.tensor_tensor(w[0], pb[:, 5, :], cs, ALU.mult)
                    V.tensor_tensor(w[1], pb[:, 6, :], sn, ALU.mult)
                    V.tensor_tensor(w[2], pb[:, 6, :], cs, ALU.mult)
                    V.tensor_tensor(w[3], pb[:, 5, :], sn, ALU.mult).then_inc(bu_read, 1)
                elif piece == 1:
                    dve.wait_ge(bu_read, 4 * layer + q + 1)
                    link(V.tensor_tensor(w[0], w[0], w[1], ALU.add))
                    link(V.tensor_tensor(w[2], w[2], w[3], ALU.subtract))
                elif piece == 2:
                    for dst, src in ((1, 0), (3, 2)):
                        for k in range(2):
                            mag = s5s[:, 1, 2 * q + k:2 * q + k + 1]
                            last = V.tensor_tensor_scan(s5w[:, dst, k, :], mag.broadcast_to([P, SEQ]),
                                                        s5w[:, src, k, :], 0.0, ALU.mult, ALU.add)
                    link(last)
                else:
                    if q:
                        dve.wait_ge(s5_used, 4 * layer + q)
                    V.tensor_tensor(w[6], w[1], cs, ALU.mult)
                    V.tensor_tensor(w[7], w[3], sn, ALU.mult)
                    V.tensor_tensor(w[4], w[1], sn, ALU.mult)
                    V.tensor_tensor(w[5], w[3], cs, ALU.mult).then_inc(s5_prod, 1)

            def attention(layer):
                L = layer
                g0 = 2 * u_attn(L)
                W = [n for _, n in CHUNKS]

                def lo_w(chunk, j):
                    lo(g0 + 4 * chunk + j, 2 * W[chunk])

                def qk_sums(j):
                    dve.wait_ge(qk_sq, 2 * L + j)
                    o = 12 * (j - 1)
                    V.tensor_reduce(stat2[:, o:o + 12], fsq[:].rearrange("p t (h d) -> p (t h) d", d=HEAD_DIM),
                                    AX.X, ALU.add).then_inc(qk_sum, 1)

                def qk_norm(j, b):
                    dve.wait_ge(qk_rstd, 2 * L + j)
                    o = 12 * (j - 1)
                    if j == 1:
                        link(V.tensor_scalar(stat2[:, 0:12], stat2[:, 0:12], HEAD_DIM ** -0.5, None, ALU.mult))
                    for t in range(TILES):
                        r = stat2[:, o + 6 * t:o + 6 * t + 6].unsqueeze(2).broadcast_to([P, HEADS, HEAD_DIM])
                        last = V.tensor_tensor(qk[:, t, HEADS * (j - 1):HEADS * j, 0:HEAD_DIM],
                                               pb[:, b + t, 0:HEADS_WIDTH].rearrange("p (h d) -> p h d", d=HEAD_DIM),
                                               r, ALU.mult)
                    last.then_inc(qk_normed, 1)

                for chunk in range(len(CHUNKS)):
                    q = chunk - (S5_CHUNK0, S5_CHUNK1)[L]
                    for j in range(4):
                        if L == 0 or chunk or j >= EARLY:
                            lo_w(chunk, j)
                        if L == 0:
                            n = 4 * chunk + j
                            for step in range(n if n < 4 else 2 * n - 4, n + 1 if n < 4 else 2 * n - 2):
                                if step < TABLE_STEPS:
                                    tables(0, step)
                            if (chunk, j) == (FK, 1):
                                coefs(0)
                        if (chunk, j) == (FVG, 0):
                            qk_norm(FQ, 2)
                        if (chunk, j) == (SQ, 0):
                            qk_norm(FK, 0)
                        if j == 0 and 1 <= q <= 4:
                            s5_piece(L, q - 1, 3)
                        if j > 0 and 0 <= q <= 3:
                            s5_piece(L, q, j - 1)
                        if (chunk, j) == (FK, 3):
                            qk_sums(FQ)
                        if (chunk, j) == (FVG, 3):
                            qk_sums(FK)
                        if (chunk, j) == (SQ, 3):
                            dve.wait_ge(fv_copied, L + 1)
                            bf = col(L, S_BF, HEADS).unsqueeze(1).broadcast_to([P, TILES, HEADS])
                            V.tensor_tensor(gatez[:], pb[:, 2:4, HEADS_WIDTH:HEADS_WIDTH + HEADS], bf,
                                            ALU.add).then_inc(gate_read, 1)
                        if (chunk, j) == (SK, 3):
                            dve.wait_ge(gate_l, L + 1)
                            V.scalar_tensor_tensor(logf[:], gatez[:], 0.0, gatel[:], ALU.min,
                                                   ALU.subtract).then_inc(logf_ready, 1)
                if L == 0:
                    s5_piece(0, 3, 3)
                V.memset(qk[:, :, 0:HEADS, 65], 1.0)
                V.memset(qk[:, :, HEADS:, 64], 1.0)
                dve.wait_ge(c_ready, L + 1)
                cps = pb[:, 2, 0:2 * HEADS].rearrange("p (t h) -> p t h", t=TILES)
                V.tensor_copy(qk[:, :, 0:HEADS, 64], cps)
                V.tensor_scalar(qk[:, :, HEADS:, 65], cps, -1.0, None, ALU.mult).then_inc(aug_ready, 1)
                lo(g0 + 2 * U_IN, D_MODEL)
                for m in range(2):
                    if m == 0:
                        dve.wait_ge(s5_used, 4 * L + 4)
                    V.scalar_tensor_tensor(s5y[:, m, :], uT[:, m, :], col(L, S_DSK + m),
                                           pb[:, 7, m * SEQ:(m + 1) * SEQ], ALU.mult, ALU.add).then_inc(s5_y, 1)
                for hd in range(HEADS):
                    dve.wait_ge(foxT_ready, HEADS * L + hd + 1)
                    V.tensor_scalar(fT[:, hd, :], pb[0:AUG, 3 + hd % 2, 0:SEQ], small[0:AUG, L, S_GQ:S_GQ + 1],
                                    None, ALU.mult)
                    V.tensor_scalar(fT[:, HEADS + hd, :], pb[0:AUG, 3 + hd % 2, SEQ:2 * SEQ],
                                    small[0:AUG, L, S_GK:S_GK + 1], None, ALU.mult).then_inc(fT_copied, 1)

                def sb_plus(b):
                    dve.wait_ge(sb_l, 2 * L + b + 1)
                    if b:
                        dve.wait_ge(a_ready, 2 * L + b)
                    V.scalar_tensor_tensor(sb_sp[:], pb[:, 5:8, 0:3 * P], 0.0, sb_u[:], ALU.max,
                                           ALU.add).then_inc(sp_ready, 1)

                def fox_maxima(grp):
                    dve.wait_ge(logits_ready, 3 * L + grp + 1)
                    b = FOX_BANKS[grp]
                    V.tensor_reduce(fox_nmax[:, grp, 0, :], pb[:, b:b + 2, 0:P], AX.X, ALU.max)
                    link(V.tensor_reduce(fox_nmax[:, grp, 1, :], pb[:, b:b + 2, P:3 * P], AX.X, ALU.max))
                    V.tensor_scalar(fox_nmax[:, grp], fox_nmax[:, grp], -1.0, None, ALU.mult).then_inc(fox_max, 1)

                def pT_copy(hd):
                    dve.wait_ge(pT_ready, HEADS * L + hd + 1)
                    V.tensor_copy(pT[:, hd, :], pb[:, 4, 0:3 * P]).then_inc(pT_odd, 1)

                def sby_copy(b):
                    dve.wait_ge(sby_ready, 2 * L + b + 1)
                    c = HEADS_WIDTH + b * SBW
                    V.tensor_copy(ymix[:, :, c:c + SBW],
                                  pb[:, SBY_BANKS[b], 0:2 * SBW].rearrange("p (t d) -> p t d", t=TILES)
                                  ).then_inc(sby_done, 1)

                def mix_sums(m):
                    dve.wait_ge(mix_sq, 2 * L + m + 1)
                    for t in range(TILES):
                        o = 12 * m + 6 * t
                        last = V.tensor_reduce(
                            stat2[:, o:o + 6],
                            sqtmp[:, t, m * HEADS_WIDTH:(m + 1) * HEADS_WIDTH].rearrange("p (h d) -> p h d", d=HEAD_DIM),
                            AX.X, ALU.add)
                    last.then_inc(mix_sum, 1)

                def mix_scale(m):
                    dve.wait_ge(mix_rstd, 2 * L + m + 1)
                    for t in range(TILES):
                        o = 12 * m + 6 * t
                        ym = ymix[:, t, m * HEADS_WIDTH:(m + 1) * HEADS_WIDTH].rearrange("p (h d) -> p h d", d=HEAD_DIM)
                        last = V.tensor_tensor(ym, ym, stat2[:, o:o + 6].unsqueeze(2).broadcast_to([P, HEADS, HEAD_DIM]),
                                               ALU.mult)
                    last.then_inc(mix_ready, 1)

                def mix_los(part):
                    dve.wait_ge(mix_hi, 8 * L + 3 + MIX_PARTS[part][1][-1])
                    for i, k in enumerate(MIX_PARTS[part][1]):
                        V.scalar_tensor_tensor(act_lo[:, k, :], pb[:, MIX_PARTS[part][0], i * SEQ:(i + 1) * SEQ],
                                               col(L, S_GO + k), act_hi[:, k, :].bitcast(F32), ALU.mult,
                                               ALU.subtract).then_inc(mix_lo, 1)

                lo(g0 + 2 * U_IN + 1, D_MODEL)
                fox_maxima(0)
                fox_maxima(1)
                sb_plus(0)
                lo(g0 + 2 * U_IN + 2, D_MODEL)
                dve.wait_ge(glu_sig, 2 * L + 2)
                V.tensor_tensor(s5y[:], s5g[:], s5sg[:], ALU.mult).then_inc(s5_r, 1)
                fox_maxima(2)
                pT_copy(1)
                pT_copy(3)
                dve.wait_ge(s5_rstd, L + 1)
                V.tensor_tensor(s5q[:], s5y[:], s5m[:], ALU.mult).then_inc(s5_norm, 1)
                sby_copy(0)
                dve.wait_ge(fox_p, 3 * L + 3)
                link(V.reciprocal(fox_rs[:], fox_rs[:]))
                pT_copy(5)
                dve.wait_ge(foxy_ready, L + 1)
                for t in range(TILES):
                    r = fox_rs[:, t, :].unsqueeze(2).broadcast_to([P, HEADS, HEAD_DIM])
                    last = V.tensor_tensor(ymix[:, t, 0:HEADS_WIDTH].rearrange("p (h d) -> p h d", d=HEAD_DIM),
                                           pb[:, t, 0:HEADS_WIDTH].rearrange("p (h d) -> p h d", d=HEAD_DIM),
                                           r, ALU.mult)
                last.then_inc(foxy_done, 1)
                sb_plus(1)
                for m in range(2):
                    dve.wait_ge(mix_hi, 8 * L + m + 1)
                    V.scalar_tensor_tensor(act_lo[:, 6 + m, :], s5q[:, m, :], col(L, S_GO + 6 + m),
                                           act_hi[:, 6 + m, :].bitcast(F32), ALU.mult,
                                           ALU.subtract).then_inc(mix_lo, 1)
                mix_sums(0)
                lo(g0 + 2 * U_IN + 3, D_MODEL)
                mix_scale(0)
                mix_los(0)
                mix_los(1)
                lo(g0 + 2 * U_IN + 4, D_MODEL)
                sby_copy(1)
                mix_sums(1)
                lo(g0 + 2 * U_IN + 5, D_MODEL)
                mix_scale(1)
                mix_los(2)
                mix_los(3)
                for j in range(6, 8 + EARLY):
                    if L and j >= 8:
                        moe_lo(4 + j - 8)
                    else:
                        lo(g0 + 2 * U_IN + j, D_MODEL)

            def residual_and_norm(n):
                def add(t, nh):
                    if nh == 0:
                        if t == 0:
                            dve.wait_ge(out_tile0, n + 1)
                        else:
                            dve.wait_ge(halves_used, out_done_at(n))
                    xs = x[:, t, nh * BANK:(nh + 1) * BANK]
                    bank = 4 + 2 * t + nh if n == 1 else OUT_BANKS[2 * t + nh]
                    V.tensor_tensor(xs, xs, pb[:, bank, :], ALU.add).then_inc(x_done, 1)

                add(0, 0)
                add(0, 1)
                norm_step(n + 1, 0, False)
                add(1, 0)
                norm_step(n + 1, 0, True)
                add(1, 1)
                norm_step(n + 1, 1, False)
                norm_step(n + 1, 1, True)

            dve.wait_ge(const_in, 16)
            dve.wait_ge(small_in, 16)
            for t in range(TILES):
                norm_step(0, t, False)
                norm_step(0, t, True)
            hT_los(0, 0, S_GA)
            attention(0)
            residual_and_norm(0)
            hT_los(1, 0, S_GF)
            g = 2 * U_FFN0 + EARLY
            for c in range(F_CHUNKS + 1):
                if c < F_CHUNKS:
                    for j in range(EARLY if c < 2 else 0, 8 if c else 8 + EARLY):
                        lo(g, HALF)
                        g += 1
                        if c in (3, 4) and 8 * (c - 3) + j < TABLE_STEPS:
                            tables(1, 8 * (c - 3) + j)
                        if c == 6 and j == 1:
                            coefs(1)
                if c:
                    for j in range(4):
                        lo(g, HALF)
                        g += 1
                if c == F_CHUNKS:
                    for j in range(EARLY):
                        lo(g + j, 2 * SSM_WIDTH)
                if c < F_CHUNKS:
                    dve.wait_ge(d_silu, c + 1)
                    if c:
                        dve.wait_ge(d_hlo, c)
                    V.tensor_tensor(d_h[:], d_sg[:], pb[:, 0:4, SEQ:2 * SEQ], ALU.mult).then_inc(d_hf, 1)
                    dve.wait_ge(d_hhi, c + 1)
                    V.tensor_tensor(d_lo[:, c % 2], d_h[:], d_hi[:, c % 2].bitcast(F32),
                                    ALU.subtract).then_inc(d_hlo, 1)
            residual_and_norm(1)
            hT_los(2, 1, S_GA)
            attention(1)
            residual_and_norm(2)

            R = smalls_r
            lg, lg2, e8, w8, sel1, sel2, sel, gates, posm = (R[:, i, :, 0:EXPERTS] for i in range(9))
            shape = [P, TILES, EXPERTS]
            revb = rev.unsqueeze(1).broadcast_to(shape)

            def bc(a):
                return a.unsqueeze(2).broadcast_to(shape)

            def argmax(src, m, dst):
                link(V.tensor_reduce(m, src, AX.X, ALU.max))
                link(V.tensor_tensor(e8, src, bc(m), ALU.is_equal))
                link(V.tensor_tensor(w8, e8, revb, ALU.mult))
                link(V.tensor_reduce(stat2[:, 4:6], w8, AX.X, ALU.max))
                link(V.tensor_tensor(dst, w8, bc(stat2[:, 4:6]), ALU.is_equal))

            dve.wait_ge(r_logits, 1)
            link(V.tensor_copy(lg, pb[:, 7, 0:2 * EXPERTS].rearrange("p (t e) -> p t e", t=TILES)))
            argmax(lg, stat2[:, 0:2], sel1)
            link(V.scalar_tensor_tensor(lg2, sel1, -3e38, lg, ALU.mult, ALU.add))
            argmax(lg2, stat2[:, 2:4], sel2)
            V.tensor_tensor(sel, sel1, sel2, ALU.add).then_inc(r_sel, 1)
            V.tensor_tensor(stat2[:, 6:8], stat2[:, 2:4], stat2[:, 0:2], ALU.subtract).then_inc(r_d, 1)
            moe_lo(4 + EARLY)
            dve.wait_ge(r_cnt, 1)
            link(V.scalar_tensor_tensor(posm, sel, -1e6,
                                        pb[:, 7, 0:2 * EXPERTS].rearrange("p (t e) -> p t e", t=TILES),
                                        ALU.mult, ALU.add))
            link(V.tensor_scalar(posm, posm, 1e6 - 1.0, None, ALU.add))
            link(V.tensor_copy(pos_i[:, :, 0:EXPERTS], posm))
            ovr, inc, oh = (R[:, 9, 0, 0:EXPERTS], R[:, 9, 1, 0:EXPERTS], R[:, 10, 0, 0:EXPERTS])
            link(V.tensor_scalar(ovr, pb[:, 7, 2 * EXPERTS:3 * EXPERTS], float(CAP), None, ALU.is_gt))
            ef = R[:, 11].rearrange("p t e -> p (t e)")

            def gate_values():
                dve.wait_ge(r_e, 1)
                link(V.tensor_scalar(stat2[:, 10:12], stat2[:, 8:10], 1.0, None, ALU.add))
                link(V.reciprocal(stat2[:, 10:12], stat2[:, 10:12]))
                link(V.tensor_tensor(stat2[:, 12:14], stat2[:, 8:10], stat2[:, 10:12], ALU.mult))
                link(V.tensor_tensor(gates, sel1, bc(stat2[:, 10:12]), ALU.mult))
                link(V.tensor_tensor(e8, sel2, bc(stat2[:, 12:14]), ALU.mult))
                link(V.tensor_tensor(gates, gates, e8, ALU.add))
                link(V.tensor_copy(gate_i[:, :, 0:EXPERTS], gates))

            def item_table():
                link(V.tensor_tensor_scan(inc, ones[:, 0:EXPERTS], ovr, 0.0, ALU.mult, ALU.add))
                link(V.memset(ef, 0.0))
                link(V.tensor_copy(ef[:, 0:EXPERTS], eidx))
                link(V.tensor_scalar(ef[:, ITEMS_MAX:ITEMS_MAX + 1], inc[:, EXPERTS - 1:EXPERTS],
                                     float(EXPERTS - 1), None, ALU.add))

            def second_item(j):
                it = EXPERTS + j
                link(V.scalar_tensor_tensor(oh, inc, float(j + 1), ovr, ALU.is_equal, ALU.mult))
                ohb = oh.unsqueeze(1).broadcast_to(shape)
                link(V.tensor_tensor(e8, posm, ohb, ALU.mult))
                link(V.tensor_reduce(stat2[:, 14:16], e8, AX.X, ALU.add))
                link(V.tensor_scalar(pos_i[:, :, it], stat2[:, 14:16], -float(CAP), None, ALU.add))
                link(V.tensor_tensor(e8, gates, ohb, ALU.mult))
                link(V.tensor_reduce(gate_i[:, :, it], e8, AX.X, ALU.add))
                link(V.tensor_tensor(w8[:, 0, :], oh, eidx, ALU.mult))
                link(V.tensor_reduce(ef[:, it:it + 1], w8[:, 0, :], AX.X, ALU.add))
                if it == ITEMS_MAX - 1:
                    V.tensor_copy(etab[0:1, 0:16], ef[0:1, 0:16]).then_inc(r_table, 1)

            def onehot(i):
                for t in range(TILES):
                    last = V.tensor_scalar(m_pm[:, t, :], iota, pos_i[:, t, bass.ds(i, 1)], None, ALU.is_equal)
                last.then_inc(m_pmr, 1)

            def stage_half(k, event):
                dve.wait_ge(m_gather, event)
                ga = col(1, S_GF + 4 * k, 4).unsqueeze(2).broadcast_to([P, 4, P])
                V.tensor_tensor(stage[:, 4 * k:4 * k + 4, :], pb[:, 7, :].rearrange("p (k s) -> p k s", k=4),
                                ga, ALU.mult).then_inc(m_staged, 1)

            def xg_lo_split(event):
                dve.wait_ge(m_xghi, event)
                V.tensor_tensor(xg_lo[:], stage[:], xg_hi[:].bitcast(F32), ALU.subtract).then_inc(m_xglo, 1)

            def add_piece(p, event):
                t, nh = p // 2, p % 2
                dve.wait_ge(m_scat, event)
                xs = x[:, t, nh * BANK:(nh + 1) * BANK]
                V.tensor_tensor(xs, xs, pb[:, 7, :], ALU.add).then_inc(m_added, 1)

            onehot(0)
            stage_half(0, 1)
            stage_half(1, 2)
            xg_lo_split(1)

            def item(i, first):
                hv = [4 + EARLY + 1 if first else 0]
                g0 = 2 * U_MOE if first else i * H_BODY + 2 * U_BASE1

                def los(n, router=False):
                    for k in range(n):
                        if router:
                            second_item(k)
                        moe_lo(hv[0], None if first else i)
                        hv[0] += 1

                for c, before in steps():
                    q = i * F_CHUNKS + c
                    los(3 - EARLY if first and c == 0 else 4)
                    if not first and 2 <= c <= 5:
                        add_piece(c - 2, i * 4 + (c - 5))
                    if c == 6:
                        stage_half(0, i * 2 + 3)
                    if first and c == 0:
                        gate_values()
                        item_table()
                    los(4, first and c == 0)
                    if c or not first:
                        dve.wait_ge(m_hhi, q)
                        b = before % 2 if c else 0
                        V.tensor_tensor(m_lo[:, b], pb[:, 6, :], m_hi[:, b].bitcast(F32),
                                        ALU.subtract).then_inc(m_hlo, 1)
                    if c == 3:
                        for t in range(TILES):
                            last = V.tensor_scalar(m_gp[:, t, :], iota, pos_i[:, t, bass.ds(i, 1)],
                                                   gate_i[:, t, bass.ds(i, 1)], ALU.is_equal, ALU.mult)
                        onehot(i + 1)
                    if c == 6:
                        stage_half(1, i * 2 + 4)
                    if c or not first:
                        los(4)
                    dve.wait_ge(m_silu, q + 1)
                    dve.wait_ge(halves_used, ffn_done(g0, c, 1, first))
                    if c or not first:
                        dve.wait_ge(m_T, q)
                    V.tensor_tensor(m_h[:], m_sg[:], pb[:, 2 * (c % 2) + 1, :], ALU.mult).then_inc(m_hf, 1)
                xg_lo_split(i + 2)

            item(0, True)
            dve.wait_ge(r_table, 1)
            last = dve.value_load(etab[0:1, ITEMS_MAX:ITEMS_MAX + 1], min_val=EXPERTS - 1, max_val=ITEMS_MAX - 2)
            with dve.Fori(1, last + 1) as i:
                item(i, False)
            dve.wait_ge(m_hhi, last * F_CHUNKS + F_CHUNKS)
            V.tensor_tensor(m_lo[:, 0], pb[:, 6, :], m_hi[:, 0].bitcast(F32), ALU.subtract).then_inc(m_hlo, 1)
            for j in range(4):
                moe_lo(H_BODY + j, last)
            for p in range(4):
                add_piece(p, last * 4 + (p + 1))

        @block.tensor
        def _(pe):
            M = nc.tensor.matmul

            def T(out, in_, n=P):
                return nc.tensor.transpose(out, in_, ident)

            def three(out, lhs, rhs, start, stop):
                (lh, ll), (rh, rl) = lhs, rhs
                M(out, lh, rh, start=start, stop=False)
                M(out, lh, rl, start=False, stop=False)
                return M(out, ll, rh, start=False, stop=stop)

            def wpair(slot, a, b):
                return whi[:, slot, a:b], wlo[:, slot, a:b]

            def apair(k, a, b):
                return act_hi[:, k, a:b], act_lo[:, k, a:b]

            def transposes(event):
                banks = XT_BANKS[event % 2]
                for t in range(TILES):
                    pe.wait_ge(normed, 2 * event + t + 1)
                    for k in range(KD):
                        last = T(pb[:, banks[k // 2], (k % 2) * SEQ + t * P:(k % 2) * SEQ + (t + 1) * P],
                                 h[:, t, k * P:(k + 1) * P])
                        if k % 2 and t:
                            last.then_inc(xT_ready, 1)

            def attention(layer):
                L = layer
                g0 = 2 * u_attn(L)

                def middle(chunk):
                    if chunk == FQ:
                        for m in range(2):
                            for t in range(TILES):
                                last = T(pb[:, 4, m * SEQ + t * P:m * SEQ + (t + 1) * P],
                                         su[:, t, m * P:(m + 1) * P])
                        last.then_inc(uT_ready, 1)
                    q = chunk - (S5_CHUNK0, S5_CHUNK1)[L]
                    if 1 <= q <= 4:
                        s5y_part(q - 1)

                def project(chunk, banks):
                    n = CHUNKS[chunk][1]
                    for j in range(4):
                        if j == 2:
                            middle(chunk)
                        g = g0 + 4 * chunk + j
                        pe.wait_ge(lo_ready, g + 1)
                        for t in range(TILES):
                            for kk in range(2):
                                k = 2 * j + kk
                                if chunk == 0 and t == 0:
                                    pe.wait_ge(hT_lo, 8 * (2 * L) + k + 1)
                                last = three(pb[:, banks[t], 0:n], apair(k, t * P, (t + 1) * P),
                                             wpair(g % RING, kk * n, (kk + 1) * n), k == 0, k == KD - 1)
                        last.then_inc(halves_used, 1)

                def project_T(chunk, banks):
                    n = CHUNKS[chunk][1]
                    for j in range(4):
                        if j == 2:
                            middle(chunk)
                        g = g0 + 4 * chunk + j
                        pe.wait_ge(lo_ready, g + 1)
                        for pr in range(3):
                            for kk in range(2):
                                k = 2 * j + kk
                                last = three(pb[:, banks[pr], 0:SEQ],
                                             wpair(g % RING, kk * n + pr * P, kk * n + (pr + 1) * P),
                                             apair(k, 0, SEQ), k == 0, k == KD - 1)
                        last.then_inc(halves_used, 1)

                def bu(q):
                    if q == 0:
                        pe.wait_ge(uT_copied, L + 1)
                        pe.wait_ge(bmat_in, 16 * (L + 1))
                    else:
                        pe.wait_ge(bu_read, 4 * L + q)
                    for kk in range(2):
                        m, j = divmod(2 * q + kk, 4)
                        if kk:
                            pe.wait_ge(bu_first, 4 * L + q + 1)
                        for ri in range(2):
                            last = M(pb[:, 5 + ri, kk * SEQ:(kk + 1) * SEQ], bmat[32 * j:32 * j + 32, ri, m, :],
                                     uT[32 * j:32 * j + 32, m, :], start=True, stop=True)
                        last.then_inc((bu_first, bu_ready)[kk], 1)

                def s5y_part(q):
                    pe.wait_ge(s5_prod, 4 * L + q + 1)
                    if q == 0:
                        pe.wait_ge(cbar_ready, L + 1)
                    for kk in range(2):
                        k = 2 * q + kk
                        m, j = divmod(k, 4)
                        for n, (ci, w) in enumerate(((0, s5w2[:, 0]), (1, s5w2[:, 1]), (2, s5w[:, 4]),
                                                     (2, s5w[:, 5]))):
                            last = M(pb[32 * j:32 * j + 32, 7, m * SEQ:(m + 1) * SEQ], cbar[:, ci, k, :],
                                     w[:, kk, :], start=(n == 0), stop=(n == 3))
                    last.then_inc(s5_used, 1)

                def before(chunk):
                    q = chunk - (S5_CHUNK0, S5_CHUNK1)[L]
                    if 0 <= q <= 3:
                        bu(q)

                project(SU, (4, 5))
                pe.wait_ge(su_copied, L + 1)
                project(FQ, (2, 3))
                before(FK)
                project(FK, (0, 1))
                before(FVG)
                pe.wait_ge(qk_normed, 2 * L + 1)
                project(FVG, (2, 3))
                before(SQ)
                pe.wait_ge(qk_normed, 2 * L + 2)
                project_T(SQ, (0, 1, 4))
                before(SK)
                pe.wait_ge(fv_copied, L + 1)
                pe.wait_ge(gate_read, L + 1)
                pe.wait_ge(sq_copied, 2 * L + 2)
                project_T(SK, (2, 3, 4))
                before(SV)
                project(SV, (0, 1))
                pe.wait_ge(logf_ready, L + 1)
                pe.wait_ge(sk_copied, 2 * L + 2)
                M(pb[:, 2, 0:HEADS], tri, logf[:, 0, :], start=True, stop=True)
                M(pb[:, 2, HEADS:2 * HEADS], tri, logf[:, 1, :], start=True, stop=False)
                M(pb[:, 2, HEADS:2 * HEADS], ones, logf[:, 0, :], start=False, stop=True).then_inc(c_ready, 1)
                if L == 0:
                    s5y_part(3)

                def sb_logits(b):
                    for j in range(3):
                        hd = 3 * b + j
                        r0, pr = HEAD_DIM * (hd % 2), hd // 2
                        for kt in range(2):
                            o, n = (0, 2 * P) if kt == 0 else (2 * P, P)
                            M(pb[:, 5 + j, o:o + n], skT[r0:r0 + HEAD_DIM, pr, kt * P:(kt + 1) * P],
                              sqT[r0:r0 + HEAD_DIM, pr, kt * P:SEQ], start=(kt == 0), stop=False,
                              skip_group_check=True)
                            last = M(pb[:, 5 + j, o:o + P], ident, smask, start=False, stop=(kt == 1),
                                     skip_group_check=True)
                    last.then_inc(z_ready, 1)

                def sb_sums(b):
                    pe.wait_ge(sp_ready, 2 * L + b + 1)
                    for j in range(3):
                        bank = 5 + j
                        M(pb[:, bank, 0:2 * P], nrev, sb_sp[:, j, 0:2 * P], start=False, stop=False,
                          skip_group_check=True)
                        M(pb[:, bank, P:2 * P], nones, sb_sp[:, j, 2 * P:3 * P], start=False, stop=False,
                          skip_group_check=True)
                        last = M(pb[:, bank, 2 * P:3 * P], nrev, sb_sp[:, j, 2 * P:3 * P], start=False, stop=True,
                                 skip_group_check=True)
                    last.then_inc(a_ready, 1)

                def sb_values(b):
                    bank = SBY_BANKS[b]
                    for j in range(3):
                        hd = 3 * b + j
                        c0, o = hd * HEAD_DIM, j * HEAD_DIM
                        M(pb[:, bank, o:o + HEAD_DIM], sb_a[:, j, 0:P], sv[:, 0, c0:c0 + HEAD_DIM],
                          start=True, stop=True)
                        M(pb[:, bank, SBW + o:SBW + o + HEAD_DIM], sb_a[:, j, P:2 * P], sv[:, 0, c0:c0 + HEAD_DIM],
                          start=True, stop=False)
                        last = M(pb[:, bank, SBW + o:SBW + o + HEAD_DIM], sb_a[:, j, 2 * P:3 * P],
                                 sv[:, 1, c0:c0 + HEAD_DIM], start=False, stop=True)
                    last.then_inc(sby_ready, 1)

                def fox_logits(grp):
                    for j in range(2):
                        hd = 2 * grp + j
                        bank = FOX_BANKS[grp] + j
                        pe.wait_ge(fT_copied, HEADS * L + (HEADS if grp else hd + 1))
                        for t in range(TILES):
                            o, n = (0, P) if t == 0 else (P, 2 * P)
                            M(pb[:, bank, o:o + n], fT[:, hd, t * P:(t + 1) * P], fT[:, HEADS + hd, 0:n],
                              start=True, stop=False)
                            last = M(pb[:, bank, o + n - P:o + n], ident, fmask, start=False, stop=True)
                    last.then_inc(logits_ready, 1)

                def prob_transposes(hd):
                    if hd >= 2:
                        pe.wait_ge((pT_even, pT_odd)[hd % 2], 3 * L + hd // 2)
                    for blk_ in range(3):
                        last = T(pb[:, 3 + hd % 2, blk_ * P:(blk_ + 1) * P], pf[:, hd, blk_ * P:(blk_ + 1) * P])
                    last.then_inc(pT_ready, 1)

                def mix_transposes(part):
                    bank, ks = MIX_PARTS[part]
                    for i, k in enumerate(ks):
                        for t in range(TILES):
                            last = T(pb[:, bank, i * SEQ + t * P:i * SEQ + (t + 1) * P], ymix[:, t, k * P:(k + 1) * P])
                    last.then_inc(mixT_ready, 1)

                def out_project(j):
                    k = OUT_K_ORDER[j]
                    g = g0 + 2 * U_IN + j
                    pe.wait_ge(lo_ready, g + 1)
                    pe.wait_ge(mix_lo, 8 * L + j + 1)
                    for t in range(TILES):
                        for nh in range(2):
                            last = three(pb[:, OUT_BANKS[2 * t + nh], :], apair(k, t * P, (t + 1) * P),
                                         wpair(g % RING, nh * BANK, (nh + 1) * BANK), j == 0, j == KD - 1)
                        if j == KD - 1 and t == 0:
                            last.then_inc(out_tile0, 1)
                    last.then_inc(halves_used, 1)

                pe.wait_ge(s5_y, 2 * L + 2)
                sb_logits(0)
                pe.wait_ge(aug_ready, L + 1)
                for hd in range(HEADS):
                    if hd >= 2:
                        pe.wait_ge(fT_copied, HEADS * L + hd - 1)
                    for j in range(2):
                        for t in range(TILES):
                            o = j * SEQ + t * P
                            last = T(pb[0:AUG, 3 + hd % 2, o:o + P], qk[:, t, j * HEADS + hd, :])
                    last.then_inc(foxT_ready, 1)
                pe.wait_ge(s5_gelu, L + 1)
                pe.wait_ge(wglu_in, 16 * (L + 1))
                for m2 in range(2):
                    for m in range(2):
                        last = M(pb[:, 2, m2 * SEQ:(m2 + 1) * SEQ], wglu[:, m, m2 * P:(m2 + 1) * P], s5g[:, m, :],
                                 start=(m == 0), stop=(m == 1))
                last.then_inc(glu_ready, 1)
                pe.wait_ge(sv_copied, L + 1)
                fox_logits(0)
                fox_logits(1)
                sb_sums(0)
                pe.wait_ge(fox_p, 3 * L + 1)
                fox_logits(2)
                pe.wait_ge(fox_p, 3 * L + 2)
                prob_transposes(0)
                prob_transposes(1)
                pe.wait_ge(s5_sq, L + 1)
                pe.wait_ge(glu_sig, 2 * L + 2)
                M(pb[:, 2, :], blk, s5q[:].rearrange("p m s -> p (m s)"), start=True, stop=True).then_inc(s5_ms, 1)
                pe.wait_ge(at_ready, 2 * L + 1)
                sb_logits(1)
                prob_transposes(2)
                prob_transposes(3)
                pe.wait_ge(s5_rstd, L + 1)
                sb_values(0)
                pe.wait_ge(fox_p, 3 * L + 3)
                prob_transposes(4)
                prob_transposes(5)
                for hd in range(HEADS):
                    pe.wait_ge((pT_even, pT_odd)[hd % 2], 3 * L + hd // 2 + 1)
                    c0 = hd * HEAD_DIM
                    M(pb[:, 0, c0:c0 + HEAD_DIM], pT[:, hd, 0:P], fv[:, 0, c0:c0 + HEAD_DIM], start=True, stop=True)
                    M(pb[:, 1, c0:c0 + HEAD_DIM], pT[:, hd, P:2 * P], fv[:, 0, c0:c0 + HEAD_DIM],
                      start=True, stop=False)
                    last = M(pb[:, 1, c0:c0 + HEAD_DIM], pT[:, hd, 2 * P:3 * P], fv[:, 1, c0:c0 + HEAD_DIM],
                             start=False, stop=True)
                last.then_inc(foxy_ready, 1)
                sb_sums(1)
                pe.wait_ge(foxy_done, L + 1)
                out_project(0)
                pe.wait_ge(sby_done, 2 * L + 1)
                pe.wait_ge(mix_ready, 2 * L + 1)
                mix_transposes(0)
                out_project(1)
                pe.wait_ge(mix_lo, 8 * L + 4)
                mix_transposes(1)
                pe.wait_ge(at_ready, 2 * L + 2)
                sb_values(1)
                for j in range(2, 5):
                    out_project(j)
                pe.wait_ge(mix_ready, 2 * L + 2)
                mix_transposes(2)
                mix_transposes(3)
                for j in range(5, 8):
                    out_project(j)

            pe.wait_ge(const_in, 16)
            transposes(0)
            attention(0)

            transposes(1)
            pe.wait_ge(hT_lo, 2 * KD)
            g = 2 * U_FFN0
            for c in range(F_CHUNKS + 1):
                if c < F_CHUNKS:
                    for part in range(2):
                        for j in range(4):
                            pe.wait_ge(lo_ready, g + 1)
                            if c and part == 0 and j == 0:
                                pe.wait_ge(d_hf, c)
                            for s in range(F_SUBS):
                                for kk in range(2):
                                    k = 2 * j + kk
                                    last = three(pb[:, s, part * SEQ:(part + 1) * SEQ],
                                                 wpair(g % RING, kk * F_CHUNK + s * P, kk * F_CHUNK + (s + 1) * P),
                                                 apair(k, 0, SEQ), k == 0, k == KD - 1)
                            last.then_inc(halves_used, 1)
                            g += 1
                if c:
                    b = (c - 1) % 2
                    pe.wait_ge(d_hlo, c)
                    for j in range(F_SUBS):
                        pe.wait_ge(lo_ready, g + 1)
                        for t in range(TILES):
                            for nh in range(2):
                                last = three(pb[:, 4 + 2 * t + nh, :],
                                             (d_hi[:, b, j, t * P:(t + 1) * P], d_lo[:, b, j, t * P:(t + 1) * P]),
                                             wpair(g % RING, nh * BANK, (nh + 1) * BANK),
                                             c == 1 and j == 0, c == F_CHUNKS and j == F_SUBS - 1)
                            if c == F_CHUNKS and j == F_SUBS - 1 and t == 0:
                                last.then_inc(out_tile0, 1)
                        last.then_inc(halves_used, 1)
                        g += 1

            transposes(2)
            attention(1)
            transposes(3)

            pe.wait_ge(wr_in, 16)
            pe.wait_ge(hT_hi, 8 * 4)
            for t in range(TILES):
                for k in range(KD):
                    last = M(pb[:, 7, t * EXPERTS:(t + 1) * EXPERTS], hT_f[:, k, t * P:(t + 1) * P], wr[:, k, :],
                             start=(k == 0), stop=(k == KD - 1))
            last.then_inc(r_logits, 1)
            sel = smalls_r[:, 6, :, 0:EXPERTS]
            pe.wait_ge(r_sel, 1)
            M(pb[:, 7, 0:EXPERTS], tri, sel[:, 0], start=True, stop=True)
            M(pb[:, 7, EXPERTS:2 * EXPERTS], tri, sel[:, 1], start=True, stop=False)
            M(pb[:, 7, EXPERTS:2 * EXPERTS], ones, sel[:, 0], start=False, stop=True)
            M(pb[:, 7, 2 * EXPERTS:3 * EXPERTS], ones, sel[:, 0], start=True, stop=False)
            M(pb[:, 7, 2 * EXPERTS:3 * EXPERTS], ones, sel[:, 1], start=False, stop=True).then_inc(r_cnt, 1)

            def gather_half(k4, staged, pm_event):
                pe.wait_ge(m_pmr, pm_event)
                if staged is not None:
                    pe.wait_ge(m_staged, staged)
                for k in range(4):
                    kk = 4 * k4 + k
                    for t in range(TILES):
                        last = M(pb[:, 7, k * P:(k + 1) * P], h[:, t, kk * P:(kk + 1) * P], m_pm[:, t, :],
                                 start=(t == 0), stop=(t == TILES - 1))
                last.then_inc(m_gather, 1)

            def scatter_piece(p):
                t, nh = p // 2, p % 2
                M(pb[:, 7, :], m_gt[:, t, :], m_y[:, nh * BANK:(nh + 1) * BANK],
                  start=True, stop=True).then_inc(m_scat, 1)

            def h_transposes(count):
                pe.wait_ge(m_hf, count)
                for s in range(F_SUBS):
                    last = T(pb[:, 6, s * P:(s + 1) * P], m_h[:, s * P:(s + 1) * P])
                last.then_inc(m_T, 1)

            def down(b, j, slot, start, stop):
                for nh in range(2):
                    last = three(pb[:, 4 + nh, :], (m_hi[:, b, j * P:(j + 1) * P], m_lo[:, b, j * P:(j + 1) * P]),
                                 wpair(slot, nh * BANK, (nh + 1) * BANK), start, stop)
                return last

            gather_half(0, None, 1)
            gather_half(1, 1, 1)

            def item(i, first):
                j_ = [0]
                g0 = 2 * U_MOE if first else i * H_BODY + 2 * U_BASE1
                s0 = 2 * U_MOE if first else 2 * (U_BASE1 + U_BODY)

                def half():
                    pe.wait_ge(lo_ready, g0 + (j_[0] + 1))
                    slot = (s0 + j_[0]) % RING
                    j_[0] += 1
                    return slot

                def gate_or_up(bank):
                    for j in range(4):
                        slot = half()
                        for kk in range(2):
                            k = 2 * j + kk
                            last = three(pb[:, bank, :], (xg_hi[:, k, :], xg_lo[:, k, :]),
                                         wpair(slot, kk * F_CHUNK, (kk + 1) * F_CHUNK), k == 0, k == KD - 1)
                        last.then_inc(halves_used, 1)

                for c, before in steps():
                    q = i * F_CHUNKS + c
                    if c == 0:
                        pe.wait_ge(m_xglo, i + 1)
                        if not first:
                            pe.wait_ge(m_hf, q)
                    elif c >= 2:
                        pe.wait_ge(m_hf, q - 1)
                    gate_or_up(2 * (c % 2))
                    if c or not first:
                        if c >= 2 or not first:
                            pe.wait_ge(m_hlo, q - 1)
                        h_transposes(q)
                    if c == 5:
                        pe.wait_ge(m_pmr, i + 2)
                        if not first:
                            pe.wait_ge(m_added, i * 4)
                        else:
                            pe.wait_ge(m_staged, 2)
                        for t in range(TILES):
                            last = T(pb[:, 7, t * P:(t + 1) * P], m_gp[:, t, :])
                        last.then_inc(m_gtT, 1)
                    if c == 6:
                        gather_half(1, i * 2 + 3, i + 2)
                    gate_or_up(2 * (c % 2) + 1)
                    if c or not first:
                        pe.wait_ge(m_hlo, q)
                        b, cc = (before % 2, before) if c else (0, F_CHUNKS - 1)
                        if cc == 0 and not first:
                            pe.wait_ge(m_ysb, i)
                        for j in range(F_SUBS):
                            slot = half()
                            last = down(b, j, slot, cc == 0 and j == 0, cc == F_CHUNKS - 1 and j == F_SUBS - 1)
                            last.then_inc(halves_used, 1)
                    if not first and 1 <= c <= 4:
                        if c == 1:
                            pe.wait_ge(m_ysb, i)
                            pe.wait_ge(m_gtc, i)
                            pe.wait_ge(m_staged, i * 2 + 2)
                        else:
                            pe.wait_ge(m_added, i * 4 + (c - 5))
                        scatter_piece(c - 1)
                    if c == 5:
                        pe.wait_ge(m_gtc, i + 1)
                        gather_half(0, None, i + 2)

            item(0, True)
            pe.wait_ge(r_table, 1)
            last = pe.value_load(etab[0:1, ITEMS_MAX:ITEMS_MAX + 1], min_val=EXPERTS - 1, max_val=ITEMS_MAX - 2)
            with pe.Fori(1, last + 1) as i:
                item(i, False)
            pe.wait_ge(m_hlo, last * F_CHUNKS + (F_CHUNKS - 1))
            h_transposes(last * F_CHUNKS + F_CHUNKS)
            pe.wait_ge(m_hlo, last * F_CHUNKS + F_CHUNKS)
            st = 2 * U_BASE1
            for j in range(4):
                pe.wait_ge(lo_ready, last * H_BODY + (H_BODY + st + j + 1))
                done = down(0, j, (st + j) % RING, False, j == 3)
                done.then_inc(halves_used, 1)
            pe.wait_ge(m_ysb, last + 1)
            pe.wait_ge(m_gtc, last + 1)
            pe.wait_ge(m_staged, last * 2 + 4)
            for p in range(4):
                if p:
                    pe.wait_ge(m_added, last * 4 + p)
                scatter_piece(p)


def constants():
    c = np.zeros((P, C_WIDTH), np.float32)
    i = np.arange(P)
    row, column = i[:, None], i[None, :]
    c[:, C_IDENT:C_IDENT + P] = row == column
    c[:, C_TRI:C_TRI + P] = row <= column
    c[:, C_NREV:C_NREV + P] = np.where(row >= column, -1.0, 0.0)
    c[:, C_ONES:C_ONES + P] = 1.0
    c[:, C_NONES:C_NONES + P] = -1.0
    c[:, C_FMASK:C_FMASK + P] = np.where(column <= row, 0.0, BIG_NEG)
    c[:, C_SMASK:C_SMASK + P] = np.where(row < column, 0.0, BIG_NEG)
    c[:, C_BLK:C_BLK + P] = np.where(row // 16 == column // 16, 1.0 / 16, 0.0)
    c[:, C_IOTA:C_IOTA + P] = column
    c[:, C_TROW:C_TROW + SEQ] = np.arange(SEQ)
    c[:, C_EPS] = EPS
    c[:, C_EIDX:C_EIDX + EXPERTS] = np.arange(EXPERTS)
    c[:, C_REV:C_REV + EXPERTS] = EXPERTS - np.arange(EXPERTS)
    return c


def by_partition(a):
    return a.reshape(DEPTH, -1, P).transpose(2, 0, 1)


def kernel(**inputs):
    import concourse.bacc as bacc
    from concourse.bass_utils import run_bass_kernel_spmd

    g = {k: np.asarray(v) for k, v in inputs.items()}
    f = np.float32
    small = np.zeros((P, DEPTH, S_WIDTH), f)
    small[:, :, S_GA:S_GA + KD] = by_partition(g["attn_norm"])
    small[:, :, S_GF:S_GF + KD] = by_partition(g["ffn_norm"])
    small[:, :, S_GO:S_GO + KD] = by_partition(g["out_norm"])
    small[:, :, S_ARE:S_ARE + KD] = by_partition(g["ssm_a_re"])
    small[:, :, S_AIM:S_AIM + KD] = by_partition(g["ssm_a_im"])
    small[:, :, S_LDT:S_LDT + KD] = by_partition(np.repeat(g["ssm_log_dt"], 64, axis=1))
    small[:, :, S_DSK:S_DSK + 2] = by_partition(g["ssm_d"])
    small[:, :, S_BGL:S_BGL + 2] = by_partition(g["ssm_b_glu"])
    small[:, :, S_BF:S_BF + HEADS] = g["b_forget"][None]
    small[:HEAD_DIM, :, S_GQ] = g["fox_q_norm"].T
    small[:HEAD_DIM, :, S_GK] = g["fox_k_norm"].T
    small[HEAD_DIM:AUG, :, S_GQ:S_GK + 1] = 1.0
    b_mat = np.zeros((DEPTH, 4, 2, 16, 2, 2, 2, 64), f)
    c_mat = np.zeros((DEPTH, 2, 64, 2, KD, 2, 16), f)
    for r, (bn, cn) in enumerate((("ssm_b_re", "ssm_c_re"), ("ssm_b_im", "ssm_c_im"))):
        b = g[bn].reshape(DEPTH, 2, 4, 2, 64, 16)
        c = g[cn].reshape(DEPTH, KD, 2, 16, 64)
        for q in range(2):
            b_mat[:, :, q, :, r, :, q, :] = b[:, :, :, q].transpose(0, 2, 4, 1, 3)
            c_mat[:, q, :, r, :, q, :] = c[:, :, q].transpose(0, 3, 1, 2)
    arrays = {
        "x_d": g["x"].reshape(SEQ, D_MODEL),
        "consts_d": constants(),
        "small_d": small,
        "b_d": b_mat.reshape(DEPTH, P, 2, 2, P),
        "c_d": c_mat.reshape(DEPTH, P, 2, KD, 32),
        "wglu_d": g["ssm_w_glu"].reshape(DEPTH, 2, P, SSM_WIDTH).transpose(0, 2, 1, 3),
        "w_in_d": g["w_in"],
        "w_out_d": g["w_out"],
        "dg_d": g["dense_w_gate"][0],
        "du_d": g["dense_w_up"][0],
        "dd_d": g["dense_w_down"][0],
        "wr_d": g["moe_w_router"][0].reshape(KD, P, EXPERTS).transpose(1, 0, 2),
        "mg_d": g["moe_w_gate"],
        "mu_d": g["moe_w_up"],
        "md_d": g["moe_w_down"],
    }
    nc = bacc.Bacc("TRN2", target_bir_lowering=False, num_devices=1)
    args = {}
    for name, a in arrays.items():
        a = arrays[name] = np.ascontiguousarray(a)
        args[name] = nc.dram_tensor(name, a.shape, mybir.dt.from_np(a.dtype), kind="ExternalInput").ap()
    args["out_d"] = nc.dram_tensor("out_d", (SEQ, D_MODEL), F32, kind="ExternalOutput").ap()
    trunk(nc, **args)
    r = run_bass_kernel_spmd(nc, [arrays], core_ids=[0])
    return r.results[0]["out_d"].reshape(1, SEQ, D_MODEL)
```

```python
import math
from contextlib import ExitStack

import numpy as np
import concourse.bass as bass
from concourse import mybir

F32 = mybir.dt.float32
F32R = mybir.dt.float32r
I32 = mybir.dt.int32
ALU = mybir.AluOpType
ACT = mybir.ActivationFunctionType
AX = mybir.AxisListType

P = 128
SEQ = 256
D_MODEL = 1024
DEPTH = 2
D_FF = 3584
HEADS = 6
HEAD_DIM = 64
HEADS_WIDTH = HEADS * HEAD_DIM
SSM_WIDTH = 256
EXPERTS = 8
EPS = 1e-6
TILES = SEQ // P
KD = D_MODEL // P
BANK = 512
F_CHUNK = 512
F_CHUNKS = D_FF // F_CHUNK
F_SUBS = F_CHUNK // P
BIG_NEG = -1e30

_E = 3 * HEADS_WIDTH + HEADS
PROJ_WIDTH = _E + 3 * HEADS_WIDTH + SSM_WIDTH
CH_SU = (PROJ_WIDTH - SSM_WIDTH, SSM_WIDTH)
CH_FQ = (0, HEADS_WIDTH)
CH_FK = (HEADS_WIDTH, HEADS_WIDTH)
CH_FVG = (2 * HEADS_WIDTH, HEADS_WIDTH + HEADS)
CH_SQ = (_E, HEADS_WIDTH)
CH_SK = (_E + HEADS_WIDTH, HEADS_WIDTH)
CH_SV = (_E + 2 * HEADS_WIDTH, HEADS_WIDTH)
CHUNKS = [CH_SU, CH_FQ, CH_FK, CH_FVG, CH_SQ, CH_SK, CH_SV]
SU, FQ, FK, FVG, SQ, SK, SV = range(7)
OUT_K_ORDER = [6, 7, 0, 1, 2, 3, 4, 5]

RAW = 6
MOE_RAW = 14
RING = 4
UNIT = 2048
HALF = UNIT // 2
U_IN, U_OUT = 2 * len(CHUNKS), KD // 2
U_CHUNK = 6
U_FFN = U_CHUNK * F_CHUNKS
U_L0 = 0
U_FFN0 = U_L0 + U_IN + U_OUT
U_L1 = U_FFN0 + U_FFN
U_MOE = U_L1 + U_IN + U_OUT
U_BODY = U_FFN
H_BODY = 2 * U_BODY
U_BASE1 = U_MOE - 2

C_IDENT, C_TRI, C_NREV, C_ONES, C_NONES, C_FMASK, C_SMASK, C_BLK, C_IOTA = [P * i for i in range(9)]
C_TROW = 9 * P
C_EIDX = C_TROW + SEQ
C_REV = C_EIDX + EXPERTS
C_WIDTH = C_REV + EXPERTS + 1

S_GA, S_GF, S_GO = 0, KD, 2 * KD
S_ARE, S_AIM, S_LDT = 3 * KD, 4 * KD, 5 * KD
S_DSK, S_BGL = 6 * KD, 6 * KD + 2
S_BF = 6 * KD + 4
S_GQ, S_GK = S_BF + HEADS, S_BF + HEADS + 1
S_EPS = S_GK + 1
S_WIDTH = S_GK + 2
AUG = HEAD_DIM + 2
ITEMS_MAX = 12
CAP = P

TWO_PI = 2.0 * math.pi
TWO_PI_A = 6.28125
TWO_PI_B = round((TWO_PI - TWO_PI_A) * 2 ** 20) / 2 ** 20
TWO_PI_C = TWO_PI - TWO_PI_A - TWO_PI_B
ROUND_ONE = 12582912.0
EARLY = 3
TABLE_STEPS = 13
COEF_STEPS = 6
COEF_START = 4 * FK
S5_CHUNK0, S5_CHUNK1 = FVG, FK
XT_BANKS = ((0, 1, 2, 3), (2, 5, 6, 7))
FOX_BANKS = (0, 3, 0)
SBW = HEADS_WIDTH // 2
SBY_BANKS = (2, 5)
OUT_BANKS = (0, 1, 3, 4)
LAST_PIECES = ((0, 0), (1, 0), (0, 1), (1, 1))
LAST_BANKS = (7, 2, 3, 0)
MIX_PARTS = ((2, (0, 1)), (2, (2,)), (6, (3, 4)), (7, (5,)))
ROUND_12 = 1.5 * 2.0 ** 11


def trunk(nc, x_d, consts_d, small_d, b_d, c_d, wglu_d, w_in_d, w_out_d,
          dg_d, du_d, dd_d, wr_d, mg_d, mu_d, md_d, out_d):
    ctx = ExitStack()
    with ctx:
        base = [-(-nc.sbuf_base // 64) * 64]
        limit = nc.sbuf_usable_end

        def size(shape):
            n = 4
            for s in shape[1:]:
                n *= s
            return -(-n // 32) * 32

        def keep(name, shape, dt=F32):
            t = nc.alloc_sbuf_tensor_at(name, shape, dt, offset=base[0])
            base[0] += size(shape)
            assert base[0] <= limit, (name, base[0], limit)
            return t

        def over(at, name, shape, dt=F32):
            t = nc.alloc_sbuf_tensor_at(name, shape, dt, offset=at)
            assert at + size(shape) <= limit, (name, at + size(shape), limit)
            return t, at + size(shape)

        def sem(name):
            return ctx.enter_context(nc.semaphore(name))

        raw = keep("raw", [P, RAW, UNIT])
        whi = keep("whi", [P, RING, HALF], F32R)
        wlo = keep("wlo", [P, RING, HALF], F32R)
        x = keep("x", [P, TILES, D_MODEL])
        at_consts = base[0]
        consts = keep("consts", [P, C_WIDTH])
        small = keep("small", [P, DEPTH, S_WIDTH])
        stat = keep("stat", [P, 64])
        stat2 = keep("stat2", [P, 64])
        gatez = keep("gatez", [P, TILES, HEADS])
        gatel = keep("gatel", [P, TILES, HEADS])
        logf = keep("logf", [P, TILES, HEADS])
        fox_nmax = keep("fox_nmax", [P, 3, TILES, 2])
        fox_rs = keep("fox_rs", [P, TILES, HEADS])
        s5s = keep("s5s", [P, 16, KD])
        etab = keep("etab", [1, 16], I32)
        wr = keep("wr", [P, KD, EXPERTS])
        ident_r = keep("ident_r", [P, P], F32R)
        masks, _ = over(at_consts + 4 * C_FMASK, "masks", [P, 2, P], F32R)
        at_act = base[0]
        act_hi = keep("act_hi", [P, KD, SEQ], F32R)
        act_lo = keep("act_lo", [P, KD, SEQ], F32R)
        hT_f, _ = over(at_act, "hT_f", [P, KD, SEQ])
        xg_hi, e = over(at_act, "xg_hi", [P, KD, P], F32R)
        xg_lo, e = over(e, "xg_lo", [P, KD, P], F32R)
        stage, e = over(e, "stage", [P, KD, P])
        smalls_r, e = over(e, "smalls_r", [P, 12, TILES, 12])
        second_oh, e = over(e, "second_oh", [P, ITEMS_MAX - EXPERTS, EXPERTS])
        second_w, e = over(e, "second_w", [P, TILES, ITEMS_MAX - EXPERTS, EXPERTS])
        logitsT, e = over(e, "logitsT", [EXPERTS, SEQ])
        m_slot, e = over(e, "m_slot", [P, TILES, P])
        assert e <= at_act + 2 * KD * SEQ * 4
        at_h = base[0]
        h = keep("h", [P, TILES, D_MODEL])
        s5y, e = over(at_h, "s5y", [P, 2, SEQ])
        s5g, e = over(e, "s5g", [P, 2, SEQ])
        s5sg, e = over(e, "s5sg", [P, 2, SEQ])
        s5q, e = over(e, "s5q", [P, 2, SEQ])
        su, e = over(at_h, "su", [P, TILES, SSM_WIDTH])
        fsq, e = over(e, "fsq", [P, TILES, HEADS_WIDTH])
        at_tab = base[0]
        tabc = keep("tabc", [P, KD, SEQ])
        tabs = keep("tabs", [P, KD, SEQ])
        bmat = keep("bmat", [P, 2, 2, P])
        cmat = keep("cmat", [P, 2, KD, 32])
        cbar = keep("cbar", [P, 3, KD, 32])
        wglu = keep("wglu", [P, 2, SSM_WIDTH])

        at_over = base[0]
        e = at_over
        s5w, e = over(e, "s5w", [P, 6, 2, SEQ])
        uT, e = over(e, "uT", [P, 2, SEQ])
        fv, e = over(e, "fv", [P, TILES, HEADS_WIDTH])
        sv, e = over(e, "sv", [P, TILES, HEADS_WIDTH])
        ymix, _ = over(e, "ymix", [P, TILES, 2 * HEADS_WIDTH])
        sqT, e = over(e, "sqT", [P, 3, SEQ])
        skT, e = over(e, "skT", [P, 3, SEQ])
        at_qk = e
        qk, e = over(e, "qk", [P, TILES, 2 * HEADS, AUG])
        fT, e = over(e, "fT", [AUG, 2 * HEADS, SEQ])
        sb_u, s = over(at_over, "sb_u", [P, 3, 3 * P])
        sb_sp, s = over(s, "sb_sp", [P, 3, 3 * P])
        sb_a, s = over(s, "sb_a", [P, 3, 3 * P])
        assert s <= at_over + 7 * 2 * SEQ * 4
        s5m, _ = over(at_qk, "s5m", [P, 2, SEQ])
        at_att = e
        pf, e = over(e, "pf", [P, HEADS, 3 * P])
        pT, e = over(e, "pT", [P, HEADS, 3 * P])
        s5w2, _ = over(at_att, "s5w2", [P, 2, 2, SEQ])
        sqtmp, _ = over(at_att, "sqtmp", [P, TILES, 2 * HEADS_WIDTH])
        ang, _ = over(at_att, "ang", [P, KD, SEQ])
        rnd, _ = over(at_att + KD * SEQ * 4, "rnd", [P, KD, SEQ])
        e = at_over
        d_sg, e = over(e, "d_sg", [P, F_SUBS, SEQ])
        d_h, e = over(e, "d_h", [P, F_SUBS, SEQ])
        d_hi, e = over(e, "d_hi", [P, 2, F_SUBS, SEQ], F32R)
        d_lo, e = over(e, "d_lo", [P, 2, F_SUBS, SEQ], F32R)
        assert e <= at_att
        e = at_tab
        raw2, e = over(e, "raw2", [P, MOE_RAW - RAW, UNIT])
        m_sg, e = over(e, "m_sg", [P, F_CHUNK])
        m_h, e = over(e, "m_h", [P, F_CHUNK])
        m_hi, e = over(e, "m_hi", [P, 2, F_CHUNK], F32R)
        m_lo, e = over(e, "m_lo", [P, 2, F_CHUNK], F32R)
        m_yhi, e = over(e, "m_yhi", [P, D_MODEL], F32R)
        m_ylo, e = over(e, "m_ylo", [P, D_MODEL], F32R)
        m_token, e = over(e, "m_token", [P, TILES, P], F32R)
        m_gate, e = over(e, "m_gate", [P, 8])
        m_sgate, e = over(e, "m_sgate", [P, 8])
        m_pm, e = over(e, "m_pm", [P, TILES, P])
        pos_i, e = over(e, "pos_i", [P, TILES, ITEMS_MAX])
        gate_i, e = over(e, "gate_i", [P, TILES, ITEMS_MAX])

        pb = ctx.enter_context(nc.psum_tensor("pb", [P, 8, BANK], F32))

        x_in = [sem(f"x_in{t}") for t in range(TILES)]
        const_in, small_in, bmat_in, cmat_in, wglu_in, wr_in, out_done = map(sem, (
            "const_in", "small_in", "bmat_in", "cmat_in", "wglu_in", "wr_in", "out_done"))
        raw_in = [sem(f"raw_in{i}") for i in range(RAW)]
        moe_in = [sem(f"moe_in{i}") for i in range(MOE_RAW)]

        def moe_raw(slot):
            if 2 <= slot < 2 + RAW:
                return raw[:, (U_MOE + slot - 2) % RAW]
            return raw2[:, (slot - 2 - RAW) % MOE_RAW]

        def moe_uses(v):
            return v // MOE_RAW + (0 if v % MOE_RAW < 2 else 1)

        hi_ready, lo_ready, halves_used = sem("hi_ready"), sem("lo_ready"), sem("halves_used")
        dve_seq, act_seq = sem("dve_seq"), sem("act_seq")
        (masks_ready, out_tile0, x_sq, x_sum, x_rstd, normed, xT_ready, hT_hi, hT_lo, su_copied, qk_rstd,
         qk_normed, fv_copied, gate_read, gate_l, logf_ready, sq_copied, sk_copied, sv_copied,
         uT_ready, uT_copied, bu_first, bu_ready, bu_read, s5_prod, s5_used, s5_y, s5_gelu, glu_ready,
         glu_sig, s5_r, s5_sq, s5_ms, s5_rstd, s5_norm, mix_hi, mix_lo, c_ready, aug_ready,
         foxT_ready, fT_copied, logits_ready, fox_max, fox_p, pT_ready, pT_even, pT_odd,
         foxy_ready, foxy_done, z_ready, sb_l, sp_ready, a_ready, at_ready, sby_ready, sby_done,
         mix_sq, mix_sum, mix_rstd, mix_ready, mixT_ready, x_done, tab_ang,
         tab_ready, s5_exp, s5_trig, cbar_ready) = map(sem, (
            "masks_ready out_tile0 x_sq x_sum x_rstd normed xT_ready hT_hi hT_lo su_copied qk_rstd "
            "qk_normed fv_copied gate_read gate_l logf_ready sq_copied sk_copied sv_copied "
            "uT_ready uT_copied bu_first bu_ready bu_read s5_prod s5_used s5_y s5_gelu glu_ready "
            "glu_sig s5_r s5_sq s5_ms s5_rstd s5_norm mix_hi mix_lo c_ready aug_ready "
            "foxT_ready fT_copied logits_ready fox_max fox_p pT_ready pT_even pT_odd "
            "foxy_ready foxy_done z_ready sb_l sp_ready a_ready at_ready sby_ready sby_done "
            "mix_sq mix_sum mix_rstd mix_ready mixT_ready x_done tab_ang "
            "tab_ready s5_exp s5_trig cbar_ready").split())
        d_silu, d_hf, d_hhi, d_hlo = map(sem, (
            "d_silu", "d_hf", "d_hhi", "d_hlo"))
        (r_logitsT, r_copied, r_logits, r_d, r_e, r_sel, r_cnt, r_table, m_silu, m_hf, m_T, m_hhi, m_hlo,
         m_ygated, m_ysb, m_pmr, m_gather, m_staged, m_xghi, m_xglo, m_gtT, m_gtc, m_scat,
         m_added) = map(sem, (
            "r_logitsT r_copied r_logits r_d r_e r_sel r_cnt r_table m_silu m_hf m_T m_hhi m_hlo "
            "m_ygated m_ysb m_pmr m_gather m_staged m_xghi m_xglo m_gtT m_gtc m_scat "
            "m_added").split())

        ident = consts[:, C_IDENT:C_IDENT + P]
        tri = consts[:, C_TRI:C_TRI + P]
        nrev = consts[:, C_NREV:C_NREV + P]
        ones = consts[:, C_ONES:C_ONES + P]
        nones = consts[:, C_NONES:C_NONES + P]
        fmask = consts[:, C_FMASK:C_FMASK + P]
        smask = consts[:, C_SMASK:C_SMASK + P]
        blk = consts[:, C_BLK:C_BLK + P]
        iota = consts[:, C_IOTA:C_IOTA + P]
        trow = consts[:, C_TROW:C_TROW + SEQ]
        eps = small[:, 0, S_EPS:S_EPS + 1]
        eps_q = small[:, 1, S_EPS:S_EPS + 1]
        eidx = consts[:, C_EIDX:C_EIDX + EXPERTS]
        rev = consts[:, C_REV:C_REV + EXPERTS]

        def g_part(slot):
            return slot % 2

        def col(layer, c, n=1):
            return small[:, layer, c:c + n]

        def u_attn(layer):
            return U_L1 if layer else U_L0

        def steps(first=False, last=False):
            for c in range(F_CHUNKS):
                yield c, (c - 1 if c else None)

        block = ctx.enter_context(nc.Block())

        def proj_done(layer, chunk):
            return 2 * u_attn(layer) + 4 * (chunk + 1)

        def out_done_at(n):
            return 2 * (U_FFN0, U_L1, U_MOE)[n]

        def ffn_done(g0, c, part, peeled):
            return g0 + (12 * c - (4 if peeled and c else 0) + 4 * (part + 1))

        @block.sync
        def _(sp):
            def small_loads(layer):
                if layer:
                    sp.wait_ge(x_done, 4)
                sp.dma_start(bmat[:], b_d[layer]).then_inc(bmat_in, 16)
                sp.dma_start(cmat[:], c_d[layer]).then_inc(cmat_in, 16)
                sp.dma_start(wglu[:], wglu_d[layer]).then_inc(wglu_in, 16)

            def load(u, src, n):
                if u >= RAW:
                    sp.wait_ge(lo_ready, 2 * (u - RAW) + 2)
                k = src.shape[1]
                dst = raw[:, u % RAW, 0:k * n].rearrange("p (k n) -> p k n", k=k)
                sp.dma_start(dst, src).then_inc(raw_in[u % RAW], 16)

            def moe_load(v, src, item=None):
                if item is not None:
                    sp.wait_ge(lo_ready, item * H_BODY + (2 * (U_BASE1 + v - MOE_RAW) + 2))
                elif v >= 2 + MOE_RAW:
                    sp.wait_ge(lo_ready, 2 * (U_BASE1 + v - MOE_RAW) + 2)
                elif v < 2 + RAW:
                    sp.wait_ge(lo_ready, 2 * (U_BASE1 + v - RAW) + 2)
                slot = v % MOE_RAW
                dst = moe_raw(slot).rearrange("p (k n) -> p k n", k=src.shape[1])
                sp.dma_start(dst, src).then_inc(moe_in[slot], 16)

            def attn_loads(layer):
                w = w_in_d[layer].rearrange("(k p) n -> p k n", p=P)
                u = u_attn(layer)
                for c0, n in CHUNKS:
                    for kh in range(2):
                        load(u, w[:, 4 * kh:4 * kh + 4, c0:c0 + n], n)
                        u += 1
                    if layer == 0 and (c0, n) == CH_SU:
                        small_loads(0)
                        sp.dma_start(wr[:], wr_d).then_inc(wr_in, 16)

            def out_loads(layer):
                w = w_out_d[layer].rearrange("(k p) n -> p k n", p=P)
                for j in range(U_OUT):
                    k = OUT_K_ORDER[2 * j]
                    load(u_attn(layer) + U_IN + j, w[:, k:k + 2, :], D_MODEL)

            def up_src(w, c, kh):
                return w.rearrange("(k p) f -> p k f", p=P)[:, 4 * kh:4 * kh + 4,
                                                            c * F_CHUNK:(c + 1) * F_CHUNK]

            def down_src(w, c, j):
                return w.rearrange("(r p) n -> p r n", p=P)[:, F_SUBS * c + 2 * j:F_SUBS * c + 2 * j + 2, :]

            for t in range(TILES):
                sp.dma_start(x[:, t, :], x_d[t * P:(t + 1) * P, :]).then_inc(x_in[t], 16)
                if t == 0:
                    sp.dma_start(small[:], small_d).then_inc(small_in, 16)
            sp.dma_start(consts[:], consts_d).then_inc(const_in, 16)
            for layer in range(DEPTH):
                attn_loads(layer)
                out_loads(layer)
                if layer == 0:
                    u = U_FFN0
                    for c in range(F_CHUNKS + 1):
                        if c < F_CHUNKS:
                            for w in (dg_d, du_d):
                                for kh in range(2):
                                    load(u, up_src(w, c, kh), F_CHUNK)
                                    u += 1
                        if c:
                            for j in range(2):
                                load(u, down_src(dd_d, c - 1, j), D_MODEL)
                                u += 1
                        if c == 2:
                            small_loads(1)

            def body(gate, up, down, prev_down):
                for c, before in steps():
                    for w in (gate, up):
                        for kh in range(2):
                            yield up_src(w, c, kh)
                    w, b = (down, before) if c else (prev_down, F_CHUNKS - 1)
                    if w is not None:
                        for i in range(2):
                            yield down_src(w, b, i)

            first_item = list(body(mg_d[0, 0], mu_d[0, 0], md_d[0, 0], None))
            for v in (2, 3):
                moe_load(v, first_item[v - 2])
            sp.wait_ge(glu_sig, 4)
            for v in (8, 9, 10):
                moe_load(v, first_item[v - 2])
            sp.wait_ge(fox_p, 6)
            moe_load(15, first_item[15 - 2])
            for v in (4, 5, 6, 7):
                moe_load(v, first_item[v - 2])
            sp.wait_ge(out_tile0, 6)
            for v in (11, 12, 13, 14, *range(16, U_BODY)):
                moe_load(v, first_item[v - 2])
            sp.wait_ge(r_table, 1)
            last = sp.value_load(etab[0:1, ITEMS_MAX:ITEMS_MAX + 1], min_val=EXPERTS - 1, max_val=ITEMS_MAX - 2)

            def expert(i):
                return sp.value_load(etab[0:1, bass.ds(i, 1)], min_val=0, max_val=EXPERTS - 1)

            def of(w, ex):
                return w[0, bass.ds(ex, 1)].rearrange("e a b -> (e a) b")

            with sp.Fori(1, last + 1) as i:
                ex, before = expert(i), expert(i - 1)
                for v, src in enumerate(body(of(mg_d, ex), of(mu_d, ex), of(md_d, ex), of(md_d, before))):
                    moe_load(v, src, i)
            ex = expert(last)
            for j in range(2):
                moe_load(U_BODY + j, down_src(of(md_d, ex), F_CHUNKS - 1, j), last)
            for n, (t, nh) in enumerate(LAST_PIECES):
                sp.wait_ge(m_added, last * 4 + (n + 1))
                cols = slice(nh * BANK, (nh + 1) * BANK)
                sp.dma_start(out_d[t * P:(t + 1) * P, cols], x[:, t, cols]).then_inc(out_done, 16)
            sp.wait_ge(out_done, 16 * len(LAST_PIECES))

        @block.scalar
        def _(act):
            A = nc.scalar.activation
            n_link = [0]

            def link(ins):
                n_link[0] += 1
                ins.then_inc(act_seq, 1)
                act.wait_ge(act_seq, n_link[0])

            def exp_ln_table():
                nc.scalar.preload_act_table_set("natural_log_exp_and_others")

            def split_hi(g, n, slot, src):
                if not isinstance(g, int) or g >= RING:
                    act.wait_ge(halves_used, g - RING + 1)
                A(whi[:, slot, 0:n], src[:, g_part(slot) * n:(g_part(slot) + 1) * n], ACT.Copy).then_inc(hi_ready, 1)

            def hi(g, n):
                u = g // 2
                if g % 2 == 0:
                    act.wait_ge(raw_in[u % RAW], 16 * (u // RAW + 1))
                split_hi(g, n, g % RING, raw[:, u % RAW])

            def moe_hi(hv, item=None):
                v = hv // 2
                if hv % 2 == 0:
                    uses = 16 * moe_uses(v)
                    act.wait_ge(moe_in[v % MOE_RAW],
                                uses if item is None else item * (16 * U_BODY // MOE_RAW) + uses)
                g = 2 * U_BASE1 + hv
                split_hi(g if item is None else item * H_BODY + g, HALF, g % RING, moe_raw(v % MOE_RAW))

            def norm_stats(event):
                def squares(t):
                    for nh in range(2):
                        if event:
                            act.wait_ge(x_done, 4 * (event - 1) + 2 * t + nh + 1)
                        last = A(h[:, t, nh * BANK:(nh + 1) * BANK], x[:, t, nh * BANK:(nh + 1) * BANK],
                                 ACT.Square, accum_out=stat[:, 2 * t + nh:2 * t + nh + 1])
                    last.then_inc(x_sq, 1)

                def rstd(t):
                    act.wait_ge(x_sum, 2 * event + t + 1)
                    link(A(stat[:, 6 + t:7 + t], stat[:, 4 + t:5 + t], ACT.Ln, scale=1.0 / D_MODEL, bias=eps))
                    A(stat[:, 8 + t:9 + t], stat[:, 6 + t:7 + t], ACT.Exp, scale=-0.5).then_inc(x_rstd, 1)

                if event == 0:
                    act.wait_ge(x_in[0], 16)
                squares(0)
                if event == 0:
                    act.wait_ge(small_in, 16)
                rstd(0)
                if event == 0:
                    act.wait_ge(x_in[1], 16)
                squares(1)
                rstd(1)

            def hT_his(event, layer, gain):
                banks = XT_BANKS[event % 2]
                for k in range(KD):
                    if k % 2 == 0:
                        act.wait_ge(xT_ready, 4 * event + k // 2 + 1)
                    dst = hT_f if event == 3 else act_hi
                    b, o = banks[k // 2], (k % 2) * SEQ
                    A(dst[:, k, :], pb[:, b, o:o + SEQ], ACT.Copy, scale=col(layer, gain + k)).then_inc(hT_hi, 1)

            def trig(layer, q):
                if q == 0:
                    act.wait_ge(tab_ang, 5 * layer + 1)
                    A(s5s[:, 8, :], s5s[:, 6, :], ACT.Sin, scale=TWO_PI * (1 - 2e-7)).then_inc(s5_trig, 1)
                    A(s5s[:, 9, :], s5s[:, 6, :], ACT.Sin, scale=math.pi).then_inc(s5_trig, 1)
                ks = slice(2 * q, 2 * q + 2)
                act.wait_ge(tab_ang, 5 * layer + q + 2)
                link(A(tabc[:, ks], ang[:, ks], ACT.Sin, scale=math.pi))
                A(tabs[:, ks], rnd[:, ks], ACT.Sin, scale=TWO_PI * (1 - 2e-7))
                link(A(tabc[:, ks], tabc[:, ks], ACT.Square))
                A(tabc[:, ks], tabc[:, ks], ACT.Copy, scale=-2.0, bias=1.0).then_inc(tab_ready, 1)

            def s5_exps(layer):
                if layer:
                    act.wait_ge(s5_y, 2 * layer)
                link(A(s5s[:, 0, :], col(layer, S_LDT, KD), ACT.Exp))
                for k in range(KD):
                    last = A(s5s[:, 1, k:k + 1], s5s[:, 0, k:k + 1], ACT.Exp, scale=col(layer, S_ARE + k))
                last.then_inc(s5_exp, 1)

            def attention(layer):
                L = layer
                g0 = 2 * u_attn(L)
                W = [n for _, n in CHUNKS]

                def his(chunk, *halves):
                    for j in halves or range(4):
                        hi(g0 + 4 * chunk + j, 2 * W[chunk])

                def square(j, b):
                    act.wait_ge(halves_used, proj_done(L, j))
                    if j == FK:
                        act.wait_ge(qk_rstd, 2 * L + 1)
                    for t in range(TILES):
                        for hd in range(HEADS):
                            o = 12 * (j - 1) + 6 * t + hd
                            last = A(fsq[:, t, hd * HEAD_DIM:(hd + 1) * HEAD_DIM],
                                     pb[:, b + t, hd * HEAD_DIM:(hd + 1) * HEAD_DIM], ACT.Square,
                                     accum_out=stat2[:, o:o + 1])
                    link(last)

                def rstd(j):
                    o = 12 * (j - 1)
                    link(A(stat2[:, 24 + o:36 + o], stat2[:, o:o + 12], ACT.Ln,
                           scale=1.0 if j == FQ else 1.0 / HEAD_DIM, bias=eps_q if j == FQ else eps))
                    A(stat2[:, o:o + 12], stat2[:, 24 + o:36 + o], ACT.Exp, scale=-0.5).then_inc(qk_rstd, 1)
                    act.wait_ge(qk_rstd, 2 * L + j)

                def normed_heads(j, b, t):
                    for hd in range(HEADS):
                        o = 12 * (j - 1) + 6 * t + hd
                        last = A(qk[:, t, HEADS * (j - 1) + hd, 0:HEAD_DIM],
                                 pb[:, b + t, hd * HEAD_DIM:(hd + 1) * HEAD_DIM], ACT.Copy, scale=stat2[:, o:o + 1])
                    if t == TILES - 1:
                        last.then_inc(qk_normed, 1)

                if L:
                    his(SU, EARLY)
                his(FQ, 0)
                act.wait_ge(halves_used, proj_done(L, SU))
                A(su[:], pb[:, 4:6, 0:SSM_WIDTH], ACT.Copy).then_inc(su_copied, 1)
                his(FQ, 1)
                if L == 0:
                    act.wait_ge(const_in, 16)
                    A(ident_r[:], ident, ACT.Copy)
                    A(masks[:, 0], fmask, ACT.Copy)
                    A(masks[:, 1], smask, ACT.Copy).then_inc(masks_ready, 1)
                    trig(0, 0)
                his(FQ, 2, 3)
                if L == 0:
                    trig(0, 1)
                    trig(0, 2)
                his(FK, 0)
                act.wait_ge(uT_ready, L + 1)
                A(uT[:].rearrange("p m s -> p (m s)"), pb[:, 4, :], ACT.Copy).then_inc(uT_copied, 1)
                his(FK, 1)
                if L == 0:
                    trig(0, 3)
                    exp_ln_table()
                his(FK, 2, 3)
                square(FQ, 2)
                his(FVG, 0)
                rstd(FQ)
                normed_heads(FQ, 2, 0)
                his(FVG, 1)
                normed_heads(FQ, 2, 1)
                his(FVG, 2, 3)
                square(FK, 0)
                his(SQ, 0)
                rstd(FK)
                normed_heads(FK, 0, 0)
                his(SQ, 1)
                normed_heads(FK, 0, 1)
                his(SQ, 2, 3)
                act.wait_ge(halves_used, proj_done(L, FVG))
                A(fv[:], pb[:, 2:4, 0:HEADS_WIDTH], ACT.Copy).then_inc(fv_copied, 1)
                his(SK, 0, 1)
                act.wait_ge(gate_read, L + 1)
                link(A(gatel[:], gatez[:], ACT.Abs))
                link(A(gatel[:], gatel[:], ACT.Exp, scale=-1.0))
                A(gatel[:], gatel[:], ACT.Ln, bias=1.0).then_inc(gate_l, 1)
                his(SK, 2, 3)
                act.wait_ge(halves_used, proj_done(L, SQ))
                A(sqT[:, 0:2, :], pb[:, 0:2, 0:SEQ], ACT.Copy, scale=HEAD_DIM ** -0.5).then_inc(sq_copied, 1)
                A(sqT[:, 2, :], pb[:, 4, 0:SEQ], ACT.Copy, scale=HEAD_DIM ** -0.5).then_inc(sq_copied, 1)
                his(SV)
                act.wait_ge(halves_used, proj_done(L, SK))
                A(skT[:, 0:2, :], pb[:, 2:4, 0:SEQ], ACT.Copy).then_inc(sk_copied, 1)
                A(skT[:, 2, :], pb[:, 4, 0:SEQ], ACT.Copy).then_inc(sk_copied, 1)
                hi(g0 + 2 * U_IN, D_MODEL)
                hi(g0 + 2 * U_IN + 1, D_MODEL)
                act.wait_ge(halves_used, proj_done(L, SV))
                A(sv[:], pb[:, 0:2, 0:HEADS_WIDTH], ACT.Copy).then_inc(sv_copied, 1)
                act.wait_ge(s5_y, 2 * L + 2)
                A(s5g[:], s5y[:], ACT.Gelu_apprx_tanh).then_inc(s5_gelu, 1)
                hi(g0 + 2 * U_IN + 2, D_MODEL)
                act.wait_ge(glu_ready, L + 1)
                for m in range(2):
                    A(s5sg[:, m, :], pb[:, 2, m * SEQ:(m + 1) * SEQ], ACT.Sigmoid,
                      bias=col(L, S_BGL + m)).then_inc(glu_sig, 1)
                exp_ln_table()

                def sb_softplus(b):
                    act.wait_ge(z_ready, 2 * L + b + 1)
                    if b:
                        act.wait_ge(sp_ready, 2 * L + b)
                    link(A(sb_u[:], pb[:, 5:8, 0:3 * P], ACT.Abs))
                    link(A(sb_u[:], sb_u[:], ACT.Exp, scale=-1.0))
                    A(sb_u[:], sb_u[:], ACT.Ln, bias=1.0).then_inc(sb_l, 1)

                def sb_weights(b):
                    act.wait_ge(a_ready, 2 * L + b + 1)
                    if b:
                        act.wait_ge(sby_ready, 2 * L + b)
                    A(sb_a[:], pb[:, 5:8, 0:3 * P], ACT.Exp).then_inc(at_ready, 1)

                def fox_probs(grp):
                    act.wait_ge(fox_max, 3 * L + grp + 1)
                    for j in range(2):
                        hd = 2 * grp + j
                        bank = FOX_BANKS[grp] + j
                        for t in range(TILES):
                            o, n = (0, P) if t == 0 else (P, 2 * P)
                            last = A(pf[:, hd, o:o + n], pb[:, bank, o:o + n], ACT.Exp,
                                     bias=fox_nmax[:, grp, t, j:j + 1], accum_out=fox_rs[:, t, hd:hd + 1])
                    last.then_inc(fox_p, 1)

                def pT_copy(hd):
                    act.wait_ge(pT_ready, HEADS * L + hd + 1)
                    A(pT[:, hd, :], pb[:, 3, 0:3 * P], ACT.Copy).then_inc(pT_even, 1)

                def mix_rms(m):
                    act.wait_ge(foxy_done if m == 0 else sby_done, (L + 1) * (m + 1))
                    w = HEADS_WIDTH
                    A(sqtmp[:, :, m * w:(m + 1) * w], ymix[:, :, m * w:(m + 1) * w], ACT.Square).then_inc(mix_sq, 1)
                    act.wait_ge(mix_sum, 2 * L + m + 1)
                    o = 12 * m
                    link(A(stat2[:, 24 + o:36 + o], stat2[:, o:o + 12], ACT.Ln, scale=1.0 / HEAD_DIM, bias=eps))
                    A(stat2[:, o:o + 12], stat2[:, 24 + o:36 + o], ACT.Exp, scale=-0.5).then_inc(mix_rstd, 1)

                def mix_his(part):
                    act.wait_ge(mixT_ready, 4 * L + part + 1)
                    for i, k in enumerate(MIX_PARTS[part][1]):
                        A(act_hi[:, k, :], pb[:, MIX_PARTS[part][0], i * SEQ:(i + 1) * SEQ], ACT.Copy,
                          scale=col(L, S_GO + k)).then_inc(mix_hi, 1)

                sb_softplus(0)
                fox_probs(0)
                fox_probs(1)
                sb_weights(0)
                act.wait_ge(s5_r, L + 1)
                A(s5q[:], s5y[:], ACT.Square).then_inc(s5_sq, 1)
                fox_probs(2)
                pT_copy(0)
                act.wait_ge(s5_ms, L + 1)
                link(A(s5m[:].rearrange("p m s -> p (m s)"), pb[:, 2, :], ACT.Ln, bias=eps))
                A(s5m[:], s5m[:], ACT.Exp, scale=-0.5).then_inc(s5_rstd, 1)
                pT_copy(2)
                sb_softplus(1)
                pT_copy(4)
                act.wait_ge(s5_norm, L + 1)
                for m in range(2):
                    A(act_hi[:, 6 + m, :], s5q[:, m, :], ACT.Copy, scale=col(L, S_GO + 6 + m)).then_inc(mix_hi, 1)
                sb_weights(1)
                hi(g0 + 2 * U_IN + 3, D_MODEL)
                mix_rms(0)
                mix_rms(1)
                mix_his(0)
                hi(g0 + 2 * U_IN + 4, D_MODEL)
                mix_his(1)
                hi(g0 + 2 * U_IN + 5, D_MODEL)
                mix_his(2)
                mix_his(3)
                for j in range(6, 8 + EARLY):
                    if L and j >= 8:
                        moe_hi(4 + j - 8)
                    else:
                        hi(g0 + 2 * U_IN + j, D_MODEL)

            exp_ln_table()
            norm_stats(0)
            for g in range(RING):
                hi(g, 2 * SSM_WIDTH)
            hT_his(0, 0, S_GA)
            s5_exps(0)
            attention(0)

            norm_stats(1)
            hT_his(1, 0, S_GF)
            g = 2 * U_FFN0 + EARLY
            for c in range(F_CHUNKS + 1):
                if c < F_CHUNKS:
                    for j in range(EARLY if c < 2 else 0, 8 if c else 8 + EARLY):
                        hi(g, HALF)
                        g += 1
                        if c == 5 and j % 2:
                            trig(1, j // 2)
                if c:
                    for j in range(4):
                        hi(g, HALF)
                        g += 1
                if c == F_CHUNKS:
                    for j in range(EARLY):
                        hi(g + j, 2 * SSM_WIDTH)
                if c < F_CHUNKS:
                    act.wait_ge(halves_used, ffn_done(2 * U_FFN0, c, 1, True))
                    if c:
                        act.wait_ge(d_hf, c)
                    A(d_sg[:], pb[:, 0:4, 0:SEQ], ACT.Silu).then_inc(d_silu, 1)
                if c == 2:
                    s5_exps(1)
                if c < F_CHUNKS:
                    act.wait_ge(d_hf, c + 1)
                    if c >= 2:
                        act.wait_ge(halves_used, ffn_done(2 * U_FFN0, c - 1, 2, True))
                    A(d_hi[:, c % 2], d_h[:], ACT.Copy).then_inc(d_hhi, 1)

            exp_ln_table()
            norm_stats(2)
            hT_his(2, 1, S_GA)
            attention(1)

            norm_stats(3)
            hT_his(3, 1, S_GF)
            act.wait_ge(r_logitsT, 1)
            A(logitsT[:], pb[0:EXPERTS, 4, 0:SEQ], ACT.Copy).then_inc(r_copied, 1)
            act.wait_ge(r_d, 1)
            A(stat2[:, 8:10], stat2[:, 6:8], ACT.Exp).then_inc(r_e, 1)
            nc.scalar.preload_act_table(ACT.Silu)
            moe_hi(4 + EARLY)

            def item(i, first):
                hv = [4 + EARLY + 1 if first else 0]
                g0 = 2 * U_MOE if first else i * H_BODY + 2 * U_BASE1

                def his(n):
                    for _ in range(n):
                        moe_hi(hv[0], None if first else i)
                        hv[0] += 1

                def xg_hi_split(after, k=None):
                    ks = slice(0, KD) if k is None else slice(4 * k, 4 * k + 4)
                    act.wait_ge(m_staged, after)
                    A(xg_hi[:, ks], stage[:, ks], ACT.Copy).then_inc(m_xghi, 1)

                if first:
                    for k in range(2):
                        xg_hi_split(k + 1, k)
                for c, before in steps():
                    q = i * F_CHUNKS + c
                    his(3 - EARLY if first and c == 0 else 4)
                    if c == 1 and not first:
                        act.wait_ge(halves_used, ffn_done(g0, 0, 2, False))
                        act.wait_ge(m_gtc, i)
                        A(m_yhi[:], pb[:, 4:6, :], ACT.Copy, scale=m_sgate[:, 0:1]).then_inc(m_ygated, 1)
                    his(4)
                    if c or not first:
                        act.wait_ge(m_T, q)
                        A(m_hi[:, before % 2 if c else 0], pb[:, 6, :], ACT.Copy).then_inc(m_hhi, 1)
                    if c == 5:
                        act.wait_ge(m_gtT, i + 1)
                        A(m_token[:].rearrange("p t s -> p (t s)"), pb[:, 7, 0:2 * P], ACT.Copy)
                        A(m_sgate[:, 0:1], pb[:, 7, 2 * P:2 * P + 1], ACT.Copy).then_inc(m_gtc, 1)
                    act.wait_ge(halves_used, ffn_done(g0, c, 0, first))
                    if c or not first:
                        act.wait_ge(m_hf, q)
                    A(m_sg[:], pb[:, 2 * (c % 2), :], ACT.Silu).then_inc(m_silu, 1)
                    if c or not first:
                        his(4)
                act.wait_ge(halves_used, ffn_done(g0, F_CHUNKS - 1, 1, first))
                xg_hi_split(i * 2 + 4)

            item(0, True)
            act.wait_ge(r_table, 1)
            last = act.value_load(etab[0:1, ITEMS_MAX:ITEMS_MAX + 1], min_val=EXPERTS - 1, max_val=ITEMS_MAX - 2)
            with act.Fori(1, last + 1) as i:
                item(i, False)
            st = 2 * U_BASE1
            act.wait_ge(m_T, last * F_CHUNKS + F_CHUNKS)
            A(m_hi[:, 0], pb[:, 6, :], ACT.Copy).then_inc(m_hhi, 1)
            for j in range(4):
                moe_hi(H_BODY + j, last)
            act.wait_ge(halves_used, last * H_BODY + (H_BODY + st + 4))
            act.wait_ge(m_gtc, last + 1)
            for nh in range(2):
                A(m_yhi[:, nh * BANK:(nh + 1) * BANK], pb[:, 4 + nh, :], ACT.Copy,
                  scale=m_sgate[:, 0:1]).then_inc(m_ygated, 1)

        @block.vector
        def _(dve):
            V = nc.vector
            n_link = [0]

            def link(ins):
                n_link[0] += 1
                ins.then_inc(dve_seq, 1)
                dve.wait_ge(dve_seq, n_link[0])

            def split_lo(g, n, slot, src):
                dve.wait_ge(hi_ready, g + 1)
                V.tensor_tensor(wlo[:, slot, 0:n], src[:, g_part(slot) * n:(g_part(slot) + 1) * n],
                                whi[:, slot, 0:n].bitcast(F32), ALU.subtract).then_inc(lo_ready, 1)

            def lo(g, n):
                split_lo(g, n, g % RING, raw[:, g // 2 % RAW])

            def moe_lo(hv, item=None):
                g = 2 * U_BASE1 + hv
                split_lo(g if item is None else item * H_BODY + g, HALF, g % RING, moe_raw(hv // 2 % MOE_RAW))

            def norm_step(event, t, scale):
                if scale:
                    dve.wait_ge(x_rstd, 2 * event + t + 1)
                    for nh in range(2):
                        cols = slice(nh * BANK, (nh + 1) * BANK)
                        V.tensor_scalar(h[:, t, cols], x[:, t, cols], stat[:, 8 + t:9 + t], None,
                                        ALU.mult).then_inc(normed, 1)
                else:
                    dve.wait_ge(x_sq, 2 * event + t + 1)
                    V.tensor_tensor(stat[:, 4 + t:5 + t], stat[:, 2 * t:2 * t + 1], stat[:, 2 * t + 1:2 * t + 2],
                                    ALU.add).then_inc(x_sum, 1)

            def hT_los(event, layer, gain):
                banks = XT_BANKS[event % 2]
                for k in range(KD):
                    dve.wait_ge(hT_hi, 8 * event + (k | 1) + 1)
                    b, o = banks[k // 2], (k % 2) * SEQ
                    V.scalar_tensor_tensor(act_lo[:, k, :], pb[:, b, o:o + SEQ], col(layer, gain + k),
                                           act_hi[:, k, :].bitcast(F32), ALU.mult, ALU.subtract).then_inc(hT_lo, 1)

            def tables(layer, step):
                th, n, phi, phi_hi, phi_lo = (s5s[:, i, :] for i in (2, 3, 6, 4, 5))
                k, part = divmod(step - 1, 3)
                ks = slice(2 * k, 2 * k + 2)
                if step == 0:
                    dve.wait_ge(s5_exp, layer + 1)
                    link(V.tensor_tensor(th, s5s[:, 0, :], col(layer, S_AIM, KD), ALU.mult))
                    link(V.tensor_scalar(n, th, 1.0 / TWO_PI, ROUND_ONE, ALU.mult, ALU.add))
                    link(V.tensor_scalar(n, n, ROUND_ONE, None, ALU.subtract))
                    for two_pi in (TWO_PI_A, TWO_PI_B, TWO_PI_C):
                        link(V.scalar_tensor_tensor(th, n, -two_pi, th, ALU.mult, ALU.add))
                    link(V.tensor_scalar(phi, th, 1.0 / TWO_PI, None, ALU.mult))
                    link(V.tensor_scalar(phi, phi, 0.5, -0.5, ALU.min, ALU.max))
                    link(V.tensor_scalar(phi_hi, phi, ROUND_12, ROUND_12, ALU.add, ALU.subtract))
                    V.tensor_tensor(phi_lo, phi, phi_hi, ALU.subtract).then_inc(tab_ang, 1)
                    dve.wait_ge(tab_ang, 5 * layer + 1)
                elif part == 0:
                    for kk in (2 * k, 2 * k + 1):
                        last = V.tensor_scalar(ang[:, kk, :], trow, phi_hi[:, kk:kk + 1], None, ALU.mult)
                    link(last)
                    link(V.tensor_scalar(rnd[:, ks], ang[:, ks], ROUND_ONE, ROUND_ONE, ALU.add, ALU.subtract))
                elif part == 1:
                    link(V.tensor_tensor(ang[:, ks], ang[:, ks], rnd[:, ks], ALU.subtract))
                    for kk in (2 * k, 2 * k + 1):
                        last = V.scalar_tensor_tensor(ang[:, kk, :], trow, phi_lo[:, kk:kk + 1], ang[:, kk, :],
                                                      ALU.mult, ALU.add)
                    link(last)
                else:
                    link(V.tensor_scalar(rnd[:, ks], ang[:, ks], ROUND_ONE, ROUND_ONE, ALU.add, ALU.subtract))
                    V.tensor_tensor(rnd[:, ks], ang[:, ks], rnd[:, ks], ALU.subtract).then_inc(tab_ang, 1)

            def coefs(layer, step):
                are, aim = col(layer, S_ARE, KD), col(layer, S_AIM, KD)
                mag, sn, sh = s5s[:, 1, :], s5s[:, 8, :], s5s[:, 9, :]
                cs, nr, ni, den, cr, ci, t1 = (s5s[:, i, :] for i in (10, 11, 12, 13, 14, 15, 7))
                shape = [P, KD, 32]
                crb = cr.unsqueeze(2).broadcast_to(shape)
                cib = ci.unsqueeze(2).broadcast_to(shape)
                if step == 0:
                    dve.wait_ge(s5_trig, 2 * layer + 2)
                    link(V.tensor_tensor(cs, sh, sh, ALU.mult))
                    link(V.tensor_scalar(cs, cs, -2.0, 1.0, ALU.mult, ALU.add))
                    link(V.tensor_tensor(nr, mag, cs, ALU.mult))
                    link(V.tensor_scalar(nr, nr, -1.0, None, ALU.add))
                    link(V.tensor_tensor(ni, mag, sn, ALU.mult))
                elif step == 1:
                    link(V.tensor_tensor(den, are, are, ALU.mult))
                    link(V.tensor_tensor(t1, aim, aim, ALU.mult))
                    link(V.tensor_tensor(den, den, t1, ALU.add))
                    link(V.reciprocal(den, den))
                elif step == 2:
                    link(V.tensor_tensor(cr, nr, are, ALU.mult))
                    link(V.tensor_tensor(t1, ni, aim, ALU.mult))
                    link(V.tensor_tensor(cr, cr, t1, ALU.add))
                    link(V.tensor_tensor(cr, cr, den, ALU.mult))
                elif step == 3:
                    link(V.tensor_tensor(ci, ni, are, ALU.mult))
                    link(V.tensor_tensor(t1, nr, aim, ALU.mult))
                    link(V.tensor_tensor(ci, ci, t1, ALU.subtract))
                    link(V.tensor_tensor(ci, ci, den, ALU.mult))
                elif step == 4:
                    dve.wait_ge(cmat_in, 16 * (layer + 1))
                    link(V.tensor_tensor(cbar[:, 0], cmat[:, 0], crb, ALU.mult))
                    link(V.tensor_tensor(cbar[:, 1], cmat[:, 1], cib, ALU.mult))
                    link(V.tensor_tensor(cbar[:, 0], cbar[:, 0], cbar[:, 1], ALU.subtract))
                    link(V.tensor_scalar(cbar[:, 1], cbar[:, 0], -1.0, None, ALU.mult))
                else:
                    link(V.tensor_tensor(cbar[:, 2], cmat[:, 0], cib, ALU.mult))
                    link(V.tensor_tensor(cmat[:, 1], cmat[:, 1], crb, ALU.mult))
                    link(V.tensor_tensor(cbar[:, 2], cbar[:, 2], cmat[:, 1], ALU.add))
                    V.tensor_scalar(cbar[:, 2], cbar[:, 2], -1.0, None, ALU.mult).then_inc(cbar_ready, 1)

            def s5_piece(layer, q, piece):
                cs = tabc[:, 2 * q:2 * q + 2, :].rearrange("p k s -> p (k s)")
                sn = tabs[:, 2 * q:2 * q + 2, :].rearrange("p k s -> p (k s)")
                w = [s5w[:, i].rearrange("p k s -> p (k s)") for i in range(6)]
                w += [s5w2[:, i].rearrange("p k s -> p (k s)") for i in range(2)]
                if piece == 0:
                    dve.wait_ge(bu_ready, 4 * layer + q + 1)
                    dve.wait_ge(tab_ready, 4 * layer + 4)
                    if q:
                        dve.wait_ge(s5_prod, 4 * layer + q)
                    V.tensor_tensor(w[0], pb[:, 5, :], cs, ALU.mult)
                    V.tensor_tensor(w[1], pb[:, 6, :], sn, ALU.mult)
                    V.tensor_tensor(w[2], pb[:, 6, :], cs, ALU.mult)
                    V.tensor_tensor(w[3], pb[:, 5, :], sn, ALU.mult).then_inc(bu_read, 1)
                elif piece == 1:
                    dve.wait_ge(bu_read, 4 * layer + q + 1)
                    link(V.tensor_tensor(w[0], w[0], w[1], ALU.add))
                    link(V.tensor_tensor(w[2], w[2], w[3], ALU.subtract))
                elif piece == 2:
                    for dst, src in ((1, 0), (3, 2)):
                        for k in range(2):
                            mag = s5s[:, 1, 2 * q + k:2 * q + k + 1]
                            last = V.tensor_tensor_scan(s5w[:, dst, k, :], mag.broadcast_to([P, SEQ]),
                                                        s5w[:, src, k, :], 0.0, ALU.mult, ALU.add)
                    link(last)
                else:
                    if q:
                        dve.wait_ge(s5_used, 4 * layer + q)
                    V.tensor_tensor(w[6], w[1], cs, ALU.mult)
                    V.tensor_tensor(w[7], w[3], sn, ALU.mult)
                    V.tensor_tensor(w[4], w[1], sn, ALU.mult)
                    V.tensor_tensor(w[5], w[3], cs, ALU.mult).then_inc(s5_prod, 1)

            def attention(layer):
                L = layer
                g0 = 2 * u_attn(L)
                W = [n for _, n in CHUNKS]

                def lo_w(chunk, j):
                    lo(g0 + 4 * chunk + j, 2 * W[chunk])

                for chunk in range(len(CHUNKS)):
                    q = chunk - (S5_CHUNK0, S5_CHUNK1)[L]
                    for j in range(4):
                        if chunk or (L and j >= EARLY):
                            lo_w(chunk, j)
                        if L == 0:
                            n = 4 * chunk + j
                            for step in range(n if n < 4 else 2 * n - 4, n + 1 if n < 4 else 2 * n - 2):
                                if step < TABLE_STEPS:
                                    tables(0, step)
                            if 0 <= n - COEF_START < COEF_STEPS:
                                coefs(0, n - COEF_START)
                        if j == 0 and 1 <= q <= 4:
                            s5_piece(L, q - 1, 3)
                        if j > 0 and 0 <= q <= 3:
                            s5_piece(L, q, j - 1)
                        if (chunk, j) == (SQ, 3):
                            dve.wait_ge(fv_copied, L + 1)
                            bf = col(L, S_BF, HEADS).unsqueeze(1).broadcast_to([P, TILES, HEADS])
                            V.tensor_tensor(gatez[:], pb[:, 2:4, HEADS_WIDTH:HEADS_WIDTH + HEADS], bf,
                                            ALU.add).then_inc(gate_read, 1)
                        if (chunk, j) == (SK, 3):
                            dve.wait_ge(gate_l, L + 1)
                            V.scalar_tensor_tensor(logf[:], gatez[:], 0.0, gatel[:], ALU.min,
                                                   ALU.subtract).then_inc(logf_ready, 1)
                if L == 0:
                    s5_piece(0, 3, 3)
                def s5_output():
                    dve.wait_ge(s5_used, 4 * L + 4)
                    for m in range(2):
                        V.scalar_tensor_tensor(s5y[:, m, :], uT[:, m, :], col(L, S_DSK + m),
                                               pb[:, 7, m * SEQ:(m + 1) * SEQ], ALU.mult, ALU.add).then_inc(s5_y, 1)

                if L:
                    s5_output()
                V.memset(qk[:, :, 0:HEADS, 65], 1.0)
                V.memset(qk[:, :, HEADS:, 64], 1.0)
                dve.wait_ge(c_ready, L + 1)
                cps = pb[:, 2, 0:2 * HEADS].rearrange("p (t h) -> p t h", t=TILES)
                V.tensor_copy(qk[:, :, 0:HEADS, 64], cps)
                V.tensor_scalar(qk[:, :, HEADS:, 65], cps, -1.0, None, ALU.mult).then_inc(aug_ready, 1)
                if L == 0:
                    s5_output()
                lo(g0 + 2 * U_IN, D_MODEL)
                for hd in range(HEADS):
                    dve.wait_ge(foxT_ready, HEADS * L + hd + 1)
                    V.tensor_scalar(fT[:, hd, :], pb[0:AUG, 3 + hd % 2, 0:SEQ], small[0:AUG, L, S_GQ:S_GQ + 1],
                                    None, ALU.mult)
                    V.tensor_scalar(fT[:, HEADS + hd, :], pb[0:AUG, 3 + hd % 2, SEQ:2 * SEQ],
                                    small[0:AUG, L, S_GK:S_GK + 1], None, ALU.mult).then_inc(fT_copied, 1)

                def sb_plus(b):
                    dve.wait_ge(sb_l, 2 * L + b + 1)
                    if b:
                        dve.wait_ge(a_ready, 2 * L + b)
                    V.scalar_tensor_tensor(sb_sp[:], pb[:, 5:8, 0:3 * P], 0.0, sb_u[:], ALU.max,
                                           ALU.add).then_inc(sp_ready, 1)

                def fox_maxima(grp):
                    dve.wait_ge(logits_ready, 3 * L + grp + 1)
                    b = FOX_BANKS[grp]
                    V.tensor_reduce(fox_nmax[:, grp, 0, :], pb[:, b:b + 2, 0:P], AX.X, ALU.max)
                    link(V.tensor_reduce(fox_nmax[:, grp, 1, :], pb[:, b:b + 2, P:3 * P], AX.X, ALU.max))
                    V.tensor_scalar(fox_nmax[:, grp], fox_nmax[:, grp], -1.0, None, ALU.mult).then_inc(fox_max, 1)

                def pT_copy(hd):
                    dve.wait_ge(pT_ready, HEADS * L + hd + 1)
                    V.tensor_copy(pT[:, hd, :], pb[:, 4, 0:3 * P]).then_inc(pT_odd, 1)

                def sby_copy(b):
                    dve.wait_ge(sby_ready, 2 * L + b + 1)
                    c = HEADS_WIDTH + b * SBW
                    V.tensor_copy(ymix[:, :, c:c + SBW],
                                  pb[:, SBY_BANKS[b], 0:2 * SBW].rearrange("p (t d) -> p t d", t=TILES)
                                  ).then_inc(sby_done, 1)

                def mix_sums(m):
                    dve.wait_ge(mix_sq, 2 * L + m + 1)
                    for t in range(TILES):
                        o = 12 * m + 6 * t
                        last = V.tensor_reduce(
                            stat2[:, o:o + 6],
                            sqtmp[:, t, m * HEADS_WIDTH:(m + 1) * HEADS_WIDTH].rearrange("p (h d) -> p h d", d=HEAD_DIM),
                            AX.X, ALU.add)
                    last.then_inc(mix_sum, 1)

                def mix_scale(m):
                    dve.wait_ge(mix_rstd, 2 * L + m + 1)
                    for t in range(TILES):
                        o = 12 * m + 6 * t
                        ym = ymix[:, t, m * HEADS_WIDTH:(m + 1) * HEADS_WIDTH].rearrange("p (h d) -> p h d", d=HEAD_DIM)
                        last = V.tensor_tensor(ym, ym, stat2[:, o:o + 6].unsqueeze(2).broadcast_to([P, HEADS, HEAD_DIM]),
                                               ALU.mult)
                    last.then_inc(mix_ready, 1)

                def mix_los(part):
                    dve.wait_ge(mix_hi, 8 * L + 3 + MIX_PARTS[part][1][-1])
                    for i, k in enumerate(MIX_PARTS[part][1]):
                        V.scalar_tensor_tensor(act_lo[:, k, :], pb[:, MIX_PARTS[part][0], i * SEQ:(i + 1) * SEQ],
                                               col(L, S_GO + k), act_hi[:, k, :].bitcast(F32), ALU.mult,
                                               ALU.subtract).then_inc(mix_lo, 1)

                lo(g0 + 2 * U_IN + 1, D_MODEL)
                fox_maxima(0)
                sb_plus(0)
                fox_maxima(1)
                lo(g0 + 2 * U_IN + 2, D_MODEL)
                dve.wait_ge(glu_sig, 2 * L + 2)
                V.tensor_tensor(s5y[:], s5g[:], s5sg[:], ALU.mult).then_inc(s5_r, 1)
                fox_maxima(2)
                pT_copy(1)
                pT_copy(3)
                dve.wait_ge(s5_rstd, L + 1)
                V.tensor_tensor(s5q[:], s5y[:], s5m[:], ALU.mult).then_inc(s5_norm, 1)
                sby_copy(0)
                sb_plus(1)
                dve.wait_ge(fox_p, 3 * L + 3)
                link(V.reciprocal(fox_rs[:], fox_rs[:]))
                pT_copy(5)
                dve.wait_ge(foxy_ready, L + 1)
                for t in range(TILES):
                    r = fox_rs[:, t, :].unsqueeze(2).broadcast_to([P, HEADS, HEAD_DIM])
                    last = V.tensor_tensor(ymix[:, t, 0:HEADS_WIDTH].rearrange("p (h d) -> p h d", d=HEAD_DIM),
                                           pb[:, t, 0:HEADS_WIDTH].rearrange("p (h d) -> p h d", d=HEAD_DIM),
                                           r, ALU.mult)
                last.then_inc(foxy_done, 1)
                for m in range(2):
                    dve.wait_ge(mix_hi, 8 * L + m + 1)
                    V.scalar_tensor_tensor(act_lo[:, 6 + m, :], s5q[:, m, :], col(L, S_GO + 6 + m),
                                           act_hi[:, 6 + m, :].bitcast(F32), ALU.mult,
                                           ALU.subtract).then_inc(mix_lo, 1)
                mix_sums(0)
                sby_copy(1)
                mix_scale(0)
                mix_sums(1)
                mix_scale(1)
                lo(g0 + 2 * U_IN + 3, D_MODEL)
                mix_los(0)
                lo(g0 + 2 * U_IN + 4, D_MODEL)
                mix_los(1)
                lo(g0 + 2 * U_IN + 5, D_MODEL)
                mix_los(2)
                mix_los(3)
                for j in range(6, 7 + EARLY):
                    if L and j >= 8:
                        moe_lo(4 + j - 8)
                    else:
                        lo(g0 + 2 * U_IN + j, D_MODEL)

            def residual_and_norm(n):
                def add(t, nh):
                    if t == 0:
                        dve.wait_ge(out_tile0, 2 * n + nh + 1)
                    else:
                        dve.wait_ge(halves_used, out_done_at(n))
                    xs = x[:, t, nh * BANK:(nh + 1) * BANK]
                    bank = 4 + 2 * t + nh if n == 1 else OUT_BANKS[2 * t + nh]
                    V.tensor_tensor(xs, xs, pb[:, bank, :], ALU.add).then_inc(x_done, 1)

                add(0, 0)
                add(0, 1)
                add(1, 0)
                norm_step(n + 1, 0, False)
                add(1, 1)
                norm_step(n + 1, 0, True)
                norm_step(n + 1, 1, False)
                norm_step(n + 1, 1, True)
                if n == 0:
                    lo(2 * U_FFN0 + EARLY - 1, HALF)
                elif n == 1:
                    lo(2 * U_L1 + EARLY - 1, 2 * SSM_WIDTH)
                else:
                    moe_lo(4 + EARLY - 1)

            for t in range(TILES):
                norm_step(0, t, False)
                norm_step(0, t, True)
            dve.wait_ge(const_in, 16)
            dve.wait_ge(small_in, 16)
            for g in range(RING):
                lo(g, 2 * SSM_WIDTH)
            hT_los(0, 0, S_GA)
            attention(0)
            residual_and_norm(0)
            hT_los(1, 0, S_GF)
            g = 2 * U_FFN0 + EARLY
            for c in range(F_CHUNKS + 1):
                if c < F_CHUNKS:
                    for j in range(EARLY if c < 2 else 0, 8 if c else 8 + EARLY):
                        lo(g, HALF)
                        g += 1
                        if c in (3, 4) and 8 * (c - 3) + j < TABLE_STEPS:
                            tables(1, 8 * (c - 3) + j)
                        if c == 6 and j < COEF_STEPS:
                            coefs(1, j)
                if c:
                    for j in range(4):
                        lo(g, HALF)
                        g += 1
                if c == F_CHUNKS:
                    for j in range(EARLY - 1):
                        lo(g + j, 2 * SSM_WIDTH)
                if c < F_CHUNKS:
                    dve.wait_ge(d_silu, c + 1)
                    if c:
                        dve.wait_ge(d_hlo, c)
                    V.tensor_tensor(d_h[:], d_sg[:], pb[:, 0:4, SEQ:2 * SEQ], ALU.mult).then_inc(d_hf, 1)
                    dve.wait_ge(d_hhi, c + 1)
                    V.tensor_tensor(d_lo[:, c % 2], d_h[:], d_hi[:, c % 2].bitcast(F32),
                                    ALU.subtract).then_inc(d_hlo, 1)
            residual_and_norm(1)
            hT_los(2, 1, S_GA)
            attention(1)
            residual_and_norm(2)

            R = smalls_r
            lg, lg2, e8, w8, sel1, sel2, sel, gates, posm = (R[:, i, :, 0:EXPERTS] for i in range(9))
            shape = [P, TILES, EXPERTS]
            revb = rev.unsqueeze(1).broadcast_to(shape)

            def bc(a):
                return a.unsqueeze(2).broadcast_to(shape)

            def argmax(src, m, dst):
                link(V.tensor_reduce(m, src, AX.X, ALU.max))
                link(V.tensor_tensor(e8, src, bc(m), ALU.is_equal))
                link(V.tensor_tensor(w8, e8, revb, ALU.mult))
                link(V.tensor_reduce(stat2[:, 4:6], w8, AX.X, ALU.max))
                link(V.tensor_tensor(dst, w8, bc(stat2[:, 4:6]), ALU.is_equal))

            dve.wait_ge(r_logits, 1)
            link(V.tensor_copy(lg, pb[:, 7, 0:2 * EXPERTS].rearrange("p (t e) -> p t e", t=TILES)))
            argmax(lg, stat2[:, 0:2], sel1)
            link(V.scalar_tensor_tensor(lg2, sel1, -3e38, lg, ALU.mult, ALU.add))
            argmax(lg2, stat2[:, 2:4], sel2)
            V.tensor_tensor(sel, sel1, sel2, ALU.add).then_inc(r_sel, 1)
            V.tensor_tensor(stat2[:, 6:8], stat2[:, 2:4], stat2[:, 0:2], ALU.subtract).then_inc(r_d, 1)
            dve.wait_ge(r_cnt, 1)
            link(V.scalar_tensor_tensor(posm, sel, -1e6,
                                        pb[:, 7, 0:2 * EXPERTS].rearrange("p (t e) -> p t e", t=TILES),
                                        ALU.mult, ALU.add))
            link(V.tensor_scalar(posm, posm, 1e6 - 1.0, None, ALU.add))
            link(V.tensor_copy(pos_i[:, :, 0:EXPERTS], posm))
            ovr, inc = R[:, 9, 0, 0:EXPERTS], R[:, 9, 1, 0:EXPERTS]
            link(V.tensor_scalar(ovr, pb[:, 7, 2 * EXPERTS:3 * EXPERTS], float(CAP), None, ALU.is_gt))
            ef = R[:, 11].rearrange("p t e -> p (t e)")

            def gate_values():
                dve.wait_ge(r_e, 1)
                link(V.tensor_scalar(stat2[:, 10:12], stat2[:, 8:10], 1.0, None, ALU.add))
                link(V.reciprocal(stat2[:, 10:12], stat2[:, 10:12]))
                link(V.tensor_tensor(stat2[:, 12:14], stat2[:, 8:10], stat2[:, 10:12], ALU.mult))
                link(V.tensor_tensor(gates, sel1, bc(stat2[:, 10:12]), ALU.mult))
                link(V.tensor_tensor(e8, sel2, bc(stat2[:, 12:14]), ALU.mult))
                link(V.tensor_tensor(gates, gates, e8, ALU.add))
                link(V.tensor_copy(gate_i[:, :, 0:EXPERTS], gates))

            def item_table():
                link(V.tensor_tensor_scan(inc, ones[:, 0:EXPERTS], ovr, 0.0, ALU.mult, ALU.add))
                link(V.memset(ef, 0.0))
                link(V.tensor_copy(ef[:, 0:EXPERTS], eidx))
                link(V.tensor_scalar(ef[:, ITEMS_MAX:ITEMS_MAX + 1], inc[:, EXPERTS - 1:EXPERTS],
                                     float(EXPERTS - 1), None, ALU.add))
                gate_values()

            def second_items(step):
                wide = [P, ITEMS_MAX - EXPERTS, EXPERTS]
                numbers = iota[:, 1:1 + ITEMS_MAX - EXPERTS].unsqueeze(2).broadcast_to(wide)
                if step == 0:
                    link(V.tensor_tensor(second_oh[:], inc.unsqueeze(1).broadcast_to(wide), numbers, ALU.is_equal))
                    link(V.tensor_tensor(second_oh[:], second_oh[:], ovr.unsqueeze(1).broadcast_to(wide), ALU.mult))
                elif step == 1:
                    for t in range(TILES):
                        last = V.tensor_tensor(second_w[:, t], posm[:, t].unsqueeze(1).broadcast_to(wide),
                                               second_oh[:], ALU.mult)
                    link(last)
                    link(V.tensor_reduce(pos_i[:, :, EXPERTS:ITEMS_MAX], second_w[:], AX.X, ALU.add))
                    link(V.tensor_scalar(pos_i[:, :, EXPERTS:ITEMS_MAX], pos_i[:, :, EXPERTS:ITEMS_MAX],
                                         -float(CAP), None, ALU.add))
                elif step == 2:
                    for t in range(TILES):
                        last = V.tensor_tensor(second_w[:, t], gates[:, t].unsqueeze(1).broadcast_to(wide),
                                               second_oh[:], ALU.mult)
                    link(last)
                    link(V.tensor_reduce(gate_i[:, :, EXPERTS:ITEMS_MAX], second_w[:], AX.X, ALU.add))
                else:
                    link(V.tensor_tensor(second_w[:, 0], second_oh[:], eidx.unsqueeze(1).broadcast_to(wide), ALU.mult))
                    link(V.tensor_reduce(ef[:, EXPERTS:ITEMS_MAX], second_w[:, 0], AX.X, ALU.add))
                    V.tensor_copy(etab[0:1, 0:16], ef[0:1, 0:16]).then_inc(r_table, 1)

            def onehot(i):
                for t in range(TILES):
                    last = V.tensor_scalar(m_pm[:, t, :], iota, pos_i[:, t, bass.ds(i, 1)], None, ALU.is_equal)
                last.then_inc(m_pmr, 1)

            def stage_half(k, event, bank=7):
                dve.wait_ge(m_gather, event)
                ga = col(1, S_GF + 4 * k, 4).unsqueeze(2).broadcast_to([P, 4, P])
                V.tensor_tensor(stage[:, 4 * k:4 * k + 4, :], pb[:, bank, :].rearrange("p (k s) -> p k s", k=4),
                                ga, ALU.mult).then_inc(m_staged, 1)

            def xg_lo_split(event, k=None):
                ks = slice(0, KD) if k is None else slice(4 * k, 4 * k + 4)
                dve.wait_ge(m_xghi, event)
                V.tensor_tensor(xg_lo[:, ks], stage[:, ks], xg_hi[:, ks].bitcast(F32), ALU.subtract).then_inc(m_xglo, 1)

            def gated_lo(event, halves=slice(0, 2)):
                dve.wait_ge(m_ygated, event)
                a, b = halves.start, halves.stop
                V.scalar_tensor_tensor(m_ylo[:, a * BANK:b * BANK],
                                       pb[:, 4 + a:4 + b, :].rearrange("p a b -> p (a b)"), m_sgate[:, 0:1],
                                       m_yhi[:, a * BANK:b * BANK].bitcast(F32), ALU.mult,
                                       ALU.subtract).then_inc(m_ysb, 1)

            def add_piece(t, nh, event, bank=7):
                dve.wait_ge(m_scat, event)
                xs = x[:, t, nh * BANK:(nh + 1) * BANK]
                V.tensor_tensor(xs, xs, pb[:, bank, :], ALU.add).then_inc(m_added, 1)

            onehot(0)
            moe_lo(4 + EARLY)
            for k in range(2):
                stage_half(k, k + 1, 7 - k)
                xg_lo_split(k + 1, k)

            def item(i, first):
                hv = [4 + EARLY + 1 if first else 0]
                g0 = 2 * U_MOE if first else i * H_BODY + 2 * U_BASE1

                def los(n, router=None):
                    for k in range(n):
                        if router:
                            router(k)
                        moe_lo(hv[0], None if first else i)
                        hv[0] += 1

                for c, before in steps():
                    q = i * F_CHUNKS + c
                    los(3 - EARLY if first and c == 0 else 4)
                    if not first and c == 1:
                        gated_lo(i)
                    if not first and 2 <= c <= 5:
                        add_piece((c - 2) // 2, c % 2, i * 4 + (c - 5))
                    if c == 6:
                        stage_half(0, i * 2 + 3)
                    if first and c == 0:
                        item_table()
                    los(4, second_items if first and c == 1 else None)
                    if c or not first:
                        dve.wait_ge(m_hhi, q)
                        b = before % 2 if c else 0
                        V.tensor_tensor(m_lo[:, b], pb[:, 6, :], m_hi[:, b].bitcast(F32),
                                        ALU.subtract).then_inc(m_hlo, 1)
                    if c == 3:
                        for t in range(TILES):
                            V.tensor_scalar(m_slot[:, t, :], iota, pos_i[:, t, bass.ds(i, 1)], None, ALU.is_equal)
                            V.tensor_copy(m_gate[:, t:t + 1], gate_i[:, t, bass.ds(i, 1)])
                        onehot(i + 1)
                    if c == 6:
                        stage_half(1, i * 2 + 4)
                    if c or not first:
                        los(4)
                    dve.wait_ge(m_silu, q + 1)
                    dve.wait_ge(halves_used, ffn_done(g0, c, 1, first))
                    if c or not first:
                        dve.wait_ge(m_T, q)
                    V.tensor_tensor(m_h[:], m_sg[:], pb[:, 2 * (c % 2) + 1, :], ALU.mult).then_inc(m_hf, 1)
                xg_lo_split(i + 3)

            item(0, True)
            dve.wait_ge(r_table, 1)
            last = dve.value_load(etab[0:1, ITEMS_MAX:ITEMS_MAX + 1], min_val=EXPERTS - 1, max_val=ITEMS_MAX - 2)
            with dve.Fori(1, last + 1) as i:
                item(i, False)
            dve.wait_ge(m_hhi, last * F_CHUNKS + F_CHUNKS)
            V.tensor_tensor(m_lo[:, 0], pb[:, 6, :], m_hi[:, 0].bitcast(F32), ALU.subtract).then_inc(m_hlo, 1)
            for j in range(4):
                moe_lo(H_BODY + j, last)
            for nh in range(2):
                gated_lo(last + (nh + 1), slice(nh, nh + 1))
            for n, (t, nh) in enumerate(LAST_PIECES):
                add_piece(t, nh, last * 4 + (n + 1), LAST_BANKS[n])

        @block.tensor
        def _(pe):
            M = nc.tensor.matmul

            def T(out, in_, n=P):
                return nc.tensor.transpose(out, in_, ident)

            def three(out, lhs, rhs, start, stop):
                (lh, ll), (rh, rl) = lhs, rhs
                M(out, lh, rh, start=start, stop=False)
                M(out, lh, rl, start=False, stop=False)
                return M(out, ll, rh, start=False, stop=stop)

            def wpair(slot, a, b):
                return whi[:, slot, a:b], wlo[:, slot, a:b]

            def apair(k, a, b):
                return act_hi[:, k, a:b], act_lo[:, k, a:b]

            def transposes(event):
                banks = XT_BANKS[event % 2]
                for t in range(TILES):
                    for k in range(KD):
                        if k % (KD // 2) == 0:
                            pe.wait_ge(normed, 4 * event + 2 * t + k // (KD // 2) + 1)
                        last = T(pb[:, banks[k // 2], (k % 2) * SEQ + t * P:(k % 2) * SEQ + (t + 1) * P],
                                 h[:, t, k * P:(k + 1) * P])
                        if k % 2 and t:
                            last.then_inc(xT_ready, 1)

            def attention(layer):
                L = layer
                g0 = 2 * u_attn(L)

                def middle(chunk):
                    if chunk == FQ:
                        for m in range(2):
                            for t in range(TILES):
                                last = T(pb[:, 4, m * SEQ + t * P:m * SEQ + (t + 1) * P],
                                         su[:, t, m * P:(m + 1) * P])
                        last.then_inc(uT_ready, 1)
                    q = chunk - (S5_CHUNK0, S5_CHUNK1)[L]
                    if 1 <= q <= 4:
                        s5y_part(q - 1)

                def project(chunk, banks):
                    n = CHUNKS[chunk][1]
                    for j in range(4):
                        if j == 2:
                            middle(chunk)
                        g = g0 + 4 * chunk + j
                        pe.wait_ge(lo_ready, g + 1)
                        for t in range(TILES):
                            for kk in range(2):
                                k = 2 * j + kk
                                if chunk == 0 and t == 0:
                                    pe.wait_ge(hT_lo, 8 * (2 * L) + k + 1)
                                last = three(pb[:, banks[t], 0:n], apair(k, t * P, (t + 1) * P),
                                             wpair(g % RING, kk * n, (kk + 1) * n), k == 0, k == KD - 1)
                        last.then_inc(halves_used, 1)

                def project_T(chunk, banks):
                    n = CHUNKS[chunk][1]
                    for j in range(4):
                        if j == 2:
                            middle(chunk)
                        g = g0 + 4 * chunk + j
                        pe.wait_ge(lo_ready, g + 1)
                        for pr in range(3):
                            for kk in range(2):
                                k = 2 * j + kk
                                last = three(pb[:, banks[pr], 0:SEQ],
                                             wpair(g % RING, kk * n + pr * P, kk * n + (pr + 1) * P),
                                             apair(k, 0, SEQ), k == 0, k == KD - 1)
                        last.then_inc(halves_used, 1)

                def bu(q):
                    if q == 0:
                        pe.wait_ge(uT_copied, L + 1)
                        pe.wait_ge(bmat_in, 16 * (L + 1))
                    else:
                        pe.wait_ge(bu_read, 4 * L + q)
                    for kk in range(2):
                        m, j = divmod(2 * q + kk, 4)
                        if kk:
                            pe.wait_ge(bu_first, 4 * L + q + 1)
                        for ri in range(2):
                            last = M(pb[:, 5 + ri, kk * SEQ:(kk + 1) * SEQ], bmat[32 * j:32 * j + 32, ri, m, :],
                                     uT[32 * j:32 * j + 32, m, :], start=True, stop=True)
                        last.then_inc((bu_first, bu_ready)[kk], 1)

                def s5y_part(q):
                    pe.wait_ge(s5_prod, 4 * L + q + 1)
                    if q == 0:
                        pe.wait_ge(cbar_ready, L + 1)
                    for kk in range(2):
                        k = 2 * q + kk
                        m, j = divmod(k, 4)
                        for n, (ci, w) in enumerate(((0, s5w2[:, 0]), (1, s5w2[:, 1]), (2, s5w[:, 4]),
                                                     (2, s5w[:, 5]))):
                            last = M(pb[32 * j:32 * j + 32, 7, m * SEQ:(m + 1) * SEQ], cbar[:, ci, k, :],
                                     w[:, kk, :], start=(n == 0), stop=(n == 3))
                    last.then_inc(s5_used, 1)

                def before(chunk):
                    q = chunk - (S5_CHUNK0, S5_CHUNK1)[L]
                    if 0 <= q <= 3:
                        bu(q)

                project(SU, (4, 5))
                pe.wait_ge(su_copied, L + 1)
                project(FQ, (2, 3))
                before(FK)
                project(FK, (0, 1))
                before(FVG)
                pe.wait_ge(qk_normed, 2 * L + 1)
                project(FVG, (2, 3))
                before(SQ)
                pe.wait_ge(qk_normed, 2 * L + 2)
                project_T(SQ, (0, 1, 4))
                before(SK)
                pe.wait_ge(fv_copied, L + 1)
                pe.wait_ge(gate_read, L + 1)
                pe.wait_ge(sq_copied, 2 * L + 2)
                project_T(SK, (2, 3, 4))
                before(SV)
                project(SV, (0, 1))
                pe.wait_ge(logf_ready, L + 1)
                pe.wait_ge(sk_copied, 2 * L + 2)
                M(pb[:, 2, 0:HEADS], tri, logf[:, 0, :], start=True, stop=True)
                M(pb[:, 2, HEADS:2 * HEADS], tri, logf[:, 1, :], start=True, stop=False)
                M(pb[:, 2, HEADS:2 * HEADS], ones, logf[:, 0, :], start=False, stop=True).then_inc(c_ready, 1)
                if L == 0:
                    s5y_part(3)

                def sb_logits(b):
                    for j in range(3):
                        hd = 3 * b + j
                        r0, pr = HEAD_DIM * (hd % 2), hd // 2
                        for kt in range(2):
                            o, n = (0, 2 * P) if kt == 0 else (2 * P, P)
                            M(pb[:, 5 + j, o:o + n], skT[r0:r0 + HEAD_DIM, pr, kt * P:(kt + 1) * P],
                              sqT[r0:r0 + HEAD_DIM, pr, kt * P:SEQ], start=(kt == 0), stop=False,
                              skip_group_check=True)
                            last = M(pb[:, 5 + j, o:o + P], ident_r[:], masks[:, 1], start=False, stop=(kt == 1),
                                     skip_group_check=True)
                    last.then_inc(z_ready, 1)

                def sb_sums(b):
                    pe.wait_ge(sp_ready, 2 * L + b + 1)
                    for j in range(3):
                        bank = 5 + j
                        M(pb[:, bank, 0:2 * P], nrev, sb_sp[:, j, 0:2 * P], start=False, stop=False,
                          skip_group_check=True)
                        M(pb[:, bank, P:2 * P], nones, sb_sp[:, j, 2 * P:3 * P], start=False, stop=False,
                          skip_group_check=True)
                        last = M(pb[:, bank, 2 * P:3 * P], nrev, sb_sp[:, j, 2 * P:3 * P], start=False, stop=True,
                                 skip_group_check=True)
                    last.then_inc(a_ready, 1)

                def sb_values(b):
                    bank = SBY_BANKS[b]
                    for j in range(3):
                        hd = 3 * b + j
                        c0, o = hd * HEAD_DIM, j * HEAD_DIM
                        M(pb[:, bank, o:o + HEAD_DIM], sb_a[:, j, 0:P], sv[:, 0, c0:c0 + HEAD_DIM],
                          start=True, stop=True)
                        M(pb[:, bank, SBW + o:SBW + o + HEAD_DIM], sb_a[:, j, P:2 * P], sv[:, 0, c0:c0 + HEAD_DIM],
                          start=True, stop=False)
                        last = M(pb[:, bank, SBW + o:SBW + o + HEAD_DIM], sb_a[:, j, 2 * P:3 * P],
                                 sv[:, 1, c0:c0 + HEAD_DIM], start=False, stop=True)
                    last.then_inc(sby_ready, 1)

                def fox_logits(grp):
                    for j in range(2):
                        hd = 2 * grp + j
                        bank = FOX_BANKS[grp] + j
                        pe.wait_ge(fT_copied, HEADS * L + (HEADS if grp else hd + 1))
                        for t in range(TILES):
                            o, n = (0, P) if t == 0 else (P, 2 * P)
                            M(pb[:, bank, o:o + n], fT[:, hd, t * P:(t + 1) * P], fT[:, HEADS + hd, 0:n],
                              start=True, stop=False)
                            last = M(pb[:, bank, o + n - P:o + n], ident_r[:], masks[:, 0], start=False, stop=True)
                    last.then_inc(logits_ready, 1)

                def prob_transposes(hd):
                    if hd >= 2:
                        pe.wait_ge((pT_even, pT_odd)[hd % 2], 3 * L + hd // 2)
                    for blk_ in range(3):
                        last = T(pb[:, 3 + hd % 2, blk_ * P:(blk_ + 1) * P], pf[:, hd, blk_ * P:(blk_ + 1) * P])
                    last.then_inc(pT_ready, 1)

                def mix_transposes(part):
                    bank, ks = MIX_PARTS[part]
                    for i, k in enumerate(ks):
                        for t in range(TILES):
                            last = T(pb[:, bank, i * SEQ + t * P:i * SEQ + (t + 1) * P], ymix[:, t, k * P:(k + 1) * P])
                    last.then_inc(mixT_ready, 1)

                def out_project(j):
                    k = OUT_K_ORDER[j]
                    g = g0 + 2 * U_IN + j
                    pe.wait_ge(lo_ready, g + 1)
                    pe.wait_ge(mix_lo, 8 * L + j + 1)
                    for t in range(TILES):
                        for nh in range(2):
                            last = three(pb[:, OUT_BANKS[2 * t + nh], :], apair(k, t * P, (t + 1) * P),
                                         wpair(g % RING, nh * BANK, (nh + 1) * BANK), j == 0, j == KD - 1)
                            if j == KD - 1 and t == 0:
                                last.then_inc(out_tile0, 1)
                    last.then_inc(halves_used, 1)

                pe.wait_ge(masks_ready, 1)
                pe.wait_ge(s5_y, 2 * L + 2)
                sb_logits(0)
                pe.wait_ge(aug_ready, L + 1)
                pe.wait_ge(s5_gelu, L + 1)
                pe.wait_ge(wglu_in, 16 * (L + 1))
                for m2 in range(2):
                    for m in range(2):
                        last = M(pb[:, 2, m2 * SEQ:(m2 + 1) * SEQ], wglu[:, m, m2 * P:(m2 + 1) * P], s5g[:, m, :],
                                 start=(m == 0), stop=(m == 1))
                last.then_inc(glu_ready, 1)
                for hd in range(HEADS):
                    if hd >= 2:
                        pe.wait_ge(fT_copied, HEADS * L + hd - 1)
                    for j in range(2):
                        for t in range(TILES):
                            o = j * SEQ + t * P
                            last = T(pb[0:AUG, 3 + hd % 2, o:o + P], qk[:, t, j * HEADS + hd, :])
                    last.then_inc(foxT_ready, 1)
                pe.wait_ge(sv_copied, L + 1)
                fox_logits(0)
                fox_logits(1)
                sb_sums(0)
                pe.wait_ge(fox_p, 3 * L + 1)
                fox_logits(2)
                pe.wait_ge(fox_p, 3 * L + 2)
                prob_transposes(0)
                prob_transposes(1)
                pe.wait_ge(s5_sq, L + 1)
                pe.wait_ge(glu_sig, 2 * L + 2)
                M(pb[:, 2, :], blk, s5q[:].rearrange("p m s -> p (m s)"), start=True, stop=True).then_inc(s5_ms, 1)
                pe.wait_ge(at_ready, 2 * L + 1)
                sb_logits(1)
                prob_transposes(2)
                prob_transposes(3)
                pe.wait_ge(s5_rstd, L + 1)
                sb_values(0)
                pe.wait_ge(fox_p, 3 * L + 3)
                prob_transposes(4)
                prob_transposes(5)
                for hd in range(HEADS):
                    if hd == 4:
                        sb_sums(1)
                    pe.wait_ge((pT_even, pT_odd)[hd % 2], 3 * L + hd // 2 + 1)
                    c0 = hd * HEAD_DIM
                    M(pb[:, 0, c0:c0 + HEAD_DIM], pT[:, hd, 0:P], fv[:, 0, c0:c0 + HEAD_DIM], start=True, stop=True)
                    M(pb[:, 1, c0:c0 + HEAD_DIM], pT[:, hd, P:2 * P], fv[:, 0, c0:c0 + HEAD_DIM],
                      start=True, stop=False)
                    last = M(pb[:, 1, c0:c0 + HEAD_DIM], pT[:, hd, 2 * P:3 * P], fv[:, 1, c0:c0 + HEAD_DIM],
                             start=False, stop=True)
                last.then_inc(foxy_ready, 1)
                pe.wait_ge(at_ready, 2 * L + 2)
                sb_values(1)
                pe.wait_ge(foxy_done, L + 1)
                out_project(0)
                pe.wait_ge(sby_done, 2 * L + 1)
                pe.wait_ge(mix_ready, 2 * L + 1)
                mix_transposes(0)
                out_project(1)
                out_project(2)
                pe.wait_ge(mix_lo, 8 * L + 4)
                mix_transposes(1)
                pe.wait_ge(mix_ready, 2 * L + 2)
                mix_transposes(2)
                mix_transposes(3)
                for j in range(3, 8):
                    out_project(j)

            pe.wait_ge(const_in, 16)
            transposes(0)
            attention(0)

            transposes(1)
            g = 2 * U_FFN0
            for c in range(F_CHUNKS + 1):
                if c < F_CHUNKS:
                    for part in range(2):
                        for j in range(4):
                            pe.wait_ge(lo_ready, g + 1)
                            if c == 0 and part == 0:
                                pe.wait_ge(hT_lo, KD + 2 * j + 2)
                            if c and part == 0 and j == 0:
                                pe.wait_ge(d_hf, c)
                            for s in range(F_SUBS):
                                for kk in range(2):
                                    k = 2 * j + kk
                                    last = three(pb[:, s, part * SEQ:(part + 1) * SEQ],
                                                 wpair(g % RING, kk * F_CHUNK + s * P, kk * F_CHUNK + (s + 1) * P),
                                                 apair(k, 0, SEQ), k == 0, k == KD - 1)
                            last.then_inc(halves_used, 1)
                            g += 1
                if c:
                    b = (c - 1) % 2
                    pe.wait_ge(d_hlo, c)
                    for j in range(F_SUBS):
                        pe.wait_ge(lo_ready, g + 1)
                        for t in range(TILES):
                            for nh in range(2):
                                last = three(pb[:, 4 + 2 * t + nh, :],
                                             (d_hi[:, b, j, t * P:(t + 1) * P], d_lo[:, b, j, t * P:(t + 1) * P]),
                                             wpair(g % RING, nh * BANK, (nh + 1) * BANK),
                                             c == 1 and j == 0, c == F_CHUNKS and j == F_SUBS - 1)
                                if c == F_CHUNKS and j == F_SUBS - 1 and t == 0:
                                    last.then_inc(out_tile0, 1)
                        last.then_inc(halves_used, 1)
                        g += 1

            transposes(2)
            attention(1)
            transposes(3)

            pe.wait_ge(wr_in, 16)
            for k in range(KD):
                pe.wait_ge(hT_hi, 8 * 3 + k + 1)
                last = M(pb[0:EXPERTS, 4, 0:SEQ], wr[:, k, :], hT_f[:, k, :], start=(k == 0), stop=(k == KD - 1))
            last.then_inc(r_logitsT, 1)
            pe.wait_ge(r_copied, 1)
            for t in range(TILES):
                last = nc.tensor.transpose(pb[:, 7, t * EXPERTS:(t + 1) * EXPERTS], logitsT[:, t * P:(t + 1) * P],
                                           ident[0:EXPERTS, 0:EXPERTS])
            last.then_inc(r_logits, 1)
            sel = smalls_r[:, 6, :, 0:EXPERTS]
            pe.wait_ge(r_sel, 1)
            M(pb[:, 7, 0:2 * EXPERTS].rearrange("p (t e) -> p t e", t=TILES), tri, sel, start=True, stop=False,
              skip_group_check=True)
            M(pb[:, 7, EXPERTS:3 * EXPERTS].rearrange("p (t e) -> p t e", t=TILES), ones,
              sel[:, 0:1].broadcast_to([P, TILES, EXPERTS]), start=False, stop=False, skip_group_check=True)
            M(pb[:, 7, 2 * EXPERTS:3 * EXPERTS], ones, sel[:, 1], start=False, stop=True,
              skip_group_check=True).then_inc(r_cnt, 1)

            def gather_half(k4, staged, pm_event, bank=7):
                pe.wait_ge(m_pmr, pm_event)
                if staged is not None:
                    pe.wait_ge(m_staged, staged)
                for k in range(4):
                    kk = 4 * k4 + k
                    for t in range(TILES):
                        last = M(pb[:, bank, k * P:(k + 1) * P], h[:, t, kk * P:(kk + 1) * P], m_pm[:, t, :],
                                 start=(t == 0), stop=(t == TILES - 1))
                last.then_inc(m_gather, 1)

            def scatter_piece(t, nh, bank=7):
                M(pb[:, bank, :], m_token[:, t, :], m_yhi[:, nh * BANK:(nh + 1) * BANK], start=True, stop=False)
                M(pb[:, bank, :], m_token[:, t, :], m_ylo[:, nh * BANK:(nh + 1) * BANK],
                  start=False, stop=True).then_inc(m_scat, 1)

            def h_transposes(count):
                pe.wait_ge(m_hf, count)
                for s in range(F_SUBS):
                    last = T(pb[:, 6, s * P:(s + 1) * P], m_h[:, s * P:(s + 1) * P])
                last.then_inc(m_T, 1)

            def down(b, j, slot, start, stop):
                for nh in range(2):
                    last = three(pb[:, 4 + nh, :], (m_hi[:, b, j * P:(j + 1) * P], m_lo[:, b, j * P:(j + 1) * P]),
                                 wpair(slot, nh * BANK, (nh + 1) * BANK), start, stop)
                return last

            gather_half(0, None, 1)
            gather_half(1, None, 1, 6)

            def item(i, first):
                j_ = [0]
                g0 = 2 * U_MOE if first else i * H_BODY + 2 * U_BASE1
                s0 = 2 * U_MOE if first else 2 * (U_BASE1 + U_BODY)

                def half():
                    pe.wait_ge(lo_ready, g0 + (j_[0] + 1))
                    slot = (s0 + j_[0]) % RING
                    j_[0] += 1
                    return slot

                def gate_or_up(bank, halves_of_x=False):
                    for j in range(4):
                        if halves_of_x and j % 2 == 0:
                            pe.wait_ge(m_xglo, j // 2 + 1)
                        slot = half()
                        for kk in range(2):
                            k = 2 * j + kk
                            last = three(pb[:, bank, :], (xg_hi[:, k, :], xg_lo[:, k, :]),
                                         wpair(slot, kk * F_CHUNK, (kk + 1) * F_CHUNK), k == 0, k == KD - 1)
                        last.then_inc(halves_used, 1)

                for c, before in steps():
                    q = i * F_CHUNKS + c
                    if c == 0:
                        if not first:
                            pe.wait_ge(m_xglo, i + 2)
                            pe.wait_ge(m_hf, q)
                    elif c >= 2:
                        pe.wait_ge(m_hf, q - 1)
                    gate_or_up(2 * (c % 2), first and c == 0)
                    if c or not first:
                        if c >= 2 or not first:
                            pe.wait_ge(m_hlo, q - 1)
                        h_transposes(q)
                    if c == 5:
                        pe.wait_ge(m_pmr, i + 2)
                        if not first:
                            pe.wait_ge(m_added, i * 4)
                        else:
                            pe.wait_ge(m_staged, 2)
                        for t in range(TILES):
                            T(pb[:, 7, t * P:(t + 1) * P], m_slot[:, t, :])
                        for t in range(TILES):
                            last = M(pb[:, 7, 2 * P:2 * P + 1], m_slot[:, t, :], m_gate[:, t:t + 1],
                                     start=(t == 0), stop=(t == TILES - 1))
                        last.then_inc(m_gtT, 1)
                    if c == 6:
                        gather_half(1, i * 2 + 3, i + 2)
                    gate_or_up(2 * (c % 2) + 1)
                    if c or not first:
                        pe.wait_ge(m_hlo, q)
                        b, cc = (before % 2, before) if c else (0, F_CHUNKS - 1)
                        if cc == 0 and not first:
                            pe.wait_ge(m_ysb, i)
                        for j in range(F_SUBS):
                            slot = half()
                            last = down(b, j, slot, cc == 0 and j == 0, cc == F_CHUNKS - 1 and j == F_SUBS - 1)
                            last.then_inc(halves_used, 1)
                    if not first and 1 <= c <= 4:
                        if c == 1:
                            pe.wait_ge(m_ysb, i)
                            pe.wait_ge(m_gtc, i)
                            pe.wait_ge(m_staged, i * 2 + 2)
                        else:
                            pe.wait_ge(m_added, i * 4 + (c - 5))
                        scatter_piece((c - 1) // 2, (c - 1) % 2)
                    if c == 5:
                        pe.wait_ge(m_gtc, i + 1)
                        gather_half(0, None, i + 2)

            item(0, True)
            pe.wait_ge(r_table, 1)
            last = pe.value_load(etab[0:1, ITEMS_MAX:ITEMS_MAX + 1], min_val=EXPERTS - 1, max_val=ITEMS_MAX - 2)
            with pe.Fori(1, last + 1) as i:
                item(i, False)
            pe.wait_ge(m_hlo, last * F_CHUNKS + (F_CHUNKS - 1))
            h_transposes(last * F_CHUNKS + F_CHUNKS)
            pe.wait_ge(m_hlo, last * F_CHUNKS + F_CHUNKS)
            st = 2 * U_BASE1
            for j in range(4):
                pe.wait_ge(lo_ready, last * H_BODY + (H_BODY + st + j + 1))
                done = down(0, j, (st + j) % RING, False, j == 3)
                done.then_inc(halves_used, 1)
            pe.wait_ge(m_gtc, last + 1)
            pe.wait_ge(m_staged, last * 2 + 4)
            for n, (t, nh) in enumerate(LAST_PIECES):
                pe.wait_ge(m_ysb, last + (nh + 1))
                scatter_piece(t, nh, LAST_BANKS[n])


def constants():
    c = np.zeros((P, C_WIDTH), np.float32)
    i = np.arange(P)
    row, column = i[:, None], i[None, :]
    c[:, C_IDENT:C_IDENT + P] = row == column
    c[:, C_TRI:C_TRI + P] = row <= column
    c[:, C_NREV:C_NREV + P] = np.where(row >= column, -1.0, 0.0)
    c[:, C_ONES:C_ONES + P] = 1.0
    c[:, C_NONES:C_NONES + P] = -1.0
    c[:, C_FMASK:C_FMASK + P] = np.where(column <= row, 0.0, BIG_NEG)
    c[:, C_SMASK:C_SMASK + P] = np.where(row < column, 0.0, BIG_NEG)
    c[:, C_BLK:C_BLK + P] = np.where(row // 16 == column // 16, 1.0 / 16, 0.0)
    c[:, C_IOTA:C_IOTA + P] = column
    c[:, C_TROW:C_TROW + SEQ] = np.arange(SEQ)
    c[:, C_EIDX:C_EIDX + EXPERTS] = np.arange(EXPERTS)
    c[:, C_REV:C_REV + EXPERTS] = EXPERTS - np.arange(EXPERTS)
    return c


def by_partition(a):
    return a.reshape(DEPTH, -1, P).transpose(2, 0, 1)


def kernel(**inputs):
    import concourse.bacc as bacc
    from concourse.bass_utils import run_bass_kernel_spmd

    g = {k: np.asarray(v) for k, v in inputs.items()}
    f = np.float32
    small = np.zeros((P, DEPTH, S_WIDTH), f)
    small[:, :, S_GA:S_GA + KD] = by_partition(g["attn_norm"])
    small[:, :, S_GF:S_GF + KD] = by_partition(g["ffn_norm"])
    small[:, :, S_GO:S_GO + KD] = by_partition(g["out_norm"])
    small[:, :, S_ARE:S_ARE + KD] = by_partition(g["ssm_a_re"])
    small[:, :, S_AIM:S_AIM + KD] = by_partition(g["ssm_a_im"])
    small[:, :, S_LDT:S_LDT + KD] = by_partition(np.repeat(g["ssm_log_dt"], 64, axis=1))
    small[:, :, S_DSK:S_DSK + 2] = by_partition(g["ssm_d"])
    small[:, :, S_BGL:S_BGL + 2] = by_partition(g["ssm_b_glu"])
    small[:, :, S_BF:S_BF + HEADS] = g["b_forget"][None]
    small[:HEAD_DIM, :, S_GQ] = g["fox_q_norm"].T
    small[:HEAD_DIM, :, S_GK] = g["fox_k_norm"].T
    small[:, 0, S_EPS] = EPS
    small[:, 1, S_EPS] = HEAD_DIM * EPS
    small[HEAD_DIM:AUG, :, S_GQ:S_GK + 1] = 1.0
    b_mat = np.zeros((DEPTH, 4, 2, 16, 2, 2, 2, 64), f)
    c_mat = np.zeros((DEPTH, 2, 64, 2, KD, 2, 16), f)
    for r, (bn, cn) in enumerate((("ssm_b_re", "ssm_c_re"), ("ssm_b_im", "ssm_c_im"))):
        b = g[bn].reshape(DEPTH, 2, 4, 2, 64, 16)
        c = g[cn].reshape(DEPTH, KD, 2, 16, 64)
        for q in range(2):
            b_mat[:, :, q, :, r, :, q, :] = b[:, :, :, q].transpose(0, 2, 4, 1, 3)
            c_mat[:, q, :, r, :, q, :] = c[:, :, q].transpose(0, 3, 1, 2)
    arrays = {
        "x_d": g["x"].reshape(SEQ, D_MODEL),
        "consts_d": constants(),
        "small_d": small,
        "b_d": b_mat.reshape(DEPTH, P, 2, 2, P),
        "c_d": c_mat.reshape(DEPTH, P, 2, KD, 32),
        "wglu_d": g["ssm_w_glu"].reshape(DEPTH, 2, P, SSM_WIDTH).transpose(0, 2, 1, 3),
        "w_in_d": g["w_in"],
        "w_out_d": g["w_out"],
        "dg_d": g["dense_w_gate"][0],
        "du_d": g["dense_w_up"][0],
        "dd_d": g["dense_w_down"][0],
        "wr_d": g["moe_w_router"][0].reshape(KD, P, EXPERTS).transpose(1, 0, 2),
        "mg_d": g["moe_w_gate"],
        "mu_d": g["moe_w_up"],
        "md_d": g["moe_w_down"],
    }
    nc = bacc.Bacc("TRN2", target_bir_lowering=False, num_devices=1)
    args = {}
    for name, a in arrays.items():
        a = arrays[name] = np.ascontiguousarray(a)
        args[name] = nc.dram_tensor(name, a.shape, mybir.dt.from_np(a.dtype), kind="ExternalInput").ap()
    args["out_d"] = nc.dram_tensor("out_d", (SEQ, D_MODEL), F32, kind="ExternalOutput").ap()
    trunk(nc, **args)
    r = run_bass_kernel_spmd(nc, [arrays], core_ids=[0])
    return r.results[0]["out_d"].reshape(1, SEQ, D_MODEL)
```
